# Optimizing a Trainium2 kernel written in Bass

```python
import jax, jax.numpy as jnp
from jax import lax
import numpy as np
import math

D_MODEL = 1024
BATCH = 1
SEQ = 256
DEPTH = 1

GRID_W = 64
CTX_LEN = 256
HEAD_DIM = 64
EPS = 1e-6
A_WIDTH = D_MODEL // 4
A_HEADS = A_WIDTH // HEAD_DIM
A_CHUNK = 128
B_WIDTH = D_MODEL // 2
B_HEADS = B_WIDTH // HEAD_DIM
B_KV_HEADS = 2
B_GROUP = B_HEADS // B_KV_HEADS
B_KV_WIDTH = B_KV_HEADS * HEAD_DIM
Q_BLOCK = 128
ROPE_AXIS_DIM = HEAD_DIM // 2
ROPE_BASE = 10000.0
C_WIDTH = D_MODEL // 4
C_HEADS = C_WIDTH // HEAD_DIM
C_CHUNK = 64
MIX_WIDTH = A_WIDTH + B_WIDTH + C_WIDTH
OFF_B = 2 * A_WIDTH
OFF_KV = OFF_B + B_WIDTH
OFF_C = OFF_KV + 2 * B_KV_WIDTH
OFF_G = OFF_C + 4 * C_WIDTH
IN_WIDTH = OFF_G + C_WIDTH
N_GROUPS = 4
EXPERTS_PER_GROUP = 8
N_EXPERTS = N_GROUPS * EXPERTS_PER_GROUP
TOP_K = 2
D_FF_EXPERT = D_MODEL // 2
MOE_BLOCK = 128


def _rms(x):
    xf = x.astype(jnp.float32)
    return (xf * lax.rsqrt(jnp.mean(xf * xf, axis=-1, keepdims=True) + EPS)).astype(x.dtype)

def axial_rope_tables(rows):
    row = jnp.repeat(jnp.arange(rows), GRID_W).astype(jnp.float32)
    col = jnp.tile(jnp.arange(GRID_W), rows).astype(jnp.float32)
    inv_freq = 1.0 / (ROPE_BASE ** (jnp.arange(0, ROPE_AXIS_DIM, 2, dtype=jnp.float32) / ROPE_AXIS_DIM))
    ang = jnp.stack([row[:, None] * inv_freq, col[:, None] * inv_freq], axis=1)
    return jnp.cos(ang)[:, None, :, None, :], jnp.sin(ang)[:, None, :, None, :]

def apply_rope(x, cos, sin):
    b, t, h, _ = x.shape
    xr = x.astype(jnp.float32).reshape(b, t, h, 2, 2, ROPE_AXIS_DIM // 2)
    rot = jnp.stack([-xr[..., 1, :], xr[..., 0, :]], axis=-2)
    return (xr * cos + rot * sin).reshape(b, t, h, HEAD_DIM).astype(x.dtype)

def chunk_mlp(z, w_s, b_s):
    b, t, _ = z.shape
    u, v = jnp.split(jax.nn.gelu(z), 2, axis=-1)
    v = _rms(v.reshape(b, t // A_CHUNK, A_CHUNK, A_HEADS, HEAD_DIM))
    mixed = jnp.einsum('hts,bnshd->bnthd', w_s, v) + b_s.T[:, :, None]
    return u * mixed.reshape(b, t, A_WIDTH)

def _gqa(q, k, v):
    s = jnp.einsum('bqkgd,bskd->bkgqs', q, k).astype(jnp.float32) * (HEAD_DIM ** -0.5)
    p = jax.nn.softmax(s, axis=-1).astype(v.dtype)
    return jnp.einsum('bkgqs,bskd->bqkgd', p, v)

def latent_attention(q, k, v, kc, vc):
    b, t, _, _ = q.shape
    keys = jnp.concatenate([k, kc], axis=1)
    vals = jnp.concatenate([v, vc], axis=1)
    qb = q.reshape(b, t // Q_BLOCK, Q_BLOCK, B_KV_HEADS, B_GROUP, HEAD_DIM).transpose(1, 0, 2, 3, 4, 5)
    out = lax.map(lambda qblk: _gqa(qblk, keys, vals), qb)
    return out.transpose(1, 0, 2, 3, 4, 5).reshape(b, t, B_WIDTH)

def forget_gate(zf, lb):
    zf32 = zf.astype(jnp.float32)
    lbh = lb.reshape(C_HEADS, HEAD_DIM)
    pos = lbh > 0.0
    log_lb = jnp.log(jnp.where(pos, lbh, 1.0))
    log_rest = jnp.log1p(-lbh) + jax.nn.log_sigmoid(zf32)
    log_f = jnp.where(pos, jnp.logaddexp(log_lb, log_rest), log_rest)
    k = (1.0 - lbh) * jax.nn.sigmoid(-zf32)
    return k, log_f

def hgrn_inputs(z, lb):
    b, t, _ = z.shape
    q, zf, zb, v = [a.reshape(b, t, C_HEADS, HEAD_DIM) for a in jnp.split(z, 4, axis=-1)]
    kf, logf_f = forget_gate(zf, lb[0])
    kb, logf_b = forget_gate(zb, lb[1])
    return jax.nn.silu(q), v, kf, logf_f, kb, logf_b

def hgrn_scan(q, k, v, log_f, s0, with_output):
    b, t, h, _ = q.shape
    nc = t // C_CHUNK

    def chunks(a):
        return a.astype(jnp.float32).reshape(b, nc, C_CHUNK, h, a.shape[-1]).transpose(1, 0, 3, 2, 4)

    qc, kc, vc = chunks(q), chunks(k), chunks(v)
    bc = jnp.cumsum(chunks(log_f), axis=3)
    tri = jnp.tril(jnp.ones((C_CHUNK, C_CHUNK), bool))[:, :, None]

    def step(s, inp):
        qi, ki, vi, bi = inp
        b_last = bi[:, :, -1:, :]
        s_new = jnp.exp(b_last[:, :, 0, :, None]) * s + jnp.einsum('bhsk,bhsv->bhkv', ki * jnp.exp(b_last - bi), vi)
        if not with_output:
            return s_new, None
        diff = bi[:, :, :, None, :] - bi[:, :, None, :, :]
        decay = jnp.where(tri, jnp.exp(jnp.where(tri, diff, 0.0)), 0.0)
        scores = jnp.einsum('bhtk,bhsk,bhtsk->bhts', qi, ki, decay)
        o = jnp.einsum('bhts,bhsv->bhtv', scores, vi) + jnp.einsum('bhtk,bhkv->bhtv', qi * jnp.exp(bi), s)
        return s_new, o

    s_fin, o = lax.scan(step, s0, (qc, kc, vc, bc))
    if with_output:
        o = o.transpose(1, 0, 3, 2, 4).reshape(b, t, h, v.shape[-1])
    return s_fin, o

def hgrn_bidir(z, zc, lb, ctx_out):
    q, v, kf, lf, kb, lbw = hgrn_inputs(z, lb)
    qc, vc, kfc, lfc, kbc, lbc = hgrn_inputs(zc, lb)
    s0 = jnp.zeros((z.shape[0], C_HEADS, HEAD_DIM, HEAD_DIM), jnp.float32)
    rev = lambda a: a[:, ::-1]
    sf, of_c = hgrn_scan(qc, kfc, vc, lfc, s0, ctx_out)
    _, of = hgrn_scan(q, kf, v, lf, sf, True)
    sb, ob_c = hgrn_scan(rev(qc), rev(kbc), rev(vc), rev(lbc), s0, ctx_out)
    _, ob = hgrn_scan(rev(q), rev(kb), rev(v), rev(lbw), sb, True)
    o = of + rev(ob)
    o_c = of_c + rev(ob_c) if ctx_out else None
    return o, o_c

def hgrn_out(o, g, w):
    b, t = g.shape[:2]
    return (_rms(o) * w).reshape(b, t, C_WIDTH).astype(g.dtype) * jax.nn.silu(g)

def hier_moe(h, w_grp, b_grp, w_exp, b_exp, w1, w3, w2):
    n_tok, d = h.shape
    g_logits = (h @ w_grp + b_grp).astype(jnp.float32)
    grp = jnp.argmax(g_logits, axis=-1)
    p_grp = jnp.take_along_axis(jax.nn.softmax(g_logits, axis=-1), grp[:, None], axis=-1)
    e_logits = (h @ w_exp + b_exp).astype(jnp.float32).reshape(n_tok, N_GROUPS, EXPERTS_PER_GROUP)
    e_in = jnp.take_along_axis(e_logits, grp[:, None, None], axis=1)[:, 0]
    top_val, top_idx = lax.top_k(e_in, TOP_K)
    gate = (jax.nn.softmax(top_val, axis=-1) * p_grp).reshape(-1)
    expert = (grp[:, None] * EXPERTS_PER_GROUP + top_idx).reshape(-1)
    tok = jnp.repeat(jnp.arange(n_tok), TOP_K)
    n_asg = n_tok * TOP_K
    order = jnp.argsort(expert)
    e_sorted, tok_sorted, gate_sorted = expert[order], tok[order], gate[order]
    counts = jax.ops.segment_sum(jnp.ones_like(expert), expert, num_segments=N_EXPERTS)
    padded = (counts + MOE_BLOCK - 1) // MOE_BLOCK * MOE_BLOCK
    starts = jnp.cumsum(counts) - counts
    pad_ends = jnp.cumsum(padded)
    pad_starts = pad_ends - padded
    dest = pad_starts[e_sorted] + jnp.arange(n_asg) - starts[e_sorted]
    n_blocks = -(-n_asg // MOE_BLOCK) + N_EXPERTS
    buf = jnp.zeros((n_blocks * MOE_BLOCK, d), h.dtype).at[dest].set(h[tok_sorted])
    blk_expert = jnp.minimum(jnp.searchsorted(pad_ends, jnp.arange(n_blocks) * MOE_BLOCK, side='right'), N_EXPERTS - 1)

    def expert_block(args):
        xb, e = args
        return (jax.nn.silu(xb @ w1[e]) * (xb @ w3[e])) @ w2[e]

    out = lax.map(expert_block, (buf.reshape(n_blocks, MOE_BLOCK, d), blk_expert)).reshape(-1, d)
    y = jax.ops.segment_sum(out[dest] * gate_sorted[:, None], tok_sorted, num_segments=n_tok)
    return y.astype(h.dtype)

def hybrid_layer(x, xc, c, c_ctx, cos, sin, lb, w_mod, b_mod, norm1_w, w_in, w_s, b_s, q_norm_w, k_norm_w,
                 hgrn_norm_w, w_out, norm2_w, w_grp, b_grp, w_exp, b_exp, w1, w3, w2, ctx_out):
    b, t, d = x.shape
    lc = xc.shape[1]
    sh1, sc1, g1, sh2, sc2, g2 = jnp.split((jax.nn.silu(c) @ w_mod + b_mod)[:, None, :], 6, axis=-1)
    n_mod = 6 if ctx_out else 2
    mod_c = jnp.split(jax.nn.silu(c_ctx) @ w_mod[:, :n_mod * d] + b_mod[:n_mod * d], n_mod)
    h = _rms(x) * norm1_w * (1.0 + sc1) + sh1
    hc = _rms(xc) * norm1_w * (1.0 + mod_c[1]) + mod_c[0]
    p = h @ w_in
    pc = hc @ w_in[:, OFF_KV:OFF_G]
    ya = chunk_mlp(p[..., :OFF_B], w_s, b_s)
    q = apply_rope(_rms(p[..., OFF_B:OFF_KV].reshape(b, t, B_HEADS, HEAD_DIM)) * q_norm_w, cos, sin)
    k, v = jnp.split(p[..., OFF_KV:OFF_C].reshape(b, t, 2 * B_KV_HEADS, HEAD_DIM), 2, axis=2)
    k = apply_rope(_rms(k) * k_norm_w, cos, sin)
    kc, vc = jnp.split(pc[..., :2 * B_KV_WIDTH].reshape(b, lc, 2 * B_KV_HEADS, HEAD_DIM), 2, axis=2)
    kc = _rms(kc) * k_norm_w
    yb = latent_attention(q, k, v, kc, vc)
    o, o_c = hgrn_bidir(p[..., OFF_C:OFF_G], pc[..., 2 * B_KV_WIDTH:], lb, ctx_out)
    yc = hgrn_out(o, p[..., OFF_G:], hgrn_norm_w)
    x = x + g1 * (jnp.concatenate([ya, yb, yc], axis=-1) @ w_out)
    h2 = _rms(x) * norm2_w * (1.0 + sc2) + sh2
    if ctx_out:
        pc_rest = hc @ w_in[:, :OFF_KV]
        pc_g = hc @ w_in[:, OFF_G:]
        ya_c = chunk_mlp(pc_rest[..., :OFF_B], w_s, b_s)
        qc = _rms(pc_rest[..., OFF_B:].reshape(b, lc, B_HEADS, HEAD_DIM)) * q_norm_w
        yb_c = _gqa(qc.reshape(b, lc, B_KV_HEADS, B_GROUP, HEAD_DIM), kc, vc).reshape(b, lc, B_WIDTH)
        yc_c = hgrn_out(o_c, pc_g, hgrn_norm_w)
        xc = xc + mod_c[2] * (jnp.concatenate([ya_c, yb_c, yc_c], axis=-1) @ w_out)
        h2c = _rms(xc) * norm2_w * (1.0 + mod_c[4]) + mod_c[3]
        tokens = jnp.concatenate([h2.reshape(-1, d), h2c.reshape(-1, d)], axis=0)
        m = hier_moe(tokens, w_grp, b_grp, w_exp, b_exp, w1, w3, w2)
        x = x + g2 * m[:b * t].reshape(b, t, d)
        xc = xc + mod_c[5] * m[b * t:].reshape(b, lc, d)
    else:
        x = x + g2 * hier_moe(h2.reshape(-1, d), w_grp, b_grp, w_exp, b_exp, w1, w3, w2).reshape(b, t, d)
    return x, xc

def first_inputs(seed: int = 0) -> dict:
    key = jax.random.key(seed)
    ks = jax.random.split(key, 24)
    nrm = lambda k, shape, scale: jax.random.normal(k, shape, jnp.float32) * scale
    return {
        'x': nrm(ks[0], (BATCH, SEQ, D_MODEL), 1.0),
        'c': nrm(ks[1], (BATCH, D_MODEL), 1.0),
        'ctx': nrm(ks[2], (BATCH, CTX_LEN, D_MODEL), 1.0),
        'c_ctx': nrm(ks[3], (D_MODEL,), 1.0),
        'w_mod': nrm(ks[4], (DEPTH, D_MODEL, 6 * D_MODEL), 0.5 * D_MODEL ** -0.5),
        'b_mod': nrm(ks[5], (DEPTH, 6 * D_MODEL), 0.02),
        'norm1_w': 1.0 + nrm(ks[6], (DEPTH, D_MODEL), 0.02),
        'w_in': nrm(ks[7], (DEPTH, D_MODEL, IN_WIDTH), D_MODEL ** -0.5),
        'w_s': nrm(ks[8], (DEPTH, A_HEADS, A_CHUNK, A_CHUNK), A_CHUNK ** -0.5),
        'b_s': 1.0 + nrm(ks[9], (DEPTH, A_HEADS, A_CHUNK), 0.02),
        'q_norm_w': 1.0 + nrm(ks[10], (DEPTH, HEAD_DIM), 0.02),
        'k_norm_w': 1.0 + nrm(ks[11], (DEPTH, HEAD_DIM), 0.02),
        'hgrn_lb_logits': nrm(ks[12], (DEPTH, 2, C_WIDTH), 1.0),
        'hgrn_norm_w': 1.0 + nrm(ks[13], (DEPTH, HEAD_DIM), 0.02),
        'w_out': nrm(ks[14], (DEPTH, MIX_WIDTH, D_MODEL), MIX_WIDTH ** -0.5),
        'norm2_w': 1.0 + nrm(ks[15], (DEPTH, D_MODEL), 0.02),
        'w_grp': nrm(ks[16], (DEPTH, D_MODEL, N_GROUPS), D_MODEL ** -0.5),
        'b_grp': nrm(ks[17], (DEPTH, N_GROUPS), 0.01),
        'w_exp': nrm(ks[18], (DEPTH, D_MODEL, N_EXPERTS), D_MODEL ** -0.5),
        'b_exp': nrm(ks[19], (DEPTH, N_EXPERTS), 0.01),
        'w1': nrm(ks[20], (DEPTH, N_EXPERTS, D_MODEL, D_FF_EXPERT), D_MODEL ** -0.5),
        'w3': nrm(ks[21], (DEPTH, N_EXPERTS, D_MODEL, D_FF_EXPERT), D_MODEL ** -0.5),
        'w2': nrm(ks[22], (DEPTH, N_EXPERTS, D_FF_EXPERT, D_MODEL), D_FF_EXPERT ** -0.5),
    }

def first_block(x, c, ctx, c_ctx, w_mod, b_mod, norm1_w, w_in, w_s, b_s, q_norm_w, k_norm_w, hgrn_lb_logits,
              hgrn_norm_w, w_out, norm2_w, w_grp, b_grp, w_exp, b_exp, w1, w3, w2):
    ROWS = x.shape[1] // GRID_W
    cos, sin = axial_rope_tables(ROWS)
    lb_sm = jax.nn.softmax(hgrn_lb_logits.astype(jnp.float32), axis=0)
    lb = jnp.cumsum(lb_sm, axis=0) - lb_sm[0]
    xc = ctx
    for l in range(DEPTH):
        x, xc = hybrid_layer(x, xc, c, c_ctx, cos, sin, lb[l], w_mod[l], b_mod[l], norm1_w[l], w_in[l], w_s[l],
                             b_s[l], q_norm_w[l], k_norm_w[l], hgrn_norm_w[l], w_out[l], norm2_w[l], w_grp[l],
                             b_grp[l], w_exp[l], b_exp[l], w1[l], w3[l], w2[l], ctx_out=(l < DEPTH - 1))
    return x


DEPTH_2 = 2

N_MIXERS = 2
N_MLA_LAYERS = (DEPTH_2 + N_MIXERS - 1) // N_MIXERS
N_HYENA_LAYERS = DEPTH_2 // N_MIXERS

MLA_HEADS = 8
Q_LORA = 256
KV_LORA = 128
QK_NOPE = 128
QK_ROPE = 64
QK_HEAD = QK_NOPE + QK_ROPE
V_HEAD = 128
ROPE_HALF = QK_ROPE // 2
ROPE_THETA = 10000.0

HYENA_ORDER = 2
SHORT_CONV = 3
FILTER_EMB = 33
FILTER_BANDS = (FILTER_EMB - 1) // 2
FILTER_WIDTH = 64
FAST_DECAY = 0.3
SLOW_DECAY = 1.5
DECAY_TARGET = 1e-2

EXPERTS_PER_GROUP_2 = 4
N_EXPERTS_2 = N_GROUPS * EXPERTS_PER_GROUP_2
D_EXPERT = 256


def rms_norm(x, g):
    xf = x.astype(jnp.float32)
    y = xf * lax.rsqrt(jnp.mean(xf * xf, axis=-1, keepdims=True) + EPS)
    return (y * g.astype(jnp.float32)).astype(x.dtype)

def modulate(h, shift, scale):
    return h * (1 + scale[:, None, :]) + shift[:, None, :]

def rope_tables(positions):
    inv_freq = 1.0 / (ROPE_THETA ** (jnp.arange(0, QK_ROPE, 2, dtype=jnp.float32) / QK_ROPE))
    ang = positions.astype(jnp.float32)[..., None] * inv_freq
    return jnp.cos(ang), jnp.sin(ang)

def apply_rope_2(x, cos, sin):
    xf = x.astype(jnp.float32)
    x1, x2 = xf[..., :ROPE_HALF], xf[..., ROPE_HALF:]
    return jnp.concatenate([x1 * cos - x2 * sin, x1 * sin + x2 * cos], axis=-1).astype(x.dtype)

def mla_mixer(h, cos, sin, w_down, q_a_g, kv_a_g, w_uq, w_ukv, q_norm_g, k_norm_g, w_o):
    B, S, _ = h.shape
    lat = h @ w_down
    c_q = lat[..., :Q_LORA]
    c_kv = lat[..., Q_LORA:Q_LORA + KV_LORA]
    k_pe = lat[..., Q_LORA + KV_LORA:]
    q = (rms_norm(c_q, q_a_g) @ w_uq).reshape(B, S, MLA_HEADS, QK_HEAD)
    kv = (rms_norm(c_kv, kv_a_g) @ w_ukv).reshape(B, S, MLA_HEADS, QK_NOPE + V_HEAD)
    cos_h, sin_h = cos[:, :, None, :], sin[:, :, None, :]
    q_nope = rms_norm(q[..., :QK_NOPE], q_norm_g[:QK_NOPE])
    q_pe = apply_rope_2(rms_norm(q[..., QK_NOPE:], q_norm_g[QK_NOPE:]), cos_h, sin_h)
    k_nope = rms_norm(kv[..., :QK_NOPE], k_norm_g[:QK_NOPE])
    k_pe = apply_rope_2(rms_norm(k_pe, k_norm_g[QK_NOPE:]), cos, sin)
    v = kv[..., QK_NOPE:]
    q = jnp.concatenate([q_nope, q_pe], axis=-1)
    k = jnp.concatenate([k_nope, jnp.broadcast_to(k_pe[:, :, None, :], (B, S, MLA_HEADS, QK_ROPE))], axis=-1)
    scale = QK_HEAD ** -0.5
    n_blk = S // Q_BLOCK
    q_blocks = q.reshape(B, n_blk, Q_BLOCK, MLA_HEADS, QK_HEAD).transpose(1, 0, 2, 3, 4)

    def attend(q_blk):
        s = jnp.einsum('bqhd,bkhd->bhqk', q_blk, k, preferred_element_type=jnp.float32) * scale
        p = jax.nn.softmax(s, axis=-1).astype(v.dtype)
        return jnp.einsum('bhqk,bkhd->bqhd', p, v)

    o = lax.map(attend, q_blocks)
    o = o.transpose(1, 0, 2, 3, 4).reshape(B, S, MLA_HEADS * V_HEAD)
    return o @ w_o

def hyena_filters(L, w1, b1, f1, w2, b2, f2, w3, b3, f3, w4):
    f32 = jnp.float32
    t = jnp.linspace(0.0, 1.0, L, dtype=f32)[:, None]
    w = 2.0 * math.pi * jnp.arange(L, dtype=f32)[:, None] / L
    fr = jnp.linspace(1e-4, FILTER_BANDS - 1, FILTER_BANDS, dtype=f32)[None, :]
    z = jnp.concatenate([t, jnp.cos(fr * w), -jnp.sin(fr * w)], axis=-1)
    hdn = jnp.sin(f1.astype(f32) * (z @ w1.astype(f32) + b1.astype(f32)))
    hdn = jnp.sin(f2.astype(f32) * (hdn @ w2.astype(f32) + b2.astype(f32)))
    hdn = jnp.sin(f3.astype(f32) * (hdn @ w3.astype(f32) + b3.astype(f32)))
    h = (hdn @ w4.astype(f32)).reshape(L, HYENA_ORDER, 2, D_MODEL)
    deltas = jnp.abs(jnp.linspace(math.log(FAST_DECAY) / DECAY_TARGET,
                                  math.log(SLOW_DECAY) / DECAY_TARGET, D_MODEL, dtype=f32))
    decay = jnp.exp(-t * deltas)
    h = h * decay[:, None, None, :]
    return h / (jnp.sum(jnp.abs(h), axis=0, keepdims=True) + EPS)

def bidir_long_conv(u, h_fwd, h_bwd, bias):
    B, L, D = u.shape
    k2 = jnp.concatenate([h_fwd, jnp.zeros((1, D), jnp.float32), h_bwd[:0:-1]], axis=0)
    k_f = jnp.fft.rfft(k2, axis=0)
    u_f = jnp.fft.rfft(u.astype(jnp.float32), n=2 * L, axis=1)
    y = jnp.fft.irfft(u_f * k_f[None], n=2 * L, axis=1)[:, :L]
    return (y + u.astype(jnp.float32) * bias.astype(jnp.float32)).astype(u.dtype)

def hyena_mixer(h, w_in, b_in, conv_w, conv_b, f_w1, f_b1, f_freq1, f_w2, f_b2, f_freq2,
                f_w3, f_b3, f_freq3, f_w4, filt_bias, w_out):
    B, L, _ = h.shape
    C = 3 * D_MODEL
    u = h @ w_in + b_in
    u = lax.conv_general_dilated(u, conv_w[:, None, :].astype(u.dtype), window_strides=(1,),
                                 padding=((SHORT_CONV // 2, SHORT_CONV // 2),),
                                 dimension_numbers=('NWC', 'WIO', 'NWC'),
                                 feature_group_count=C) + conv_b
    x1, x2, v = jnp.split(u, 3, axis=-1)
    filt = hyena_filters(L, f_w1, f_b1, f_freq1, f_w2, f_b2, f_freq2, f_w3, f_b3, f_freq3, f_w4)
    z = v
    for o, gate in enumerate((x1, x2)):
        z = gate * bidir_long_conv(z, filt[:, o, 0], filt[:, o, 1], filt_bias[o])
    return z @ w_out

def hier_moe_2(h, wg, bg, we, be, w_gate, w_up, w_down):
    B, S, D = h.shape
    t = h.reshape(B * S, D)
    T = t.shape[0]
    g_prob = jax.nn.softmax((t @ wg).astype(jnp.float32) + bg.astype(jnp.float32), axis=-1)
    g_w, g_idx = lax.top_k(g_prob, 1)
    e_logits = ((t @ we).astype(jnp.float32) + be.astype(jnp.float32)).reshape(T, N_GROUPS, EXPERTS_PER_GROUP_2)
    e_logits = jnp.take_along_axis(e_logits, g_idx[:, :, None], axis=1)[:, 0]
    e_w, e_idx = lax.top_k(jax.nn.softmax(e_logits, axis=-1), TOP_K)
    weights = g_w * (e_w / jnp.sum(e_w, axis=-1, keepdims=True))
    expert = g_idx * EXPERTS_PER_GROUP_2 + e_idx
    combine = jnp.sum(jax.nn.one_hot(expert, N_EXPERTS_2, dtype=jnp.float32) * weights[..., None], axis=1)
    combine = combine.astype(t.dtype)
    out = jnp.zeros_like(t)
    for e in range(N_EXPERTS_2):
        a = jax.nn.silu(t @ w_gate[e]) * (t @ w_up[e])
        out = out + combine[:, e:e + 1] * (a @ w_down[e])
    return out.reshape(B, S, D)

def second_inputs(seed: int = 0) -> dict:
    key = jax.random.key(seed)
    ks = iter(jax.random.split(key, 64))
    D = D_MODEL
    NA, NH = N_MLA_LAYERS, N_HYENA_LAYERS

    def nrm(shape, scale):
        return jax.random.normal(next(ks), shape, jnp.float32) * scale

    def gain(shape):
        return 1.0 + nrm(shape, 0.02)

    x = nrm((BATCH, SEQ, D), 1.0)
    c = nrm((BATCH, D), 1.0)
    offs = jax.random.randint(next(ks), (BATCH, 1), 0, 1024, dtype=jnp.int32)
    positions = offs + jnp.arange(SEQ, dtype=jnp.int32)[None, :]
    return {
        "x": x, "c": c, "positions": positions,
        "ada_w": nrm((DEPTH_2, D, 6 * D), 0.5 * D ** -0.5),
        "ada_b": nrm((DEPTH_2, 6 * D), 0.02),
        "norm_mix_g": gain((DEPTH_2, D)),
        "norm_ffn_g": gain((DEPTH_2, D)),
        "mla_w_down": nrm((NA, D, Q_LORA + KV_LORA + QK_ROPE), D ** -0.5),
        "mla_q_a_g": gain((NA, Q_LORA)),
        "mla_kv_a_g": gain((NA, KV_LORA)),
        "mla_w_uq": nrm((NA, Q_LORA, MLA_HEADS * QK_HEAD), Q_LORA ** -0.5),
        "mla_w_ukv": nrm((NA, KV_LORA, MLA_HEADS * (QK_NOPE + V_HEAD)), KV_LORA ** -0.5),
        "mla_q_norm_g": gain((NA, QK_HEAD)),
        "mla_k_norm_g": gain((NA, QK_HEAD)),
        "mla_w_o": nrm((NA, MLA_HEADS * V_HEAD, D), (MLA_HEADS * V_HEAD) ** -0.5),
        "hy_w_in": nrm((NH, D, 3 * D), D ** -0.5),
        "hy_b_in": nrm((NH, 3 * D), 0.02),
        "hy_conv_w": nrm((NH, SHORT_CONV, 3 * D), SHORT_CONV ** -0.5),
        "hy_conv_b": nrm((NH, 3 * D), 0.02),
        "hy_f_w1": nrm((NH, FILTER_EMB, FILTER_WIDTH), FILTER_EMB ** -0.5),
        "hy_f_b1": nrm((NH, FILTER_WIDTH), 0.1),
        "hy_f_freq1": gain((NH, FILTER_WIDTH)),
        "hy_f_w2": nrm((NH, FILTER_WIDTH, FILTER_WIDTH), FILTER_WIDTH ** -0.5),
        "hy_f_b2": nrm((NH, FILTER_WIDTH), 0.1),
        "hy_f_freq2": gain((NH, FILTER_WIDTH)),
        "hy_f_w3": nrm((NH, FILTER_WIDTH, FILTER_WIDTH), FILTER_WIDTH ** -0.5),
        "hy_f_b3": nrm((NH, FILTER_WIDTH), 0.1),
        "hy_f_freq3": gain((NH, FILTER_WIDTH)),
        "hy_f_w4": nrm((NH, FILTER_WIDTH, HYENA_ORDER * 2 * D), FILTER_WIDTH ** -0.5),
        "hy_filt_bias": nrm((NH, HYENA_ORDER, D), 1.0),
        "hy_w_out": nrm((NH, D, D), D ** -0.5),
        "moe_wg": nrm((DEPTH_2, D, N_GROUPS), D ** -0.5),
        "moe_bg": nrm((DEPTH_2, N_GROUPS), 0.01),
        "moe_we": nrm((DEPTH_2, D, N_EXPERTS_2), D ** -0.5),
        "moe_be": nrm((DEPTH_2, N_EXPERTS_2), 0.01),
        "moe_w_gate": nrm((DEPTH_2, N_EXPERTS_2, D, D_EXPERT), D ** -0.5),
        "moe_w_up": nrm((DEPTH_2, N_EXPERTS_2, D, D_EXPERT), D ** -0.5),
        "moe_w_down": nrm((DEPTH_2, N_EXPERTS_2, D_EXPERT, D), D_EXPERT ** -0.5),
    }

def second_block(x, c, positions, ada_w, ada_b, norm_mix_g, norm_ffn_g,
              mla_w_down, mla_q_a_g, mla_kv_a_g, mla_w_uq, mla_w_ukv, mla_q_norm_g, mla_k_norm_g, mla_w_o,
              hy_w_in, hy_b_in, hy_conv_w, hy_conv_b,
              hy_f_w1, hy_f_b1, hy_f_freq1, hy_f_w2, hy_f_b2, hy_f_freq2,
              hy_f_w3, hy_f_b3, hy_f_freq3, hy_f_w4, hy_filt_bias, hy_w_out,
              moe_wg, moe_bg, moe_we, moe_be, moe_w_gate, moe_w_up, moe_w_down):
    cos, sin = rope_tables(positions)
    c_act = jax.nn.silu(c.astype(jnp.float32))
    for i in range(DEPTH_2):
        mod = (c_act @ ada_w[i].astype(jnp.float32) + ada_b[i].astype(jnp.float32)).astype(x.dtype)
        sh1, sc1, g1, sh2, sc2, g2 = jnp.split(mod, 6, axis=-1)
        h = modulate(rms_norm(x, norm_mix_g[i]), sh1, sc1)
        j = i // N_MIXERS
        if i % N_MIXERS == 0:
            y = mla_mixer(h, cos, sin, mla_w_down[j], mla_q_a_g[j], mla_kv_a_g[j], mla_w_uq[j],
                          mla_w_ukv[j], mla_q_norm_g[j], mla_k_norm_g[j], mla_w_o[j])
        else:
            y = hyena_mixer(h, hy_w_in[j], hy_b_in[j], hy_conv_w[j], hy_conv_b[j],
                            hy_f_w1[j], hy_f_b1[j], hy_f_freq1[j], hy_f_w2[j], hy_f_b2[j], hy_f_freq2[j],
                            hy_f_w3[j], hy_f_b3[j], hy_f_freq3[j], hy_f_w4[j], hy_filt_bias[j], hy_w_out[j])
        x = x + g1[:, None, :] * y
        h = modulate(rms_norm(x, norm_ffn_g[i]), sh2, sc2)
        x = x + g2[:, None, :] * hier_moe_2(h, moe_wg[i], moe_bg[i], moe_we[i], moe_be[i],
                                          moe_w_gate[i], moe_w_up[i], moe_w_down[i])
    return x


def setup_inputs(seed=0):
    out = dict(first_inputs(seed))
    for name, value in second_inputs(seed + 1).items():
        if name != "x":
            out[name + "_2"] = value
    return out


def reference(
    x, c, ctx, c_ctx, w_mod, b_mod, norm1_w, w_in, w_s, b_s, q_norm_w, k_norm_w, hgrn_lb_logits,
    hgrn_norm_w, w_out, norm2_w, w_grp, b_grp, w_exp, b_exp, w1, w3, w2, c_2, positions_2,
    ada_w_2, ada_b_2, norm_mix_g_2, norm_ffn_g_2, mla_w_down_2, mla_q_a_g_2, mla_kv_a_g_2,
    mla_w_uq_2, mla_w_ukv_2, mla_q_norm_g_2, mla_k_norm_g_2, mla_w_o_2, hy_w_in_2, hy_b_in_2,
    hy_conv_w_2, hy_conv_b_2, hy_f_w1_2, hy_f_b1_2, hy_f_freq1_2, hy_f_w2_2, hy_f_b2_2,
    hy_f_freq2_2, hy_f_w3_2, hy_f_b3_2, hy_f_freq3_2, hy_f_w4_2, hy_filt_bias_2, hy_w_out_2,
    moe_wg_2, moe_bg_2, moe_we_2, moe_be_2, moe_w_gate_2, moe_w_up_2, moe_w_down_2,
):
    x = first_block(
        x, c, ctx, c_ctx, w_mod, b_mod, norm1_w, w_in, w_s, b_s, q_norm_w, k_norm_w,
        hgrn_lb_logits, hgrn_norm_w, w_out, norm2_w, w_grp, b_grp, w_exp, b_exp, w1, w3, w2,
    )
    return second_block(
        x, c_2, positions_2, ada_w_2, ada_b_2, norm_mix_g_2, norm_ffn_g_2, mla_w_down_2,
        mla_q_a_g_2, mla_kv_a_g_2, mla_w_uq_2, mla_w_ukv_2, mla_q_norm_g_2, mla_k_norm_g_2,
        mla_w_o_2, hy_w_in_2, hy_b_in_2, hy_conv_w_2, hy_conv_b_2, hy_f_w1_2, hy_f_b1_2,
        hy_f_freq1_2, hy_f_w2_2, hy_f_b2_2, hy_f_freq2_2, hy_f_w3_2, hy_f_b3_2, hy_f_freq3_2,
        hy_f_w4_2, hy_filt_bias_2, hy_w_out_2, moe_wg_2, moe_bg_2, moe_we_2, moe_be_2,
        moe_w_gate_2, moe_w_up_2, moe_w_down_2,
    )


_drawn_inputs = setup_inputs


def setup_inputs(seed=0):
    import zlib

    import numpy as np

    out = dict(_drawn_inputs(seed))
    spreads = {}
    factors = {'ctx': 2.843,
     'norm1_w': 5.013,
     'b_s': 6.331,
     'q_norm_w': 8.0,
     'k_norm_w': 8.0,
     'hgrn_norm_w': 8.0,
     'norm2_w': 3.578,
     'b_grp': 8.0,
     'b_exp': 7.807,
     'norm_mix_g_2': 3.288,
     'norm_ffn_g_2': 3.407,
     'mla_q_a_g_2': 8.0,
     'mla_kv_a_g_2': 8.0,
     'mla_q_norm_g_2': 8.0,
     'mla_k_norm_g_2': 8.0,
     'hy_b_in_2': 4.047,
     'hy_conv_b_2': 3.316,
     'hy_f_freq1_2': 8.0,
     'hy_f_freq2_2': 8.0,
     'hy_f_freq3_2': 7.081,
     'moe_bg_2': 8.0,
     'moe_be_2': 8.0}
    for name, (base, spread) in spreads.items():
        noise = np.random.default_rng([zlib.crc32(name.encode()), seed]).standard_normal(out[name].shape)
        drawn = base * np.exp(spread * noise) if base else spread * noise
        out[name] = __import__('jax').numpy.asarray(drawn.astype(out[name].dtype))
    for name, factor in factors.items():
        out[name] = (out[name] * factor).astype(out[name].dtype)
    return out
```

```python
from contextlib import ExitStack

import numpy as np

import concourse.bass as bass
import concourse.mybir as mybir

F32 = mybir.dt.float32
I32 = mybir.dt.int32
U32 = mybir.dt.uint32
ACT = mybir.ActivationFunctionType
ALU = mybir.AluOpType
AX = mybir.AxisListType.X

P = 128
TOKENS = 256
TT = TOKENS // P
D = 1024
KD = D // P
EPS = 1e-6
BANK = 512

A_HEADS, HD = 4, 64
B_HEADS, B_KV = 8, 2
C_HEADS = 4
CW = C_HEADS * HD
OFF_B, OFF_KV, OFF_C, OFF_G, IN_W = 512, 1024, 1280, 2304, 2560
CTX_W = OFF_G - OFF_KV
GRID_W = 64

MLA_HEADS, Q_LORA, KV_LORA, NOPE, ROPE, VH = 8, 256, 128, 128, 64, 128
HALF = ROPE // 2
LEVELS = 7
BIG = 1e30
SLOT = 4096
SLOTS = 5

TWO_PI_1 = 6.28125
TWO_PI_2 = float(np.float32(2 * np.pi - 6.28125))
TWO_PI_3 = float(2 * np.pi - 6.28125 - np.float64(np.float32(2 * np.pi - 6.28125)))
ROUND = 1.5 * 2.0 ** 23
PI_IN = 3.1415925


def shape_constants():
    t = np.arange(P)
    fwd, bwd, mask_f, mask_b = [], [], [], []
    r = t[:, None]
    for j in range(LEVELS):
        size = 2 << j
        mid = t // size * size + size // 2
        right = (t >> j & 1) == 1
        fwd.append(np.where(right, (r >= mid) & (r <= t), (r > t) & (r < mid)))
        bwd.append(np.where(right, (r >= mid) & (r < t), (r >= t) & (r < mid)))
        same = (r // size) == (t // size)
        rright = (r >> j & 1) == 1
        mask_f.append(same & ~rright & right)
        mask_b.append(same & rright & ~right)
    fwd.append(r <= t)
    bwd.append(r >= t)
    after_f, after_b = r > t, r < t
    scan = np.concatenate(fwd + bwd + [after_f, after_b] + mask_f + mask_b, axis=1)
    scan = scan.astype(np.float32)

    row = np.repeat(np.arange(TOKENS // GRID_W), GRID_W).astype(np.float32)
    col = np.tile(np.arange(GRID_W), TOKENS // GRID_W).astype(np.float32)
    inv = (1.0 / (np.float32(10000.0) ** (np.arange(0, 32, 2, dtype=np.float32) / np.float32(32)))).astype(np.float32)
    ang = np.stack([row[:, None] * inv, col[:, None] * inv], axis=1)
    cos = np.repeat(np.cos(ang)[:, :, None, :], 2, axis=2).reshape(TOKENS, HD)
    sin = np.stack([-np.sin(ang), np.sin(ang)], axis=2).reshape(TOKENS, HD)
    axial = np.concatenate([cos, sin], axis=1).astype(np.float32)
    axial = axial.reshape(TT, P, 2 * HD).transpose(1, 0, 2).reshape(P, -1)

    inv2 = (1.0 / (np.float32(10000.0) ** (np.arange(0, ROPE, 2, dtype=np.float32) / np.float32(ROPE)))).astype(np.float32)
    freq = np.tile(inv2[None, :], (P, 1)).astype(np.float32)

    L = TOKENS
    f, s = np.arange(L)[None, :], np.arange(L)[:, None]
    w = 2 * np.pi * ((f * s) % (2 * L)) / (2 * L)
    alt = np.where(np.arange(L) % 2 == 0, 1.0, -1.0)
    real, imag = np.cos(w), -np.sin(w)
    imag[:, 0] = alt
    ahead = np.concatenate([real, imag], axis=1)
    back_r = 2 * np.cos(w).T / (2 * L)
    back_r[0] /= 2
    back_i = -2 * np.sin(w).T / (2 * L)
    back_i[0] = alt / (2 * L)
    back = np.concatenate([back_r, back_i], axis=0)
    tl = np.linspace(0.0, 1.0, L, dtype=np.float32)[:, None]
    deltas = np.abs(np.linspace(np.log(0.3) / 1e-2, np.log(1.5) / 1e-2, D, dtype=np.float32))
    decay = np.exp(-tl * deltas)
    fold = lambda a, n: a.reshape(n, P, -1).transpose(1, 0, 2).reshape(P, -1)
    fourier = np.concatenate([fold(ahead, 2), fold(back, 4), fold(decay, 2)], axis=1).astype(np.float32)

    bands = 16
    wl = (2.0 * np.pi * np.arange(L, dtype=np.float32)[:, None] / L).astype(np.float32)
    fr = np.linspace(1e-4, bands - 1, bands, dtype=np.float32)[None, :]
    feats = np.concatenate([tl, np.cos(fr * wl), -np.sin(fr * wl)], axis=-1).astype(np.float32)
    return {
        "k_scan": scan, "k_axial": axial, "k_freq": freq, "k_fourier": fourier,
        "k_feats": np.ascontiguousarray(feats.T), "k_ident": np.eye(P, dtype=np.float32),
    }


class Lane:

    def __init__(self, sem):
        self.sem, self.count, self.steps, self.seen = sem, 0, [], {}

    def wait(self, *tokens):
        for tok in tokens:
            if tok is None:
                continue
            if isinstance(tok, list):
                self.wait(*tok)
                continue
            sem, value = tok
            if self.seen.get(id(sem), 0) < value:
                self.seen[id(sem)] = value
                self.steps.append(lambda e, s=sem, v=value: e.wait_ge(s, v))

    def last(self):
        return (self.sem, self.count) if self.count else None

    def put(self, make, *after, signal=True):
        self.wait(*after)
        if not signal:
            self.steps.append(lambda e: make())
            return None
        self.count += 1
        self.steps.append(lambda e: make().then_inc(self.sem, 1))
        return self.sem, self.count

    def dma(self, out, in_, sem, *after):
        self.wait(*after)
        self.steps.append(lambda e: e.dma_start(out, in_).then_inc(sem, 16))

    def run(self, engine):
        for step in self.steps:
            step(engine)


class Bank:

    def __init__(self, tensor):
        self.t, self.free = tensor, []


class Slot:
    def __init__(self, tensor, sem):
        self.t, self.sem, self.count, self.free = tensor, sem, 0, []


def build(nc, a, out, taps=None):
    ctx = ExitStack()
    with ctx:
        def sb(name, shape, dt=F32):
            return ctx.enter_context(nc.sbuf_tensor(name, shape, dt))

        def sem(name):
            return ctx.enter_context(nc.semaphore(name))

        slots = [Slot(sb(f"weights{i}", [P, SLOT]), sem(f"weights{i}_in")) for i in range(SLOTS)]
        x = sb("x", [P, TT, D])
        mod = sb("mod", [P, 6, D])
        h_rows = sb("h_rows", [P, TT, D])
        h_cols = sb("h_cols", [P, KD, TOKENS])
        norm_w = sb("norm_w", [P, 2, D])
        work = sb("work", [P, 17600])
        ident = sb("ident", [P, P])
        ones = sb("ones", [P, P])
        small = sb("small", [P, 384])
        banks = [Bank(ctx.enter_context(nc.psum_tensor(f"bank{i}", [P, BANK], F32))) for i in range(8)]

        tensor, vector, scalar, pool, sync = (Lane(sem(n)) for n in (
            "tensor_done", "vector_done", "scalar_done", "pool_done", "sync_done"))

        def dve(make, *after, chain=True):
            return vector.put(make, vector.last() if chain else None, *after)

        def act(make, *after, chain=True):
            return scalar.put(make, scalar.last() if chain else None, *after)

        def mms(out_ap, pairs, *after, start=True, stop=True, signal=True, loose=False):
            tensor.wait(*after)
            tok = None
            for i, (l, r) in enumerate(pairs):
                end = i == len(pairs) - 1
                tok = tensor.put(
                    lambda l=l, r=r, s=start and i == 0, e=stop and end: nc.tensor.matmul(
                        out_ap, l, r, start=s, stop=e, skip_group_check=loose),
                    signal=end and signal)
            return tok

        def turn(out_ap, in_ap, *after, signal=True):
            n = in_ap.shape[0]
            return tensor.put(lambda: nc.tensor.transpose(out_ap, in_ap, ident[0:n, 0:n]), *after, signal=signal)

        def a_fn(out_ap, in_ap, func, *after, chain=True, **kw):
            return act(lambda: nc.scalar.activation(out_ap, in_ap, func, **kw), *after, chain=chain)

        def v_copy(out_ap, in_ap, *after, chain=True):
            return dve(lambda: nc.vector.tensor_copy(out_ap, in_ap), *after, chain=chain)

        def v_tt(out_ap, p, q, op, *after, chain=True):
            return dve(lambda: nc.vector.tensor_tensor(out_ap, p, q, op), *after, chain=chain)

        def v_ts(out_ap, p, s1, s2, op0, op1, *after, chain=True):
            if s2 is None:
                return dve(lambda: nc.vector.tensor_scalar(out_ap, p, s1, None, op0), *after, chain=chain)
            return dve(lambda: nc.vector.tensor_scalar(out_ap, p, s1, s2, op0, op1), *after, chain=chain)

        def v_stt(out_ap, p, s, q, op0, op1, *after, chain=True):
            return dve(lambda: nc.vector.scalar_tensor_tensor(out=out_ap, in0=p, scalar=s, in1=q, op0=op0, op1=op1),
                       *after, chain=chain)

        def v_recip(out_ap, in_ap, *after):
            return dve(lambda: nc.vector.reciprocal(out_ap, in_ap), *after)

        def v_sum(out_ap, in_ap, *after):
            return dve(lambda: nc.vector.reduce_sum(out_ap, in_ap, AX), *after)

        def v_max(out_ap, in_ap, *after):
            return dve(lambda: nc.vector.reduce_max(out_ap, in_ap, AX), *after)

        bank_at = [0]

        def next_bank():
            b = banks[bank_at[0] % 8]
            bank_at[0] += 1
            return b

        slot_at = [0]

        def load(*pieces):
            s = slots[slot_at[0] % SLOTS]
            slot_at[0] += 1
            for view, src in pieces:
                s.count += 16
                sync.dma(view(s.t), src, s.sem, *s.free)
            s.free = []
            return s, (s.sem, s.count)

        def side_load(name, pieces, *after, lane=None):
            s = sem(name + "_in")
            for dst, src in pieces:
                (lane or pool).dma(dst, src, s, *after)
            return s, 16 * len(pieces)

        def cut(at, *dims):
            n = int(np.prod(dims))
            assert at + n <= 17600, (at, n)
            v = work[:, at:at + n]
            if len(dims) == 1:
                return v
            if len(dims) == 2:
                return v.rearrange("p (a b) -> p a b", a=dims[0])
            if len(dims) == 3:
                return v.rearrange("p (a b c) -> p a b c", a=dims[0], b=dims[1])
            return v.rearrange("p (a b c d) -> p a b c d", a=dims[0], b=dims[1], c=dims[2])

        def tap(name, ap, *toks):
            if taps is not None and name in taps:
                s = sem("tap_" + name)
                pool.dma(taps[name], ap, s, *toks)
                for l in (tensor, vector, scalar, pool, sync):
                    l.wait((s, 16))

        def everyone():
            return [l.last() for l in (tensor, vector, scalar, pool)]

        got_ident = side_load("ident", [(ident[:, :], a["k_ident"])], lane=scalar)
        made_ones = vector.put(lambda: nc.vector.memset(ones[:, :], 1.0))
        tensor.wait(got_ident, made_ones)

        def rstd(dst, ssum, width, *after):
            t = v_ts(ssum, ssum, 1.0 / width, EPS, ALU.mult, ALU.add, *after)
            t = a_fn(ssum, ssum, ACT.Sqrt, t)
            return v_recip(dst, ssum, t)

        def head_norm(src, dst, groups, width, weight, sq, stat, *after):
            t = v_tt(sq, src, src, ALU.mult, *after)
            t = v_sum(stat, sq, t)
            t = rstd(stat, stat, width, t)
            t = v_tt(dst, src, stat.unsqueeze(2).to_broadcast([P, groups, width]), ALU.mult, t)
            if weight is not None:
                t = v_tt(dst, dst, weight, ALU.mult, t)
            return t

        def modulation(c_in, w, b_row, dst, n_parts, cond, rep, name, *after):
            got_c = side_load(name + "_c", [(cond, c_in)], *after)
            got_b = side_load(name + "_b", [(dst[:, 0:n_parts, :], b_row.partition_broadcast(P))], *after)
            t = a_fn(cond, cond, ACT.Silu, got_c, *after)
            t = v_copy(rep, cond.unsqueeze(2).to_broadcast([P, KD, P]), t, *after)
            wv = w.rearrange("(p k) n -> p k n", k=KD)
            vector.wait(got_b)
            flat = dst.rearrange("p a b -> p (a b)")
            for c in range(n_parts * D // BANK):
                s, got = load((lambda v: v[:, :].rearrange("p (k n) -> p k n", k=KD),
                               wv[:, :, c * BANK:(c + 1) * BANK]))
                ws = s.t[:, :].rearrange("p (k n) -> p k n", k=KD)
                b = next_bank()
                m = mms(b.t[:, :], [(rep[:, k, :], ws[:, k, :]) for k in range(KD)], got, t, *b.free)
                s.free = [m]
                piece = flat[:, c * BANK:(c + 1) * BANK]
                b.free = [v_tt(piece, b.t[:, :], piece, ALU.add, m, chain=False)]
            return b.free[0]

        def norm_modulate(src, weight, scale, shift, *after, fold=True):
            t = None
            if fold:
                t = v_stt(scale, scale, 1.0, weight, ALU.add, ALU.mult, *after)
            ss = small[:, 0:TT]
            q = [a_fn(h_rows[:, i, :], src[:, i, :], ACT.Square, *after, accum_out=ss[:, i:i + 1]) for i in range(TT)]
            t = rstd(small[:, 4:4 + TT], ss, D, *q, t)
            for i in range(TT):
                t = v_stt(h_rows[:, i, :], src[:, i, :], small[:, 4 + i:5 + i], scale, ALU.mult, ALU.mult, t)
                t = v_tt(h_rows[:, i, :], h_rows[:, i, :], shift, ALU.add, t)
            return t

        def rows_to_cols(piece, dst, n, *after):
            toks = []
            for k0 in range(0, n, 2):
                b = next_bank()
                bv = b.t[:, :].rearrange("p (k t) -> p k t", k=2)
                m = None
                for k in range(k0, min(k0 + 2, n)):
                    for i in range(TT):
                        m = turn(bv[:, k - k0, i * P:(i + 1) * P], piece(i, k), *after, *b.free)
                kk = min(2, n - k0)
                if (k0 // 2) % 2:
                    b.free = [v_copy(dst[:, k0:k0 + kk, :], bv[:, 0:kk, :], m, *after, chain=False)]
                else:
                    b.free = [a_fn(dst[:, k0:k0 + kk, :], bv[:, 0:kk, :], ACT.Copy, m, *after, chain=False)]
                toks += b.free
            return toks

        def strided(i, k):
            return h_rows[:, i, :].rearrange("p (f k) -> p k f", k=KD)[:, k, :]

        def product_rows(cols, n_k, weight, w_view, width, put, *after):
            for c0 in range(0, width, BANK):
                n = min(BANK, width - c0)
                s, got = load((lambda v, n=n: v[:, 0:n_k * n].rearrange("p (k n) -> p k n", k=n_k),
                               w_view(weight)[:, :, c0:c0 + n]))
                ws = s.t[:, 0:n_k * n].rearrange("p (k n) -> p k n", k=n_k)
                for i in range(TT):
                    b = next_bank()
                    m = mms(b.t[:, 0:n], [(cols[:, k, i * P:(i + 1) * P], ws[:, k, :]) for k in range(n_k)],
                            got, *after, *b.free)
                    b.free = [put(i, c0, n, b, m)]
                s.free = [m]
            return [b.free[0], m]

        by_p = lambda w: w.rearrange("(p k) n -> p k n", k=KD)
        by_k = lambda w: w.rearrange("(k p) n -> p k n", p=P)

        def residual(gate):
            def put(i, c0, n, b, m):
                tmp = h_rows[:, i, c0:c0 + n]
                t = v_tt(tmp, b.t[:, 0:n], gate[:, c0:c0 + n], ALU.mult, m)
                free = t
                v_tt(x[:, i, c0:c0 + n], x[:, i, c0:c0 + n], tmp, ALU.add, t)
                return free
            return put

        def route(logits, n_grp, per, comb, at, *after):
            n_exp = n_grp * per
            g, e = logits[:, :, 0:n_grp], logits[:, :, n_grp:n_grp + n_exp]
            s = lambda o, n: small[:, at + o:at + o + n]
            gmax, ex, gsum, picked = s(0, TT), s(8, TT * n_grp), s(16, TT), s(24, TT * n_grp)
            masked, hot1, hot2, top = s(40, TT * n_exp), s(104, TT * n_exp), s(168, TT * n_exp), s(232, 16)
            cnt = s(250, TT * n_exp)
            v3 = lambda ap, n: ap.rearrange("p (i n) -> p i n", i=TT)
            bc = lambda ap, n: ap.unsqueeze(2).to_broadcast([P, TT, n])

            def first_of(hot, values, best, n, t):
                t = v_tt(v3(hot, n), values, bc(best, n), ALU.is_equal, t)
                for i in range(TT):
                    h, c = v3(hot, n)[:, i, :], v3(cnt[:, 0:TT * n], n)[:, i, :]
                    t = dve(lambda h=h, c=c: nc.vector.tensor_tensor_scan(c, h, h, 0.0, ALU.add, ALU.bypass), t)
                c = cnt[:, 0:TT * n]
                return v_stt(hot, c, 1.0, hot, ALU.is_equal, ALU.mult, t)

            t = v_max(gmax, g, *after)
            t = v_tt(v3(ex, n_grp), g, bc(gmax, n_grp), ALU.subtract, t)
            t = a_fn(ex, ex, ACT.Exp, t)
            t = v_sum(gsum, v3(ex, n_grp), t)
            t = v_recip(gsum, gsum, t)
            t = first_of(picked, g, gmax, n_grp, t)
            t = v_ts(picked, picked, BIG, -BIG, ALU.mult, ALU.add, t)
            for i in range(TT):
                ei = e[:, i, :].rearrange("p (a b) -> p a b", a=n_grp)
                mi = v3(masked, n_exp)[:, i, :].rearrange("p (a b) -> p a b", a=n_grp)
                pi = v3(picked, n_grp)[:, i, :].unsqueeze(2).to_broadcast([P, n_grp, per])
                t = v_tt(mi, ei, pi, ALU.add, t)
            m1, m2, w1, w2 = top[:, 0:2], top[:, 2:4], top[:, 4:6], top[:, 6:8]
            t = v_max(m1, v3(masked, n_exp), t)
            t = first_of(hot1, v3(masked, n_exp), m1, n_exp, t)
            t = v_stt(masked, hot1, -2 * BIG, masked, ALU.mult, ALU.add, t)
            t = v_max(m2, v3(masked, n_exp), t)
            t = first_of(hot2, v3(masked, n_exp), m2, n_exp, t)
            t = v_tt(w2, m2, m1, ALU.subtract, t)
            t = a_fn(w2, w2, ACT.Exp, t)
            t = v_ts(w1, w2, 1.0, None, ALU.add, None, t)
            t = v_recip(w1, w1, t)
            t = v_tt(w1, w1, gsum, ALU.mult, t)
            t = v_tt(w2, w2, w1, ALU.mult, t)
            for i in range(TT):
                c = comb[:, i, 0:n_exp]
                t = v_ts(c, v3(hot1, n_exp)[:, i, :], w1[:, i:i + 1], None, ALU.mult, None, t)
                t = v_stt(c, v3(hot2, n_exp)[:, i, :], w2[:, i:i + 1], c, ALU.mult, ALU.add, t)
            return t

        def experts(layer, n_grp, per, ff, gate_w, up_w, down_w, wg, we, bg, be, *after):
            n_exp, n_ft = n_grp * per, ff // P
            route_w, route_b = cut(0, KD, n_grp + n_exp), cut(400, n_grp + n_exp)
            logits, comb = cut(440, TT, n_grp + n_exp), cut(520, TT, n_exp)
            got = side_load(layer + "_route", [
                (route_w[:, :, 0:n_grp], by_p(wg)), (route_w[:, :, n_grp:n_grp + n_exp], by_p(we)),
                (route_b[:, 0:n_grp], bg.partition_broadcast(P)),
                (route_b[:, n_grp:n_grp + n_exp], be.partition_broadcast(P))], *after)
            b = next_bank()
            for i in range(TT):
                m = mms(b.t[:, i * 64:i * 64 + n_grp + n_exp],
                        [(h_cols[:, k, i * P:(i + 1) * P], route_w[:, k, :]) for k in range(KD)],
                        got, *after, *b.free)
            bv = b.t[:, 0:TT * 64].rearrange("p (i n) -> p i n", i=TT)[:, :, 0:n_grp + n_exp]
            t = v_tt(logits, bv, route_b.unsqueeze(1).to_broadcast([P, TT, n_grp + n_exp]), ALU.add, m)
            b.free = [t]
            t = route(logits, n_grp, per, comb, 32, t)
            tap(layer + "_comb", comb, t)

            diag = [cut(1000 + 256 * j, TT, P) for j in range(2)]
            spread = [cut(1600 + 256 * j, TOKENS) for j in range(2)]
            gated = [cut(2200 + 256 * j, TOKENS) for j in range(3)]
            act_cols = [cut(3000 + 256 * j, TOKENS) for j in range(8)]
            diag_free, spread_free, gated_free, cols_free = [None] * 2, [None] * 2, [None] * 3, [None] * 8
            total, pair = banks[0:4], banks[4:7]
            spread_bank = banks[7]
            pending = []
            n = 0
            last = None

            def down(e, ft, s, got_down, tok, index, final):
                wd = s.t[:, (0 if n_ft == 4 else (e % 2) * 2048):][:, 0:n_ft * D].rearrange("p (k n) -> p k n", k=n_ft)
                col = act_cols[index % 8]
                m = None
                for i in range(TT):
                    for half in range(2):
                        tb = total[i * 2 + half]
                        first = e == 0 and ft == 0
                        m = mms(tb.t[:, :], [(col[:, i * P:(i + 1) * P], wd[:, ft, half * BANK:(half + 1) * BANK])],
                                tok, got_down, *(tb.free if first else []), start=first, stop=final,
                                signal=(i == TT - 1 and half == 1), loose=True)
                cols_free[index % 8] = m
                if ft == n_ft - 1 and (n_ft == 4 or e % 2 == 1):
                    s.free = [m]
                return m

            down_slot = None
            for e in range(n_exp):
                j = e % 2
                for i in range(TT):
                    dt = v_ts(diag[j][:, i, :], ident[:, :], comb[:, i, e:e + 1], None, ALU.mult, None,
                              diag_free[j], t if e == 0 else None, chain=(e == 0))
                for i in range(TT):
                    m = mms(spread_bank.t[:, i * P:(i + 1) * P], [(ones[:, :], diag[j][:, i, :])],
                            dt, *spread_bank.free)
                diag_free[j] = m
                sp = a_fn(spread[j], spread_bank.t[:, 0:TOKENS], ACT.Copy, m, spread_free[j], chain=False)
                spread_bank.free = [sp]
                if n_ft == 4:
                    s1, got1 = load((lambda v: v[:, :], gate_w[e].rearrange("(p k) f -> p (k f)", k=KD)))
                    s3, got3 = load((lambda v: v[:, :], up_w[e].rearrange("(p k) f -> p (k f)", k=KD)))
                    w1v = s1.t[:, :].rearrange("p (k f) -> p k f", k=KD)
                    w3v = s3.t[:, :].rearrange("p (k f) -> p k f", k=KD)
                    down_slot, got_down = load((lambda v: v[:, :].rearrange("p (k n) -> p k n", k=4), by_k(down_w[e])))
                else:
                    s1, got1 = load((lambda v: v[:, 0:2048], gate_w[e].rearrange("(p k) f -> p (k f)", k=KD)),
                                    (lambda v: v[:, 2048:4096], up_w[e].rearrange("(p k) f -> p (k f)", k=KD)))
                    s3, got3 = s1, got1
                    w1v = s1.t[:, 0:2048].rearrange("p (k f) -> p k f", k=KD)
                    w3v = s1.t[:, 2048:4096].rearrange("p (k f) -> p k f", k=KD)
                    if e % 2 == 0:
                        down_slot, got_down = load(*[
                            (lambda v, q=q: v[:, q * 2048:(q + 1) * 2048].rearrange("p (k n) -> p k n", k=2),
                             by_k(down_w[e + q])) for q in range(2)])
                for ft in range(n_ft):
                    b = pair[n % 3]
                    f = slice(ft * P, (ft + 1) * P)
                    mms(b.t[:, 0:TOKENS], [(w1v[:, k, f], h_cols[:, k, :]) for k in range(KD)], got1, *b.free)
                    m = mms(b.t[:, TOKENS:2 * TOKENS], [(w3v[:, k, f], h_cols[:, k, :]) for k in range(KD)], got3)
                    if ft == n_ft - 1:
                        s1.free = [m]
                        s3.free = [m]
                    g = gated[n % 3]
                    t1 = a_fn(g, b.t[:, 0:TOKENS], ACT.Silu, m, gated_free[n % 3], chain=False)
                    t2 = pool.put(lambda g=g, q=spread[j]: nc.gpsimd.tensor_tensor(g, g, q, ALU.mult), t1, sp)
                    t3 = v_tt(act_cols[n % 8], b.t[:, TOKENS:2 * TOKENS], g, ALU.mult, t2, cols_free[n % 8],
                              chain=False)
                    b.free = [t3]
                    gated_free[n % 3] = t3
                    if ft == n_ft - 1:
                        spread_free[j] = t2
                    pending.append((e, ft, down_slot, got_down, t3, n))
                    if len(pending) > 1:
                        last = down(*pending.pop(0), False)
                    n += 1
            last = down(*pending.pop(0), True)
            for i in range(TT):
                for half in range(2):
                    b = total[i * 2 + half]
                    put = residual(mod[:, 5, :])
                    b.free = [put(i, half * BANK, BANK, b, last)]
            return vector.last()

        def into_h_cols(*after):
            return rows_to_cols(strided, h_cols, KD, *after)

        def softmax_rows(scores, n, scale, probs, st, m, *after):
            t = v_max(st[:, 0:1], scores, m)
            t = v_ts(st[:, 1:2], st[:, 0:1], -scale, None, ALU.mult, None, t)
            e = a_fn(probs, scores, ACT.Exp, t, *after, scale=scale, bias=st[:, 1:2], accum_out=st[:, 2:3])
            t = v_recip(st[:, 3:4], st[:, 2:3], e)
            return e, v_ts(probs, probs, st[:, 3:4], None, ALU.mult, None, t)

        context = cut(7680, TT, D)
        ctx_cols = cut(9728, KD, TOKENS)
        ctx_mod = cut(11776, 2, D)
        rep, cond = cut(13824, KD, P), cut(14848, KD)
        rep_c, cond_c = cut(14880, KD, P), cut(15904, KD)
        rows = lambda ap: ap.rearrange("(i p) d -> p i d", p=P)
        got_x = side_load("x", [(x[:, :, :], rows(a["x"][0]))], lane=scalar)
        got_ctx = side_load("context", [(context, rows(a["ctx"][0]))], lane=scalar)
        got_w = side_load("norm_w", [(norm_w[:, 0, :], a["norm1_w"][0].partition_broadcast(P)),
                                     (norm_w[:, 1, :], a["norm2_w"][0].partition_broadcast(P))])
        c_cols = lambda v: v.rearrange("(p k) -> p k", k=KD)
        t_modc = modulation(c_cols(a["c_ctx"]), a["w_mod"][0][:, 0:2 * D], a["b_mod"][0][0:2 * D], ctx_mod, 2,
                            cond_c, rep_c, "ctx")
        t = norm_modulate(context, norm_w[:, 0, :], ctx_mod[:, 1, :], ctx_mod[:, 0, :], got_ctx, got_w, t_modc)
        t_ctx = rows_to_cols(strided, ctx_cols, KD, t)
        t_mod = modulation(c_cols(a["c"][0]), a["w_mod"][0], a["b_mod"][0], mod, 6, cond, rep, "mod")
        t = norm_modulate(x, norm_w[:, 0, :], mod[:, 1, :], mod[:, 0, :], got_x, t_mod, *t_ctx)
        tap("h", h_rows[:, :, :], t)
        t_h = into_h_cols(t)

        proj = cut(0, TT, IN_W)
        ctx_proj = cut(5120, TT, CTX_W)
        flip = [0]

        def copy_out(dst_of):
            def put(i, c0, n, b, m):
                flip[0] ^= 1
                if flip[0]:
                    return v_copy(dst_of(i, c0, n), b.t[:, 0:n], m, chain=False)
                return a_fn(dst_of(i, c0, n), b.t[:, 0:n], ACT.Copy, m, chain=False)
            return put

        for c0 in range(0, IN_W, BANK):
            s, got = load((lambda v: v[:, :].rearrange("p (k n) -> p k n", k=KD),
                           by_p(a["w_in"][0])[:, :, c0:c0 + BANK]))
            ws = s.t[:, :].rearrange("p (k n) -> p k n", k=KD)
            lo, hi = max(c0, OFF_KV), min(c0 + BANK, OFF_G)
            put_x = copy_out(lambda i, c, n: proj[:, i, c:c + n])
            put_c = copy_out(lambda i, c, n: ctx_proj[:, i, c:c + n])
            for i in range(TT):
                b = next_bank()
                m = mms(b.t[:, :], [(h_cols[:, k, i * P:(i + 1) * P], ws[:, k, :]) for k in range(KD)],
                        got, *t_h, *b.free)
                b.free = [put_x(i, c0, BANK, b, m)]
                if lo < hi:
                    b = next_bank()
                    m = mms(b.t[:, 0:hi - lo],
                            [(ctx_cols[:, k, i * P:(i + 1) * P], ws[:, k, lo - c0:hi - c0]) for k in range(KD)],
                            *t_ctx, *b.free)
                    b.free = [put_c(i, lo - OFF_KV, hi - lo, b, m)]
            s.free = [m]
        projected = everyone()
        tap("p", proj, *projected)
        tap("pc", ctx_proj, *projected)

        mix_cols = h_cols
        ws_t = cut(7680, A_HEADS, P)
        bs_cols = cut(8192, A_HEADS)
        gelu = cut(8200, TT, OFF_B)
        sq = cut(9224, 16, HD)
        got = side_load("chunk", [(ws_t, a["w_s_t"]), (bs_cols, a["b_s_t"])], *projected)
        t = a_fn(gelu, proj[:, :, 0:OFF_B], ACT.Gelu_apprx_tanh, *projected)
        ya = h_rows[:, :, 0:256]
        for i in range(TT):
            v = gelu[:, i, 256:512].rearrange("p (h d) -> p h d", h=A_HEADS)
            t = head_norm(v, v, A_HEADS, HD, None, sq[:, 0:A_HEADS, :], small[:, 8:12], t, *projected)
            b = next_bank()
            for h in range(A_HEADS):
                m = mms(b.t[:, h * HD:(h + 1) * HD], [(ws_t[:, h, :], v[:, h, :])], got, t, *b.free)
            for h in range(A_HEADS):
                f = slice(h * HD, (h + 1) * HD)
                b.free = [v_stt(ya[:, i, f], b.t[:, f], bs_cols[:, h:h + 1], gelu[:, i, f], ALU.add, ALU.mult, m, got)]
        t_a = b.free[0]
        b = next_bank()
        bv = b.t[:, :].rearrange("p (k t) -> p k t", k=2)
        for k in range(2):
            for i in range(TT):
                m = turn(bv[:, k, i * P:(i + 1) * P], ya[:, i, k * P:(k + 1) * P], t_a, *b.free)
        b.free = [a_fn(mix_cols[:, 0:2, :], bv, ACT.Copy, m)]
        done_a = everyone()

        axial = cut(7680, TT, 2, HD)
        qk_w = cut(7936, 10, HD)
        rot = cut(8576, 10, HD)
        sq = cut(9216, 10, HD)
        q_cols = cut(9856, 4, TOKENS)
        k_cols = cut(10880, B_KV, 2 * TOKENS)
        k_pair = cut(11904, 2 * TT, B_KV, 2, HD)
        probs = [cut(12928 + 512 * j, 512) for j in range(3)]
        probs_t = [cut(14464 + 1024 * j, 4, TOKENS) for j in range(2)]
        got = side_load("attention", [
            (axial, a["k_axial"].rearrange("p (i c d) -> p i c d", i=TT, c=2))]
            + [(qk_w[:, h, :], a["q_norm_w" if h < B_HEADS else "k_norm_w"][0].partition_broadcast(P))
               for h in range(10)], *done_a)
        vector.wait(got, *done_a)
        for i in range(TT):
            qk = proj[:, i, OFF_B:OFF_KV + 128].rearrange("p (h d) -> p h d", h=10)
            t = head_norm(qk, qk, 10, HD, qk_w, sq, small[:, 8:18])
            x4 = qk.rearrange("p h (a s e) -> p (h a) s e", a=2, s=2)
            r4 = rot.rearrange("p h (a s e) -> p (h a) s e", a=2, s=2)
            t = v_copy(r4[:, :, 0, :], x4[:, :, 1, :])
            t = v_copy(r4[:, :, 1, :], x4[:, :, 0, :])
            t = v_tt(rot, rot, axial[:, i, 1, :].unsqueeze(1).to_broadcast([P, 10, HD]), ALU.mult)
            t = v_tt(qk, qk, axial[:, i, 0, :].unsqueeze(1).to_broadcast([P, 10, HD]), ALU.mult)
            t = v_tt(qk, qk, rot, ALU.add)
            kk = ctx_proj[:, i, 0:128].rearrange("p (h d) -> p h d", h=2)
            t = head_norm(kk, kk, 2, HD, qk_w[:, 8:10, :], sq[:, 0:2, :], small[:, 8:10])
            for c in range(2):
                t = v_copy(k_pair[:, i, :, c, :], proj[:, i, OFF_KV:OFF_KV + 128].rearrange("p (h d) -> p h d", h=2))
                t = v_copy(k_pair[:, TT + i, :, c, :], kk)
        t_qk = t
        t_q = rows_to_cols(lambda i, k: proj[:, i, OFF_B + k * P:OFF_B + (k + 1) * P], q_cols, 4, t_qk)
        t_k = []
        for g in range(B_KV):
            b = next_bank()
            for i in range(2 * TT):
                m = turn(b.t[:, i * P:(i + 1) * P], k_pair[:, i, g].rearrange("p a b -> p (a b)"), t_qk, *b.free)
            b.free = [v_copy(k_cols[:, g, :], b.t[:, :], m)]
            t_k += b.free
        scale = HD ** -0.5
        jobs = [(h, i) for h in range(B_HEADS) for i in range(TT)]
        probs_free, probs_t_free = [None] * 3, [None] * 2
        state = {}

        def scores_of(n):
            h, i = jobs[n]
            part = slice(64 * (h % 2), 64 * (h % 2) + 64)
            b = next_bank()
            m = mms(b.t[:, :], [(q_cols[part, h // 2, i * P:(i + 1) * P], k_cols[part, h // 4, :])],
                    *t_q, *t_k, *b.free)
            state[n] = (b, m)

        def attend(n):
            h, i = jobs[n]
            b, m = state[n]
            pr, pt = probs[n % 3], probs_t[h % 2]
            e, t = softmax_rows(b.t[:, :], 512, scale, pr, small[:, 32 + 4 * (n % 4):36 + 4 * (n % 4)], m, probs_free[n % 3])
            b.free = [e]
            b2 = next_bank()
            for kt in range(4):
                m = turn(b2.t[:, kt * P:(kt + 1) * P], pr[:, kt * P:(kt + 1) * P], t, *b2.free)
            probs_free[n % 3] = m
            tc = a_fn(pt[:, :, i * P:(i + 1) * P], b2.t[:, :].rearrange("p (k t) -> p k t", k=4), ACT.Copy, m,
                      probs_t_free[h % 2])
            b2.free = [tc]
            if i == TT - 1:
                b3 = next_bank()
                part = slice(64 * (h % 2), 64 * (h % 2) + 64)
                g = h // 4
                vals = [proj[:, kt, OFF_KV + 128 + g * HD:OFF_KV + 128 + (g + 1) * HD] for kt in range(TT)] + \
                       [ctx_proj[:, kt, 128 + g * HD:128 + (g + 1) * HD] for kt in range(TT)]
                m = mms(b3.t[part, 0:TOKENS], [(vals[kt], pt[:, kt, :]) for kt in range(4)], tc, *b3.free)
                probs_t_free[h % 2] = m
                b3.free = [v_copy(mix_cols[part, 2 + h // 2, :], b3.t[part, 0:TOKENS], m)]

        scores_of(0)
        for n in range(len(jobs)):
            if n + 1 < len(jobs):
                scores_of(n + 1)
            attend(n)
        done_b = everyone()

        s_scan, got_scan = load((lambda v: v[:, 0:4096], a["k_scan"]))
        kc = s_scan.t
        sums = [kc[:, 0:1024], kc[:, 1024:2048]]
        after = [kc[:, 2048:2176], kc[:, 2176:2304]]
        masks = [kc[:, 2304 + d * 896:2304 + (d + 1) * 896].rearrange("p (j t) -> p j t", j=LEVELS) for d in range(2)]
        logf = cut(7680, 2 * TT, 2, CW)
        keys = cut(9728, 2 * TT, 2, CW)
        lb = cut(11776, 4, 2, CW)
        q_act = h_rows[:, :, 0:256]
        tmp1 = h_rows[:, 0, 256:768].rearrange("p (a b) -> p a b", a=2)
        tmp2 = h_rows[:, 1, 256:768].rearrange("p (a b) -> p a b", a=2)
        got = side_load("bounds", [(lb[:, 0], a["hgrn_lb_logits"][0].partition_broadcast(P))], *done_b)
        scalar.wait(*done_b)
        t = v_tt(lb[:, 1], lb[:, 0], lb[:, 0], ALU.subtract, got, *done_b)
        t = a_fn(lb[:, 1], lb[:, 1], ACT.Exp, t)
        t = v_recip(lb[:, 2], lb[:, 1], t)
        t = v_tt(lb[:, 1], lb[:, 1], lb[:, 2], ALU.mult, t)
        t = v_tt(lb[:, 1], lb[:, 1], lb[:, 1], ALU.subtract, t)
        t = v_ts(lb[:, 2], lb[:, 1], -1.0, 1.0, ALU.mult, ALU.add, t)
        t_lb = a_fn(lb[:, 3], lb[:, 2], ACT.Ln, t)
        zs = [proj[:, i, OFF_C + CW:OFF_C + 3 * CW].rearrange("p (a b) -> p a b", a=2) for i in range(TT)] + \
             [ctx_proj[:, i, 256 + CW:256 + 3 * CW].rearrange("p (a b) -> p a b", a=2) for i in range(TT)]
        for n, z in enumerate(zs):
            t = a_fn(tmp1, z, ACT.Abs, t_lb, vector.last())
            t = a_fn(tmp1, tmp1, ACT.Exp, scale=-1.0)
            t = a_fn(tmp1, tmp1, ACT.Ln, bias=1.0)
            t = v_stt(logf[:, n], z, 0.0, tmp1, ALU.min, ALU.subtract, t)
            t = v_tt(logf[:, n], logf[:, n], lb[:, 3], ALU.add, t)
        for n, z in enumerate(zs):
            t = a_fn(keys[:, n], z, ACT.Sigmoid, scale=-1.0)
            t = v_tt(keys[:, n], keys[:, n], lb[:, 2], ALU.mult, t)
        t_q = a_fn(q_act, proj[:, :, OFF_C:OFF_C + CW], ACT.Silu)
        t_in = [t, t_q]

        q_c = cut(11776, 2, TOKENS)
        k_c = [cut(12288 + 512 * d, 2, TOKENS) for d in range(2)]
        gates = cut(13312, 8, 2, TOKENS)
        att = [h_rows[:, par, 256:768].rearrange("p (c t) -> p c t", c=4) for par in range(2)]
        rows64 = [slice(0, 64), slice(64, 128)]
        vector.wait(t_q)
        t_q = rows_to_cols(lambda i, k: q_act[:, i, k * P:(k + 1) * P], q_c, 2, *t_in)
        t_k = []
        for d in range(2):
            t_k += rows_to_cols(lambda i, k: keys[:, i, d, k * P:(k + 1) * P], k_c[d], 2, *t_in)
        ksum = gates[:, 0]
        t = v_tt(ksum, k_c[0], k_c[1], ALU.add, *t_k)
        blocks = [(i, pair_) for i in range(TT) for pair_ in range(2)]
        for par in range(2):
            b = next_bank()
            for c, (i, pair_) in enumerate(blocks):
                m = mms(b.t[:, c * P:(c + 1) * P],
                        [(ksum[rows64[par], pair_, i * P:(i + 1) * P], q_c[rows64[par], pair_, i * P:(i + 1) * P])],
                        t, *t_q, *t_in, *b.free)
            b.free = [v_tt(att[par], b.t[:, :].rearrange("p (c t) -> p c t", c=4),
                           ident[:, :].unsqueeze(1).to_broadcast([P, 4, P]), ALU.mult, m)]
        q_in = [proj[:, :, 0:256], proj[:, :, 256:512]]
        for d in range(2):
            gate_free = [tensor.last(), vector.last()]
            t_g = []
            for pair_ in range(2):
                for i in range(TT):
                    for half in range(2):
                        b = next_bank()
                        m = mms(b.t[:, :], [(logf[:, i, d, pair_ * P:(pair_ + 1) * P],
                                             sums[d][:, half * BANK:(half + 1) * BANK])], got_scan, *t_in, *b.free)
                        b.free = [a_fn(gates[:, half * 4:half * 4 + 4, pair_, i * P:(i + 1) * P],
                                       b.t[:, :].rearrange("p (j t) -> p j t", j=4), ACT.Exp, m, *gate_free)]
            t_g = b.free[0]
            for j in range(LEVELS):
                w = 1 << j
                cutj = lambda ap: ap.rearrange("p a (b s w) -> p (a b) s w", s=2, w=w)
                gj, qj, kj = cutj(gates[:, j]), cutj(q_c), cutj(k_c[d])
                qs, ks = (1, 0) if d == 0 else (0, 1)
                t = v_tt(gj[:, :, qs, :], gj[:, :, qs, :], qj[:, :, qs, :], ALU.mult, t_g, *t_q)
                t = v_tt(gj[:, :, ks, :], gj[:, :, ks, :], kj[:, :, ks, :], ALU.mult, *t_k)
                mask = masks[d][:, j, :].bitcast(U32).unsqueeze(1).to_broadcast([P, 4, P])
                for par in range(2):
                    b = next_bank()
                    for c, (i, pair_) in enumerate(blocks):
                        g = gates[rows64[par], j, pair_, i * P:(i + 1) * P]
                        m = mms(b.t[:, c * P:(c + 1) * P], [(g, g)], t, *b.free)
                    b.free = [dve(lambda par=par, b=b, mask=mask: nc.vector.copy_predicated(
                        att[par], mask, b.t[:, :].rearrange("p (c t) -> p c t", c=4)), m, got_scan)]
            t = v_tt(q_in[d], gates[:, 7], q_c, ALU.mult)
        t_att = t

        st_free = everyone()
        vals = [proj[:, i, OFF_C + 3 * CW:OFF_C + 4 * CW] for i in range(TT)] + \
               [ctx_proj[:, i, 256 + 3 * CW:256 + 4 * CW] for i in range(TT)]
        st = [[gates[:, 2 * d + j].rearrange("p a b -> p (a b)")[:, 0:128].rearrange("p (a b) -> p a b", a=2)
               for j in range(2)] for d in range(2)]
        order = [[2, 3, 0], [3, 2, 1]]
        state_at = {}
        for d in range(2):
            for step, n in enumerate(order[d]):
                b = next_bank()
                m = mms(b.t[:, 0:CW], [(after[d], logf[:, n, d, :])], got_scan, *t_in, *b.free)
                for pair_ in range(2):
                    m = mms(b.t[:, CW + 2 * pair_:CW + 2 * pair_ + 1],
                            [(logf[:, n, d, pair_ * P:(pair_ + 1) * P], ones[:, 0:1])])
                te = a_fn(small[:, 60:62], b.t[:, CW:CW + 4:2], ACT.Exp, m, vector.last())
                t = a_fn(gates[:, 5, 0, :], b.t[:, 0:CW], ACT.Exp, vector.last())
                b.free = [t]
                t = v_tt(keys[:, n, d, :], keys[:, n, d, :], gates[:, 5, 0, :], ALU.mult, t, *st_free)
                b = next_bank()
                for h in range(C_HEADS):
                    part = slice(64 * (h % 2), 64 * (h % 2) + 64)
                    m = mms(b.t[part, (h // 2) * HD:(h // 2 + 1) * HD],
                            [(keys[:, n, d, h * HD:(h + 1) * HD], vals[n][:, h * HD:(h + 1) * HD])], t, *b.free)
                new = st[d][step % 2]
                bv = b.t[:, 0:2 * HD].rearrange("p (a b) -> p a b", a=2)
                if step == 0:
                    b.free = [v_copy(new, bv, m, *st_free)]
                else:
                    old = st[d][(step - 1) % 2]
                    for pair_ in range(2):
                        b.free = [v_stt(new[:, pair_, :], old[:, pair_, :], small[:, 60 + pair_:61 + pair_],
                                        bv[:, pair_, :], ALU.mult, ALU.add, m, te, *st_free)]
                if step >= 1:
                    tile = (0 if step == 1 else 1) if d == 0 else (1 if step == 1 else 0)
                    state_at[d, tile] = (new, b.free[0])
        o_rows = gates[:, 6:8].rearrange("p j a b -> p (j a b)")[:, 0:512].rearrange("p (i c) -> p i c", i=TT)
        for i in range(TT):
            for par in range(2):
                b = next_bank()
                for pair_ in range(2):
                    h = 2 * pair_ + par
                    o_part = b.t[:, pair_ * HD:(pair_ + 1) * HD]
                    m = mms(o_part, [(att[par][:, 2 * i + pair_, :], vals[i][:, h * HD:(h + 1) * HD])],
                            t_att, state_at[0, i][1], state_at[1, i][1], *b.free, stop=False)
                    m = mms(o_part, [(q_in[d][rows64[par], pair_, i * P:(i + 1) * P],
                                      state_at[d, i][0][rows64[par], pair_, :]) for d in range(2)], start=False)
                o4 = o_rows[:, i, :].rearrange("p (a b d) -> p a b d", a=2, b=2)
                b.free = [v_copy(o4[:, :, par, :], b.t[:, 0:P].rearrange("p (a d) -> p a d", a=2), m)]
        tap("o", o_rows, b.free[0])
        s_scan.free = everyone()
        w_c = cut(9728, C_HEADS, HD)
        sq = cut(9984, C_HEADS, HD)
        sil = cut(10240, TT, CW)
        got = side_load("hgrn_w", [(w_c[:, h, :], a["hgrn_norm_w"][0].partition_broadcast(P)) for h in range(C_HEADS)],
                        *everyone())
        t = a_fn(sil, proj[:, :, OFF_G:IN_W], ACT.Silu, *everyone())
        vector.wait(got, t)
        for i in range(TT):
            o = o_rows[:, i, :].rearrange("p (h d) -> p h d", h=C_HEADS)
            t = head_norm(o, o, C_HEADS, HD, w_c, sq, small[:, 8:12])
            t = v_tt(o_rows[:, i, :], o_rows[:, i, :], sil[:, i, :], ALU.mult)
        t = rows_to_cols(lambda i, k: o_rows[:, i, k * P:(k + 1) * P], mix_cols[:, 6:8, :], 2, t)
        mixed = everyone()
        tap("mix", mix_cols[:, :, :], *mixed)

        product_rows(mix_cols, KD, a["w_out"][0], by_k, D, residual(mod[:, 2, :]), *mixed)
        done = everyone()
        tap("x1", x[:, :, :], *done)
        t = norm_modulate(x, norm_w[:, 1, :], mod[:, 4, :], mod[:, 3, :], *done)
        t = into_h_cols(t, *done)
        experts("one", 4, 8, 512, a["w1"][0], a["w3"][0], a["w2"][0], a["w_grp"][0], a["w_exp"][0],
                a["b_grp"][0], a["b_exp"][0], *t, *everyone())
        done = everyone()
        tap("xa", x[:, :, :], *done)

        for layer in range(2):
            name = f"two{layer}"
            rep, cond = cut(0, KD, P), cut(1024, KD)
            got_w = side_load(name + "_norm_w", [
                (norm_w[:, 0, :], a["norm_mix_g_2"][layer].partition_broadcast(P)),
                (norm_w[:, 1, :], a["norm_ffn_g_2"][layer].partition_broadcast(P))], *done)
            t_mod = modulation(c_cols(a["c_2"][0]), a["ada_w_2"][layer], a["ada_b_2"][layer], mod, 6, cond, rep,
                               name, *done)
            t = norm_modulate(x, norm_w[:, 0, :], mod[:, 1, :], mod[:, 0, :], got_w, t_mod, *done)
            t_h = into_h_cols(t, *done)
            ready = everyone()

            if layer == 0:
                lat = cut(0, TT, 448)
                cq_c, ckv_c = cut(896, 2, TOKENS), cut(1408, 1, TOKENS)
                q = cut(1664, TT, 1536)
                kv = cut(4736, TT, 2048)
                q_pe = cut(8832, TT, 8, ROPE)
                k_pe2 = cut(9856, TT, 2, ROPE)
                qn_c, qp_c = cut(10112, 8, TOKENS), cut(12160, 4, TOKENS)
                kn_c, kp_c = cut(13184, 8, TOKENS), cut(15232, 1, TOKENS)
                pr = [cut(15488 + 256 * j, TOKENS) for j in range(3)]
                pt = [cut(16256 + 512 * j, TT, TOKENS) for j in range(2)]
                w_lat = h_rows[:, 0, 0:384]
                w_q, w_k = h_rows[:, 0, 384:576], h_rows[:, 0, 576:768]
                ang, cs, sn, red = (cut(17280 + 64 * j, TT, HALF) for j in range(4))
                pos_i, freq = h_rows[:, 0, 768:770].bitcast(I32), h_rows[:, 0, 800:832]
                pos_f = h_rows[:, 0, 770:772]
                sq = h_rows[:, 1, :]
                got = side_load("latent", [
                    (w_lat[:, 0:Q_LORA], a["mla_q_a_g_2"][0].partition_broadcast(P)),
                    (w_lat[:, Q_LORA:384], a["mla_kv_a_g_2"][0].partition_broadcast(P)),
                    (w_q, a["mla_q_norm_g_2"][0].partition_broadcast(P)),
                    (w_k, a["mla_k_norm_g_2"][0].partition_broadcast(P)),
                    (pos_i, a["positions_2_cols"]), (freq, a["k_freq"])], *ready)
                vector.wait(got)
                t = v_copy(pos_f, pos_i, *ready)
                for i in range(TT):
                    t = v_ts(ang[:, i, :], freq, pos_f[:, i:i + 1], None, ALU.mult, None)
                for dst, turns in ((sn, 0.0), (cs, 0.25)):
                    t = v_ts(red, ang, float(1 / (2 * np.pi)), turns, ALU.mult, ALU.add)
                    t = v_ts(red, red, ROUND, -ROUND, ALU.add, ALU.add)
                    t = v_stt(dst, red, -TWO_PI_1, ang, ALU.mult, ALU.add)
                    t = v_stt(dst, red, -TWO_PI_2, dst, ALU.mult, ALU.add)
                    t = v_stt(dst, red, -TWO_PI_3, dst, ALU.mult, ALU.add)
                    t = v_ts(dst, dst, float(np.pi / 2) * turns * 4, PI_IN, ALU.add, ALU.min)
                    t = v_ts(dst, dst, -PI_IN, None, ALU.max, None)
                    t_trig = a_fn(dst, dst, ACT.Sin, t)

                product_rows(h_cols, KD, a["mla_w_down_2"][0], by_p, 448,
                             copy_out(lambda i, c, n: lat[:, i, c:c + n]), *t_h)
                vector.wait(*everyone())
                for i in range(TT):
                    g3 = lambda ap, g: ap.rearrange("p (g w) -> p g w", g=g)
                    for lo, hi in ((0, Q_LORA), (Q_LORA, 384)):
                        t = head_norm(g3(lat[:, i, lo:hi], 1), g3(lat[:, i, lo:hi], 1), 1, hi - lo,
                                      g3(w_lat[:, lo:hi], 1), g3(sq[:, 0:hi - lo], 1), small[:, 8:9], t_trig)
                    t = head_norm(g3(lat[:, i, 384:448], 1), g3(lat[:, i, 384:448], 1), 1, ROPE,
                                  g3(w_k[:, NOPE:], 1), g3(sq[:, 0:ROPE], 1), small[:, 8:9])
                    x1_, x2_ = lat[:, i, 384:416], lat[:, i, 416:448]
                    c_, s_ = cs[:, i, :], sn[:, i, :]
                    u1, u2 = sq[:, 0:32], sq[:, 32:64]
                    o1, o2 = k_pe2[:, i, 0, 0:32], k_pe2[:, i, 0, 32:64]
                    v_tt(u1, x1_, c_, ALU.mult)
                    v_tt(u2, x2_, s_, ALU.mult)
                    v_tt(o1, u1, u2, ALU.subtract)
                    v_tt(u1, x1_, s_, ALU.mult)
                    v_tt(u2, x2_, c_, ALU.mult)
                    v_tt(o2, u1, u2, ALU.add)
                    t = v_copy(k_pe2[:, i, 1, :], k_pe2[:, i, 0, :])
                t_cq = rows_to_cols(lambda i, k: lat[:, i, k * P:(k + 1) * P], cq_c, 2, t)
                t_ckv = rows_to_cols(lambda i, k: lat[:, i, Q_LORA:384], ckv_c, 1, t)
                t_kp = rows_to_cols(lambda i, k: k_pe2[:, i].rearrange("p a b -> p (a b)"), kp_c, 1, t)
                product_rows(cq_c, 2, a["mla_w_uq_2"][0], by_k, 1536,
                             copy_out(lambda i, c, n: q[:, i, c:c + n]), *t_cq)
                product_rows(ckv_c, 1, a["mla_w_ukv_2"][0], by_k, 2048,
                             copy_out(lambda i, c, n: kv[:, i, c:c + n]), *t_ckv)
                vector.wait(*everyone())
                for i in range(TT):
                    qi = q[:, i, :].rearrange("p (h d) -> p h d", h=8)
                    ki = kv[:, i, :].rearrange("p (h d) -> p h d", h=8)
                    sq3 = sq.rearrange("p (h d) -> p h d", h=8)
                    bw = lambda ap, n: ap.unsqueeze(1).to_broadcast([P, 8, n])
                    head_norm(qi[:, :, 0:NOPE], qi[:, :, 0:NOPE], 8, NOPE, bw(w_q[:, 0:NOPE], NOPE), sq3, small[:, 8:16])
                    head_norm(ki[:, :, 0:NOPE], ki[:, :, 0:NOPE], 8, NOPE, bw(w_k[:, 0:NOPE], NOPE), sq3, small[:, 8:16])
                    head_norm(qi[:, :, NOPE:], qi[:, :, NOPE:], 8, ROPE, bw(w_q[:, NOPE:], ROPE), sq3[:, :, 0:ROPE],
                              small[:, 8:16])
                    x1_, x2_ = qi[:, :, NOPE:NOPE + 32], qi[:, :, NOPE + 32:]
                    c_, s_ = bw(cs[:, i, :], HALF), bw(sn[:, i, :], HALF)
                    u1, u2 = sq3[:, :, 0:32], sq3[:, :, 32:64]
                    v_tt(u1, x1_, c_, ALU.mult)
                    v_tt(u2, x2_, s_, ALU.mult)
                    v_tt(q_pe[:, i, :, 0:32], u1, u2, ALU.subtract)
                    v_tt(u1, x1_, s_, ALU.mult)
                    v_tt(u2, x2_, c_, ALU.mult)
                    t = v_tt(q_pe[:, i, :, 32:64], u1, u2, ALU.add)
                t_qn = rows_to_cols(lambda i, h: q[:, i, h * 192:h * 192 + NOPE], qn_c, 8, t)
                t_kn = rows_to_cols(lambda i, h: kv[:, i, h * 256:h * 256 + NOPE], kn_c, 8, t)
                t_qp = rows_to_cols(lambda i, k: q_pe[:, i, 2 * k:2 * k + 2, :].rearrange("p a b -> p (a b)"),
                                    qp_c, 4, t)
                out_c = h_cols
                scale = (NOPE + ROPE) ** -0.5
                jobs = [(h, i) for h in range(8) for i in range(TT)]
                pr_free, pt_free, state = [None] * 3, [None] * 2, {}

                def scores2(n):
                    h, i = jobs[n]
                    part = slice(64 * (h % 2), 64 * (h % 2) + 64)
                    b = next_bank()
                    mms(b.t[:, 0:TOKENS], [(qn_c[:, h, i * P:(i + 1) * P], kn_c[:, h, :])],
                        *t_qn, *t_kn, *b.free, stop=False)
                    m = mms(b.t[:, 0:TOKENS], [(qp_c[part, h // 2, i * P:(i + 1) * P], kp_c[part, 0, :])],
                            *t_qp, *t_kp, start=False)
                    state[n] = (b, m)

                def attend2(n):
                    h, i = jobs[n]
                    b, m = state[n]
                    r, tr = pr[n % 3], pt[h % 2]
                    e, t = softmax_rows(b.t[:, 0:TOKENS], TOKENS, scale, r,
                                        small[:, 32 + 4 * (n % 4):36 + 4 * (n % 4)], m, pr_free[n % 3])
                    b.free = [e]
                    b2 = next_bank()
                    for kt in range(TT):
                        m = turn(b2.t[:, kt * P:(kt + 1) * P], r[:, kt * P:(kt + 1) * P], t, *b2.free)
                    pr_free[n % 3] = m
                    tc = a_fn(tr[:, :, i * P:(i + 1) * P], b2.t[:, 0:TOKENS].rearrange("p (k t) -> p k t", k=TT),
                              ACT.Copy, m, pt_free[h % 2])
                    b2.free = [tc]
                    if i == TT - 1:
                        b3 = next_bank()
                        m = mms(b3.t[:, 0:TOKENS], [(kv[:, kt, h * 256 + NOPE:(h + 1) * 256], tr[:, kt, :])
                                                    for kt in range(TT)], tc, *b3.free)
                        pt_free[h % 2] = m
                        b3.free = [v_copy(out_c[:, h, :], b3.t[:, 0:TOKENS], m)]

                scores2(0)
                for n in range(len(jobs)):
                    if n + 1 < len(jobs):
                        scores2(n + 1)
                    attend2(n)
                product_rows(out_c, KD, a["mla_w_o_2"][0], by_k, D, residual(mod[:, 2, :]), *everyone())
            else:
                u = cut(0, 24, TOKENS)
                params = cut(6144, 5, 24)
                padded = [cut(6272 + 264 * j, 264) for j in range(3)]
                hidden = cut(7064, TOKENS)
                red = cut(7320, TOKENS)
                f_small = cut(7576, 208)
                kr, ki, kn = cut(7784, TT, D), cut(9832, TT, D), cut(11880, 1, D)
                hf, hb = cut(12904, TT, BANK), cut(13928, TT, BANK)
                ab = cut(14952, TT, BANK)
                spec, prod = cut(12904, 4, BANK), cut(14952, 4, BANK)
                norm_r = cut(17000, BANK)
                bias = norm_w[0:1, 0, :]
                got = side_load("hyena", [
                    (params.rearrange("p a b -> p (a b)"), a["hy_cols"]),
                    (f_small[0:33, 0:64], a["hy_f_w1_2"][0]), (f_small[0:64, 64:128], a["hy_f_w2_2"][0]),
                    (f_small[0:64, 128:192], a["hy_f_w3_2"][0]), (f_small[0:64, 192:198], a["hy_f_cols"]),
                    (red[0:33, :], a["k_feats"]),
                ], *ready)
                tensor.wait(got)
                zeroed = [dve(lambda q=q: nc.vector.memset(q, 0.0), *ready) for q in padded]
                vector.wait(got)
                scalar.wait(got)
                pad_free = [zeroed[-1]] * 3
                wv = by_p(a["hy_w_in_2"][0])
                n = 0
                for c0 in range(0, 3 * D, BANK):
                    s, got_s = load((lambda v: v[:, :].rearrange("p (k n) -> p k n", k=KD), wv[:, :, c0:c0 + BANK]))
                    ws = s.t[:, :].rearrange("p (k n) -> p k n", k=KD)
                    for f in range(4):
                        b = next_bank()
                        m = mms(b.t[:, 0:TOKENS], [(ws[:, k, f * P:(f + 1) * P], h_cols[:, k, :]) for k in range(KD)],
                                got_s, *t_h, *b.free)
                        pd = padded[n % 3]
                        t = a_fn(pd[:, 1:257], b.t[:, 0:TOKENS], ACT.Identity, m, pad_free[n % 3],
                                 bias=params[:, 0, n:n + 1], chain=False)
                        b.free = [t]
                        v_ts(u[:, n, :], pd[:, 1:257], params[:, 2, n:n + 1], params[:, 4, n:n + 1], ALU.mult, ALU.add, t)
                        v_stt(u[:, n, :], pd[:, 0:256], params[:, 1, n:n + 1], u[:, n, :], ALU.mult, ALU.add)
                        pad_free[n % 3] = v_stt(u[:, n, :], pd[:, 2:258], params[:, 3, n:n + 1], u[:, n, :],
                                                ALU.mult, ALU.add)
                        n += 1
                    s.free = [m]
                tap("u", u, vector.last())
                for l, (w_l, src, rows_n) in enumerate(((f_small[0:33, 0:64], red, 33), (f_small[0:64, 64:128], hidden, 64),
                                                        (f_small[0:64, 128:192], hidden, 64))):
                    b = next_bank()
                    m = mms(b.t[0:64, 0:TOKENS], [(w_l, src[0:rows_n, :])], vector.last(), scalar.last(), *b.free)
                    hd, rd = hidden[0:64, :], red[0:64, :]
                    t = v_ts(hd, b.t[0:64, 0:TOKENS], f_small[0:64, 192 + 2 * l:193 + 2 * l],
                             f_small[0:64, 193 + 2 * l:194 + 2 * l], ALU.add, ALU.mult, m)
                    b.free = [t]
                    v_ts(rd, hd, float(1 / (2 * np.pi)), ROUND, ALU.mult, ALU.add)
                    v_ts(rd, rd, -ROUND, None, ALU.add, None)
                    v_stt(hd, rd, -TWO_PI_1, hd, ALU.mult, ALU.add)
                    v_stt(hd, rd, -TWO_PI_2, hd, ALU.mult, ALU.add)
                    v_stt(hd, rd, -TWO_PI_3, hd, ALU.mult, ALU.add)
                    t = v_ts(hd, hd, PI_IN, -PI_IN, ALU.min, ALU.max)
                    t = a_fn(hd, hd, ACT.Sin, t)
                s_four, got_four = load((lambda v: v[:, :], a["k_fourier"]))
                s_w4, got_w4 = load((lambda v: v[0:64, :], a["hy_f_w4_2"][0]))
                fc = s_four.t
                ahead = fc[:, 0:1024].rearrange("p (k f) -> p k f", k=TT)
                back = fc[:, 1024:2048].rearrange("p (k t) -> p k t", k=4)
                decay = fc[:, 2048:4096].rearrange("p (k d) -> p k d", k=TT)
                z_rows = h_rows
                def cols_to_rows(src, after_):
                    toks = []
                    for i in range(TT):
                        for q4 in range(2):
                            b = next_bank()
                            for k in range(4):
                                m = turn(b.t[:, k * P:(k + 1) * P], src(q4 * 4 + k)[:, i * P:(i + 1) * P], *after_, *b.free)
                            b.free = [a_fn(z_rows[:, i, q4 * BANK:(q4 + 1) * BANK], b.t[:, :], ACT.Copy, m)]
                            toks += b.free
                    return toks
                done_u = everyone()
                t_z = cols_to_rows(lambda k: u[:, 16 + k, :], done_u)
                for o in range(2):
                    got_b = side_load(f"bias{o}", [(bias, a["hy_filt_bias_2"][0][o:o + 1, :])], *everyone())
                    for hv in range(2):
                        dcol = slice(hv * BANK, (hv + 1) * BANK)
                        free = everyone()
                        for side, dst in ((0, hf), (1, hb)):
                            c0 = (o * 2 + side) * D + hv * BANK
                            b_s = next_bank()
                            for i in range(TT):
                                b = next_bank()
                                if b is b_s:
                                    b = next_bank()
                                m = mms(b.t[:, :], [(hidden[0:64, i * P:(i + 1) * P], s_w4.t[0:64, c0:c0 + BANK])],
                                        got_w4, *free, *b.free)
                                b.free = [v_tt(dst[:, i, :], b.t[:, :], decay[:, i, dcol], ALU.mult, m, got_four, *free)]
                                t = a_fn(ab[:, i, :], dst[:, i, :], ACT.Abs, b.free[0], tensor.last())
                            m = mms(b_s.t[:, :], [(ones[:, :], ab[:, i, :]) for i in range(TT)], t, *b_s.free)
                            t = v_ts(norm_r, b_s.t[:, :], EPS, None, ALU.add, None, m)
                            b_s.free = [t]
                            v_recip(norm_r, norm_r)
                            for i in range(TT):
                                v_tt(dst[:, i, :], dst[:, i, :], norm_r, ALU.mult)
                        v_tt(hf[0:1, 0, :], hf[0:1, 0, :], bias[:, dcol], ALU.add, got_b)
                        dve(lambda: nc.vector.memset(hb[0:1, 0, :], 0.0))
                        t = v_tt(ab, hf, hb, ALU.add)
                        t = v_tt(hf, hf, hb, ALU.subtract)
                        for ft in range(TT):
                            for part_, (dst, filt) in enumerate(((kr, ab), (ki, hf))):
                                b = next_bank()
                                m = mms(b.t[:, :], [(ahead[:, i, part_ * TOKENS + ft * P:part_ * TOKENS + (ft + 1) * P],
                                                     filt[:, i, :]) for i in range(TT)], t, *b.free)
                                b.free = [v_copy(dst[:, ft, dcol], b.t[:, :], m)]
                        v_copy(kn[:, 0, dcol], kr[:, 0, dcol])
                        b = next_bank()
                        m = mms(b.t[0:1, :], [(ahead[:, i, TOKENS:TOKENS + 1], ab[:, i, :]) for i in range(TT)], t, *b.free)
                        b.free = [v_copy(kn[0:1, 0, dcol], b.t[0:1, :], m)]
                        dve(lambda d=dcol: nc.vector.memset(ki[0:1, 0, d], 0.0))
                    if o == 0:
                        tap("kr", kr, vector.last())
                    for hv in range(2):
                        dcol = slice(hv * BANK, (hv + 1) * BANK)
                        free = everyone()
                        for f4 in range(4):
                            b = next_bank()
                            m = mms(b.t[:, :], [(ahead[:, i, f4 * P:(f4 + 1) * P], z_rows[:, i, dcol]) for i in range(TT)],
                                    *t_z, *free, *b.free)
                            b.free = [a_fn(spec[:, f4, :], b.t[:, :], ACT.Copy, m, *free, chain=False)]
                        vector.wait(b.free[0])
                        for ft in range(TT):
                            ur, ui = spec[:, ft, :], spec[:, 2 + ft, :]
                            kni = kn[:, 0, dcol] if ft == 0 else kr[:, 1, dcol]
                            v_tt(prod[:, ft, :], ur, kr[:, ft, dcol], ALU.mult)
                            v_tt(norm_r, ui, ki[:, ft, dcol], ALU.mult)
                            v_tt(prod[:, ft, :], prod[:, ft, :], norm_r, ALU.subtract)
                            v_tt(prod[:, 2 + ft, :], ur, ki[:, ft, dcol], ALU.mult)
                            v_tt(norm_r, ui, kni, ALU.mult)
                            t = v_tt(prod[:, 2 + ft, :], prod[:, 2 + ft, :], norm_r, ALU.add)
                        for dt in range(4):
                            k = hv * 4 + dt
                            b = next_bank()
                            m = mms(b.t[:, 0:TOKENS], [(prod[:, f4, dt * P:(dt + 1) * P], back[:, f4, :]) for f4 in range(4)],
                                    t, *b.free)
                            gate_u = u[:, o * 8 + k, :]
                            b.free = [v_tt(gate_u, b.t[:, 0:TOKENS], gate_u, ALU.mult, m)]
                    if o == 0:
                        t_z = cols_to_rows(lambda k: u[:, k, :], everyone())
                s_four.free = everyone()
                s_w4.free = everyone()
                product_rows(u[:, 8:16, :], KD, a["hy_w_out_2"][0], by_k, D, residual(mod[:, 2, :]), *everyone())

            done = everyone()
            tap(f"xmix{layer}", x[:, :, :], *done)
            if layer == 1:
                pass
            t = norm_modulate(x, norm_w[:, 1, :], mod[:, 4, :], mod[:, 3, :], *done)
            t = into_h_cols(t, *done)
            experts(name, 4, 4, 256, a["moe_w_gate_2"][layer], a["moe_w_up_2"][layer], a["moe_w_down_2"][layer],
                    a["moe_wg_2"][layer], a["moe_we_2"][layer], a["moe_bg_2"][layer], a["moe_be_2"][layer],
                    *t, *everyone())
            done = everyone()
            tap(f"xout{layer}", x[:, :, :], *done)

        stored = sem("stored")
        sync.dma(out[0].rearrange("(i p) d -> p i d", p=P), x[:, :, :], stored, *done)
        sync.wait((stored, 16))

        block = ctx.enter_context(nc.Block())

        @block.sync
        def _(e):
            sync.run(e)

        @block.tensor
        def _(e):
            tensor.run(e)

        @block.vector
        def _(e):
            vector.run(e)

        @block.scalar
        def _(e):
            scalar.run(e)

        @block.gpsimd
        def _(e):
            pool.run(e)


def lay_out(inputs):
    arrays = {k: np.ascontiguousarray(v) for k, v in inputs.items()}
    arrays["w_s_t"] = np.ascontiguousarray(arrays.pop("w_s")[0].transpose(2, 0, 1))
    arrays["b_s_t"] = np.ascontiguousarray(arrays.pop("b_s")[0].T)
    arrays["positions_2_cols"] = np.ascontiguousarray(arrays.pop("positions_2")[0].astype(np.int32).reshape(TT, P).T)
    cols = [arrays.pop("hy_b_in_2")[0], *arrays.pop("hy_conv_w_2")[0], arrays.pop("hy_conv_b_2")[0]]
    arrays["hy_cols"] = np.ascontiguousarray(
        np.stack([c.reshape(24, P) for c in cols]).transpose(2, 0, 1).reshape(P, 120))
    arrays["hy_f_cols"] = np.ascontiguousarray(np.stack(
        [arrays.pop(f"hy_f_{w}{l}_2")[0] for l in (1, 2, 3) for w in ("b", "freq")], axis=1))
    arrays.update(shape_constants())
    return arrays


def kernel(**inputs):
    import concourse.bacc as bacc
    from concourse.bass_utils import run_bass_kernel_spmd

    arrays = lay_out(inputs)
    nc = bacc.Bacc("TRN2", target_bir_lowering=False, num_devices=1)
    handles = {k: nc.dram_tensor(f"in_{k}", v.shape, mybir.dt.from_np(v.dtype), kind="ExternalInput").ap()
               for k, v in arrays.items()}
    out = nc.dram_tensor("out", (1, TOKENS, D), F32, kind="ExternalOutput").ap()
    build(nc, handles, out)
    result = run_bass_kernel_spmd(nc, [{f"in_{k}": v for k, v in arrays.items()}], core_ids=[0])
    return result.results[0]["out"]
```

```python
from contextlib import ExitStack

import numpy as np

import concourse.bass as bass
import concourse.mybir as mybir

F32 = mybir.dt.float32
I32 = mybir.dt.int32
U32 = mybir.dt.uint32
ACT = mybir.ActivationFunctionType
ALU = mybir.AluOpType
AX = mybir.AxisListType.X

P = 128
TOKENS = 256
TT = TOKENS // P
D = 1024
KD = D // P
EPS = 1e-6
BANK = 512

A_HEADS, HD = 4, 64
B_HEADS, B_KV = 8, 2
C_HEADS = 4
CW = C_HEADS * HD
OFF_B, OFF_KV, OFF_C, OFF_G, IN_W = 512, 1024, 1280, 2304, 2560
CTX_W = OFF_G - OFF_KV
GRID_W = 64

MLA_HEADS, Q_LORA, KV_LORA, NOPE, ROPE, VH = 8, 256, 128, 128, 64, 128
HALF = ROPE // 2
LEVELS = 7
BIG = 1e30
SLOT = 4096
SLOTS = 5
WORK = 15872
SPARE = 4096


PLACES = 64

TWO_PI_1 = 6.28125
TWO_PI_2 = float(np.float32(2 * np.pi - 6.28125))
TWO_PI_3 = float(2 * np.pi - 6.28125 - np.float64(np.float32(2 * np.pi - 6.28125)))
ROUND = 1.5 * 2.0 ** 23
PI_IN = 3.1415925


def shape_constants():
    t = np.arange(P)
    fwd, bwd, mask_f, mask_b = [], [], [], []
    r = t[:, None]
    for j in range(LEVELS):
        size = 2 << j
        mid = t // size * size + size // 2
        right = (t >> j & 1) == 1
        fwd.append(np.where(right, (r >= mid) & (r <= t), (r > t) & (r < mid)))
        bwd.append(np.where(right, (r >= mid) & (r < t), (r >= t) & (r < mid)))
        same = (r // size) == (t // size)
        rright = (r >> j & 1) == 1
        mask_f.append(same & ~rright & right)
        mask_b.append(same & rright & ~right)
    fwd.append(r <= t)
    bwd.append(r >= t)
    after_f, after_b = r > t, r < t
    scan = np.concatenate(fwd + bwd + [after_f, after_b] + mask_f + mask_b, axis=1)
    scan = scan.astype(np.float32)

    row = np.repeat(np.arange(TOKENS // GRID_W), GRID_W).astype(np.float32)
    col = np.tile(np.arange(GRID_W), TOKENS // GRID_W).astype(np.float32)
    inv = (1.0 / (np.float32(10000.0) ** (np.arange(0, 32, 2, dtype=np.float32) / np.float32(32)))).astype(np.float32)
    ang = np.stack([row[:, None] * inv, col[:, None] * inv], axis=1)
    cos = np.repeat(np.cos(ang)[:, :, None, :], 2, axis=2).reshape(TOKENS, HD)
    sin = np.stack([-np.sin(ang), np.sin(ang)], axis=2).reshape(TOKENS, HD)
    axial = np.concatenate([cos, sin], axis=1).astype(np.float32)
    axial = axial.reshape(TT, P, 2 * HD).transpose(1, 0, 2).reshape(P, -1)

    inv2 = (1.0 / (np.float32(10000.0) ** (np.arange(0, ROPE, 2, dtype=np.float32) / np.float32(ROPE)))).astype(np.float32)
    freq = np.tile(inv2[None, :], (P, 1)).astype(np.float32)

    L = TOKENS
    f, s = np.arange(L)[None, :], np.arange(L)[:, None]
    w = 2 * np.pi * ((f * s) % (2 * L)) / (2 * L)
    alt = np.where(np.arange(L) % 2 == 0, 1.0, -1.0)
    real, imag = np.cos(w), -np.sin(w)
    imag[:, 0] = alt
    ahead = np.concatenate([real, imag], axis=1)
    back_r = 2 * np.cos(w).T / (2 * L)
    back_r[0] /= 2
    back_i = -2 * np.sin(w).T / (2 * L)
    back_i[0] = alt / (2 * L)
    back = np.concatenate([back_r, back_i], axis=0)
    tl = np.linspace(0.0, 1.0, L, dtype=np.float32)[:, None]
    deltas = np.abs(np.linspace(np.log(0.3) / 1e-2, np.log(1.5) / 1e-2, D, dtype=np.float32))
    decay = np.exp(-tl * deltas)
    fold = lambda a, n: a.reshape(n, P, -1).transpose(1, 0, 2).reshape(P, -1)
    fourier = np.concatenate([fold(ahead, 2), fold(back, 4), fold(decay, 2)], axis=1).astype(np.float32)

    bands = 16
    wl = (2.0 * np.pi * np.arange(L, dtype=np.float32)[:, None] / L).astype(np.float32)
    fr = np.linspace(1e-4, bands - 1, bands, dtype=np.float32)[None, :]
    feats = np.concatenate([tl, np.cos(fr * wl), -np.sin(fr * wl)], axis=-1).astype(np.float32)
    return {
        "k_scan": scan, "k_axial": axial, "k_freq": freq, "k_fourier": fourier,
        "k_before": np.concatenate([(r < t), np.tile(np.arange(PLACES), (P, 1))], axis=1).astype(np.float32),
        "k_feats": np.ascontiguousarray(feats.T), "k_ident": np.eye(P, dtype=np.float32),
    }


class Lane:

    def __init__(self, sem):
        self.sem, self.count, self.steps, self.seen = sem, 0, [], {}

    def wait(self, *tokens):
        for tok in tokens:
            if tok is None:
                continue
            if isinstance(tok, list):
                self.wait(*tok)
                continue
            sem, value = tok
            if self.seen.get(id(sem), 0) < value:
                self.seen[id(sem)] = value
                self.steps.append(lambda e, s=sem, v=value: e.wait_ge(s, v))

    def last(self):
        return (self.sem, self.count) if self.count else None

    def put(self, make, *after, signal=True):
        self.wait(*after)
        if not signal:
            self.steps.append(lambda e: make())
            return None
        self.count += 1
        self.steps.append(lambda e, s=self.sem: make().then_inc(s, 1))
        return self.sem, self.count

    def dma(self, out, in_, sem, *after):
        self.wait(*after)
        self.steps.append(lambda e: e.dma_start(out, in_).then_inc(sem, 16))

    def run(self, engine):
        for step in self.steps:
            step(engine)

    def enter(self, sem):
        self.outside = self.sem, self.count, self.steps, self.seen
        self.sem, self.count, self.steps, self.seen = sem, 0, [], dict(self.seen)

    def leave(self, flag, written):
        inside = self.steps
        self.sem, self.count, self.steps, self.seen = self.outside
        self.wait(written)

        def branch(e):
            with e.If(e.value_load(flag) > 0):
                for step in inside:
                    step(e)
        self.steps.append(branch)


class Bank:

    def __init__(self, tensor):
        self.t, self.free = tensor, []


class Slot:
    def __init__(self, tensor, sem):
        self.t, self.sem, self.count, self.free, self.held = tensor, sem, 0, [], False


def build(nc, a, out, taps=None):
    ctx = ExitStack()
    with ctx:
        def sb(name, shape, dt=F32):
            return ctx.enter_context(nc.sbuf_tensor(name, shape, dt))

        def sem(name):
            return ctx.enter_context(nc.semaphore(name))

        slots = [Slot(sb(f"weights{i}", [P, SLOT]), sem(f"weights{i}_in")) for i in range(SLOTS)]
        x = sb("x", [P, TT, D])
        mod = sb("mod", [P, 3, D])
        h_rows = sb("h_rows", [P, TT, D])
        h_cols = sb("h_cols", [P, KD, TOKENS])
        norm_w = sb("norm_w", [P, 2, D])
        work = sb("work", [P, WORK])
        spare = sb("spare", [P, SPARE])
        c_rep = sb("c_rep", [P, 2, KD, 32])
        ident = sb("ident", [P, P])
        ones = sb("ones", [P, P])
        before = sb("before", [P, P])
        places = sb("places", [P, PLACES])
        overflow = sb("overflow", [P, 8], I32)
        small = sb("small", [P, 384])
        banks = [Bank(ctx.enter_context(nc.psum_tensor(f"bank{i}", [P, BANK], F32))) for i in range(8)]

        tensor, vector, scalar, pool, sync = (Lane(sem(n)) for n in (
            "tensor_done", "vector_done", "scalar_done", "pool_done", "sync_done"))
        lanes = ((tensor, "tensor"), (vector, "vector"), (scalar, "scalar"), (pool, "pool"), (sync, "sync"))

        def dve(make, *after, chain=True):
            return vector.put(make, vector.last() if chain else None, *after)

        def act(make, *after, chain=True):
            return scalar.put(make, scalar.last() if chain else None, *after)

        def mms(out_ap, pairs, *after, start=True, stop=True, signal=True, loose=False):
            tensor.wait(*after)
            tok = None
            for i, (l, r) in enumerate(pairs):
                end = i == len(pairs) - 1
                tok = tensor.put(
                    lambda l=l, r=r, s=start and i == 0, e=stop and end: nc.tensor.matmul(
                        out_ap, l, r, start=s, stop=e, skip_group_check=loose),
                    signal=end and signal)
            return tok

        def turn(out_ap, in_ap, *after, signal=True):
            n = in_ap.shape[0]
            return tensor.put(lambda: nc.tensor.transpose(out_ap, in_ap, ident[0:n, 0:n]), *after, signal=signal)

        def a_fn(out_ap, in_ap, func, *after, chain=True, **kw):
            return act(lambda: nc.scalar.activation(out_ap, in_ap, func, **kw), *after, chain=chain)

        def v_copy(out_ap, in_ap, *after, chain=True):
            return dve(lambda: nc.vector.tensor_copy(out_ap, in_ap), *after, chain=chain)

        def v_tt(out_ap, p, q, op, *after, chain=True):
            return dve(lambda: nc.vector.tensor_tensor(out_ap, p, q, op), *after, chain=chain)

        def v_ts(out_ap, p, s1, s2, op0, op1, *after, chain=True):
            if s2 is None:
                return dve(lambda: nc.vector.tensor_scalar(out_ap, p, s1, None, op0), *after, chain=chain)
            return dve(lambda: nc.vector.tensor_scalar(out_ap, p, s1, s2, op0, op1), *after, chain=chain)

        def v_stt(out_ap, p, s, q, op0, op1, *after, chain=True):
            return dve(lambda: nc.vector.scalar_tensor_tensor(out=out_ap, in0=p, scalar=s, in1=q, op0=op0, op1=op1),
                       *after, chain=chain)

        def v_recip(out_ap, in_ap, *after):
            return dve(lambda: nc.vector.reciprocal(out_ap, in_ap), *after)

        def v_sum(out_ap, in_ap, *after):
            return dve(lambda: nc.vector.reduce_sum(out_ap, in_ap, AX), *after)

        def v_max(out_ap, in_ap, *after):
            return dve(lambda: nc.vector.reduce_max(out_ap, in_ap, AX), *after)

        bank_at = [0]

        def next_bank():
            b = banks[bank_at[0] % 7]
            bank_at[0] += 1
            return b

        slot_at = [0]

        def load(*pieces):
            while slots[slot_at[0] % SLOTS].held:
                slot_at[0] += 1
            s = slots[slot_at[0] % SLOTS]
            slot_at[0] += 1
            for view, src in pieces:
                s.count += 16
                sync.dma(view(s.t), src, s.sem, *s.free)
            s.free = []
            return s, (s.sem, s.count)

        def side_load(name, pieces, *after, lane=None):
            s = sem(name + "_in")
            for dst, src in pieces:
                (lane or pool).dma(dst, src, s, *after)
            return s, 16 * len(pieces)

        def cut(at, *dims):
            n = int(np.prod(dims))
            assert at + n <= WORK, (at, n)
            v = work[:, at:at + n]
            if len(dims) == 1:
                return v
            if len(dims) == 2:
                return v.rearrange("p (a b) -> p a b", a=dims[0])
            if len(dims) == 3:
                return v.rearrange("p (a b c) -> p a b c", a=dims[0], b=dims[1])
            return v.rearrange("p (a b c d) -> p a b c d", a=dims[0], b=dims[1], c=dims[2])

        def tap(name, ap, *toks):
            if taps is not None and name in taps:
                s = sem("tap_" + name)
                pool.dma(taps[name], ap, s, *toks)
                for l in (tensor, vector, scalar, pool, sync):
                    l.wait((s, 16))

        def everyone():
            return [l.last() for l in (tensor, vector, scalar, pool)]

        got_ident = side_load("ident", [(ident[:, :], a["k_ident"]), (before[:, :], a["k_before"][:, 0:P]),
                                        (places[:, :], a["k_before"][:, P:])], lane=scalar)
        vector.wait(got_ident)
        made_ones = vector.put(lambda: nc.vector.memset(ones[:, :], 1.0))
        tensor.wait(got_ident, made_ones)

        def rstd(dst, ssum, width, *after):
            t = v_ts(ssum, ssum, 1.0 / width, EPS, ALU.mult, ALU.add, *after)
            t = a_fn(ssum, ssum, ACT.Sqrt, t)
            return v_recip(dst, ssum, t)

        def head_norm(src, dst, groups, width, weight, sq, stat, *after):
            t = v_tt(sq, src, src, ALU.mult, *after)
            t = v_sum(stat, sq, t)
            t = rstd(stat, stat, width, t)
            t = v_tt(dst, src, stat.unsqueeze(2).to_broadcast([P, groups, width]), ALU.mult, t)
            if weight is not None:
                t = v_tt(dst, dst, weight, ALU.mult, t)
            return t

        def repeat_silu(c_in, cond, rep, name, *after):
            got = side_load(name, [(cond, c_in)], *after, lane=scalar)
            t = a_fn(cond, cond, ACT.Silu, got, *after)
            return v_copy(rep, cond.unsqueeze(2).to_broadcast([P, KD, 32]), t, *after)

        def modulation(rep, w, b_row, stored, groups, name, *after):
            wv = w.rearrange("(p k) n -> p k n", k=KD)
            four = 4 * BANK
            for g in groups:
                cols = slice(g * four, (g + 1) * four)
                bias, tmp = (spare[:, j * BANK:(j + 1) * BANK] for j in range(2))
                got_b = side_load(f"{name}_b{g}", [
                    (bias[32 * j:32 * j + 32, :], b_row[g * four + j * BANK:g * four + (j + 1) * BANK].partition_broadcast(32))
                    for j in range(4)], *after, *spare_free[0])
                b = mod_bank
                for k0 in range(0, KD, 2):
                    s, got = load((lambda v: v[:, :].rearrange("p (k n) -> p k n", k=2), wv[:, k0:k0 + 2, cols]))
                    ws = s.t[:, :].rearrange("p (k n) -> p k n", k=2)
                    for k in range(2):
                        for j in range(4):
                            m = mms(b.t[32 * j:32 * j + 32, :], [(rep[:, k0 + k, :], ws[:, k, j * BANK:(j + 1) * BANK])],
                                    got, *after, *b.free, start=k0 + k == 0, stop=k0 + k == KD - 1, loose=True,
                                    signal=k == 1 and j == 3)
                    s.free = [m]
                    if k0 < KD - 2:
                        yield
                t = v_tt(tmp, b.t[:, :], bias, ALU.add, m, got_b)
                b.free = [t]
                done = sem(f"{name}_stored{g}")
                pool.dma(stored[cols].rearrange("(j n) -> j n", j=4), tmp[0:P:32, :], done, t)
                spare_free[0] = [(done, 16)]
                mod_stored[name, g] = (done, 16)
                yield

        def filters(*after):
            W = D // 4
            at = lambda o, *d: spare[:, o:o + int(np.prod(d))].rearrange("p (a b) -> p a b", a=d[0]) if len(d) > 1 \
                else spare[:, o:o + d[0]]
            hidden, turns, f_small = at(0, TOKENS), at(256, TOKENS), at(512, 208)
            hf, hb, ab = at(720, TT, W), at(1232, TT, W), at(1744, TT, W)
            norm_r, imag, skip = at(2256, W), at(2512, TT, W), at(3024, W)
            got = side_load("filters", [
                (f_small[0:33, 0:64], a["hy_f_w1_2"][0]), (f_small[0:64, 64:128], a["hy_f_w2_2"][0]),
                (f_small[0:64, 128:192], a["hy_f_w3_2"][0]), (f_small[0:64, 192:198], a["hy_f_cols"]),
                (turns[0:33, :], a["k_feats"])], *after, *spare_free[0])
            b = mod_bank
            yield
            layers = ((f_small[0:33, 0:64], turns[0:33, :]), (f_small[0:64, 64:128], hidden[0:64, :]),
                      (f_small[0:64, 128:192], hidden[0:64, :]))
            t = None
            for l, (w_l, src) in enumerate(layers):
                m = mms(b.t[0:64, 0:TOKENS], [(w_l, src)], got, t, *b.free)
                hd, rd = hidden[0:64, :], turns[0:64, :]
                t = v_ts(hd, b.t[0:64, 0:TOKENS], f_small[0:64, 192 + 2 * l:193 + 2 * l],
                         f_small[0:64, 193 + 2 * l:194 + 2 * l], ALU.add, ALU.mult, m, *after)
                b.free = [t]
                v_ts(rd, hd, float(1 / (2 * np.pi)), ROUND, ALU.mult, ALU.add)
                v_ts(rd, rd, -ROUND, None, ALU.add, None)
                v_stt(hd, rd, -TWO_PI_1, hd, ALU.mult, ALU.add)
                v_stt(hd, rd, -TWO_PI_2, hd, ALU.mult, ALU.add)
                v_stt(hd, rd, -TWO_PI_3, hd, ALU.mult, ALU.add)
                t = v_ts(hd, hd, PI_IN, -PI_IN, ALU.min, ALU.max)
                t = a_fn(hd, hd, ACT.Sin, t)
                yield
            t_hidden = t
            s_four, got_four = load((lambda v: v[:, :], a["k_fourier"]))
            s_w4, got_w4 = load((lambda v: v[0:64, :], a["hy_f_w4_2"][0]))
            s_four.held = s_w4.held = True
            ahead = s_four.t[:, 0:1024].rearrange("p (k f) -> p k f", k=TT)
            decay = s_four.t[:, 2048:4096].rearrange("p (k d) -> p k d", k=TT)
            hb_stored = imag_stored = nyquist_stored = m = None
            for o in range(2):
                for q in range(4):
                    cols = slice(q * W, (q + 1) * W)
                    got_skip = side_load(f"skip{o}{q}", [(skip[0:1, :], a["hy_filt_bias_2"][0][o:o + 1, cols])],
                                         vector.last(), *after)
                    for side, dst in ((0, hf), (1, hb)):
                        c0 = (o * 2 + side) * D + q * W
                        for i in range(TT):
                            m = mms(b.t[:, i * W:(i + 1) * W],
                                    [(hidden[0:64, i * P:(i + 1) * P], s_w4.t[0:64, c0:c0 + W])],
                                    got_w4, t_hidden, *b.free)
                        t = v_tt(dst, b.t[:, :].rearrange("p (i c) -> p i c", i=TT), decay[:, :, cols], ALU.mult,
                                 m, got_four, hb_stored, tensor.last())
                        b.free = [t]
                        t = a_fn(ab, dst, ACT.Abs, t, tensor.last())
                        yield
                        m = mms(b.t[:, 0:W], [(ones[:, :], ab[:, i, :]) for i in range(TT)], t, *b.free)
                        t = v_ts(norm_r, b.t[:, 0:W], EPS, None, ALU.add, None, m, nyquist_stored)
                        b.free = [t]
                        v_recip(norm_r, norm_r)
                        t = v_tt(dst, dst, norm_r.unsqueeze(1).to_broadcast([P, TT, W]), ALU.mult)
                        yield
                    v_tt(hf[0:1, 0, :], hf[0:1, 0, :], skip[0:1, :], ALU.add, got_skip)
                    dve(lambda: nc.vector.memset(hb[0:1, 0, :], 0.0))
                    v_tt(ab, hf, hb, ALU.add, tensor.last())
                    t = v_tt(hf, hf, hb, ALU.subtract)
                    real = hb
                    for ft in range(TT):
                        m = mms(b.t[:, ft * W:(ft + 1) * W],
                                [(ahead[:, i, ft * P:(ft + 1) * P], ab[:, i, :]) for i in range(TT)], t, *b.free)
                    t = v_copy(real, b.t[:, :].rearrange("p (i c) -> p i c", i=TT), m)
                    b.free = [t]
                    done = sem(f"real{o}{q}")
                    pool.dma(spectra["real"][o][:, :, cols], real, done, t)
                    hb_stored = (done, 16)
                    yield
                    for ft in range(TT):
                        m = mms(b.t[:, ft * W:(ft + 1) * W],
                                [(ahead[:, i, TOKENS + ft * P:TOKENS + (ft + 1) * P], hf[:, i, :]) for i in range(TT)],
                                t, *b.free)
                    v_copy(imag, b.t[:, :].rearrange("p (i c) -> p i c", i=TT), m, imag_stored)
                    t = dve(lambda: nc.vector.memset(imag[0:1, 0, :], 0.0))
                    b.free = [t]
                    done_i = sem(f"imag{o}{q}")
                    pool.dma(spectra["imag"][o][:, :, cols], imag, done_i, t)
                    imag_stored = (done_i, 16)
                    m = mms(b.t[0:1, 0:W], [(ahead[:, i, TOKENS:TOKENS + 1], ab[:, i, :]) for i in range(TT)], t, *b.free)
                    t = v_copy(norm_r[0:1, :], b.t[0:1, 0:W], m)
                    b.free = [t]
                    done_n = sem(f"nyquist{o}{q}")
                    pool.dma(spectra["nyquist"][o][:, cols], norm_r[0:1, :], done_n, t)
                    nyquist_stored = (done_n, 16)
                    spectrum_stored[o, q] = [hb_stored, imag_stored, nyquist_stored]
                    if o == 1 and q == 3:
                        spare_free[0] = spectrum_stored[o, q]
                        s_four.free, s_w4.free = [tensor.last(), vector.last()], [tensor.last()]
                        s_four.held = s_w4.held = False
                    yield

        spectra = {n: nc.dram_tensor("filter_" + n, shape, F32, kind="Internal").ap() for n, shape in (
            ("real", (2, P, TT, D)), ("imag", (2, P, TT, D)), ("nyquist", (2, 1, D)))}
        spectrum_stored = {}

        def mod_load(name, stored, part, at, *after):
            return side_load(f"{name}_part{part}", [(mod[:, at, :], stored[part * D:(part + 1) * D].partition_broadcast(P))],
                             mod_stored[name, part // 2], *after)

        ws_t = spare[:, 1024:1536].rearrange("p (h t) -> p h t", h=A_HEADS)
        bs_cols = spare[:, 1536:1540]
        axial = spare[:, 1540:1796].rearrange("p (i c d) -> p i c d", i=TT, c=2)
        qk_w = spare[:, 1796:2436].rearrange("p (h d) -> p h d", h=10)
        w_c = spare[:, 2436:2692].rearrange("p (h d) -> p h d", h=C_HEADS)
        lb_logits = spare[:, 2692:3204].rearrange("p (a b) -> p a b", a=2)
        latent = spare[:, 3292:4096]

        mod_stored, spare_free, mod_bank = {}, [[]], banks[7]
        background = []

        def step():
            while background:
                try:
                    next(background[0])
                    return
                except StopIteration:
                    background.pop(0)

        def finish():
            while background:
                step()

        def norm_modulate(src, weight, scale, shift, *after, fold=True):
            t = None
            if fold:
                t = v_stt(scale, scale, 1.0, weight, ALU.add, ALU.mult, *after)
            ss = small[:, 0:TT]
            q = [a_fn(h_rows[:, i, :], src[:, i, :], ACT.Square, *after, accum_out=ss[:, i:i + 1]) for i in range(TT)]
            t = rstd(small[:, 4:4 + TT], ss, D, *q, t)
            for i in range(TT):
                t = v_stt(h_rows[:, i, :], src[:, i, :], small[:, 4 + i:5 + i], scale, ALU.mult, ALU.mult, t)
                t = v_tt(h_rows[:, i, :], h_rows[:, i, :], shift, ALU.add, t)
            return t

        def rows_to_cols(piece, dst, n, *after):
            toks = []
            for k0 in range(0, n, 2):
                b = next_bank()
                bv = b.t[:, :].rearrange("p (k t) -> p k t", k=2)
                m = None
                for k in range(k0, min(k0 + 2, n)):
                    for i in range(TT):
                        m = turn(bv[:, k - k0, i * P:(i + 1) * P], piece(i, k), *after, *b.free)
                kk = min(2, n - k0)
                if (k0 // 2) % 2:
                    b.free = [v_copy(dst[:, k0:k0 + kk, :], bv[:, 0:kk, :], m, *after, chain=False)]
                else:
                    b.free = [a_fn(dst[:, k0:k0 + kk, :], bv[:, 0:kk, :], ACT.Copy, m, *after, chain=False)]
                toks += b.free
            return toks

        def strided(i, k):
            return h_rows[:, i, :].rearrange("p (f k) -> p k f", k=KD)[:, k, :]

        def product_rows(cols, n_k, weight, w_view, width, put, *after):
            for c0 in range(0, width, BANK):
                n = min(BANK, width - c0)
                s, got = load((lambda v, n=n: v[:, 0:n_k * n].rearrange("p (k n) -> p k n", k=n_k),
                               w_view(weight)[:, :, c0:c0 + n]))
                ws = s.t[:, 0:n_k * n].rearrange("p (k n) -> p k n", k=n_k)
                for i in range(TT):
                    b = next_bank()
                    m = mms(b.t[:, 0:n], [(cols[:, k, i * P:(i + 1) * P], ws[:, k, :]) for k in range(n_k)],
                            got, *after, *b.free)
                    b.free = [put(i, c0, n, b, m)]
                s.free = [m]
                step()
            return [b.free[0], m]

        by_p = lambda w: w.rearrange("(p k) n -> p k n", k=KD)
        by_k = lambda w: w.rearrange("(k p) n -> p k n", p=P)

        def residual(gate):
            def put(i, c0, n, b, m):
                tmp = h_rows[:, i, c0:c0 + n]
                t = v_tt(tmp, b.t[:, 0:n], gate[:, c0:c0 + n], ALU.mult, m)
                free = t
                v_tt(x[:, i, c0:c0 + n], x[:, i, c0:c0 + n], tmp, ALU.add, t)
                return free
            return put

        router = []

        def route_load(name, w, bias, *after):
            n = w.shape[1]
            place = norm_w[:, 0, :]
            wv, bv = place[:, 0:KD * n].rearrange("p (k n) -> p k n", k=KD), place[:, KD * 36:KD * 36 + n]
            got = side_load(name + "_route", [(wv, by_p(w)), (bv, bias.partition_broadcast(P))], *after)
            router.append((wv, bv, got))

        def route(logits, n_grp, per, comb, chosen, at, *after):
            n_exp = n_grp * per
            g, e = logits[:, :, 0:n_grp], logits[:, :, n_grp:n_grp + n_exp]
            s = lambda o, n: small[:, at + o:at + o + n]
            gmax, ex, gsum, picked = s(0, TT), s(8, TT * n_grp), s(16, TT), s(24, TT * n_grp)
            masked, hot1, hot2, top = s(40, TT * n_exp), s(104, TT * n_exp), s(168, TT * n_exp), s(232, 16)
            cnt = s(250, TT * n_exp)
            v3 = lambda ap, n: ap.rearrange("p (i n) -> p i n", i=TT)
            bc = lambda ap, n: ap.unsqueeze(2).to_broadcast([P, TT, n])

            def first_of(hot, values, best, n, t):
                t = v_tt(v3(hot, n), values, bc(best, n), ALU.is_equal, t)
                for i in range(TT):
                    h, c = v3(hot, n)[:, i, :], v3(cnt[:, 0:TT * n], n)[:, i, :]
                    t = dve(lambda h=h, c=c: nc.vector.tensor_tensor_scan(c, h, h, 0.0, ALU.add, ALU.bypass), t)
                c = cnt[:, 0:TT * n]
                return v_stt(hot, c, 1.0, hot, ALU.is_equal, ALU.mult, t)

            t = v_max(gmax, g, *after)
            t = v_tt(v3(ex, n_grp), g, bc(gmax, n_grp), ALU.subtract, t)
            t = a_fn(ex, ex, ACT.Exp, t)
            t = v_sum(gsum, v3(ex, n_grp), t)
            t = v_recip(gsum, gsum, t)
            t = first_of(picked, g, gmax, n_grp, t)
            t = v_ts(picked, picked, BIG, -BIG, ALU.mult, ALU.add, t)
            for i in range(TT):
                ei = e[:, i, :].rearrange("p (a b) -> p a b", a=n_grp)
                mi = v3(masked, n_exp)[:, i, :].rearrange("p (a b) -> p a b", a=n_grp)
                pi = v3(picked, n_grp)[:, i, :].unsqueeze(2).to_broadcast([P, n_grp, per])
                t = v_tt(mi, ei, pi, ALU.add, t)
            m1, m2, w1, w2 = top[:, 0:2], top[:, 2:4], top[:, 4:6], top[:, 6:8]
            t = v_max(m1, v3(masked, n_exp), t)
            t = first_of(hot1, v3(masked, n_exp), m1, n_exp, t)
            t = v_stt(masked, hot1, -2 * BIG, masked, ALU.mult, ALU.add, t)
            t = v_max(m2, v3(masked, n_exp), t)
            t = first_of(hot2, v3(masked, n_exp), m2, n_exp, t)
            t = v_tt(w2, m2, m1, ALU.subtract, t)
            t = a_fn(w2, w2, ACT.Exp, t)
            t = v_ts(w1, w2, 1.0, None, ALU.add, None, t)
            t = v_recip(w1, w1, t)
            t = v_tt(chosen.rearrange("p i n -> p (i n)"), hot1, hot2, ALU.add, t)
            t = v_tt(w1, w1, gsum, ALU.mult, t)
            t = v_tt(w2, w2, w1, ALU.mult, t)
            for i in range(TT):
                c = comb[:, i, 0:n_exp]
                t = v_ts(c, v3(hot1, n_exp)[:, i, :], w1[:, i:i + 1], None, ALU.mult, None, t)
                t = v_stt(c, v3(hot2, n_exp)[:, i, :], w2[:, i:i + 1], c, ALU.mult, ALU.add, t)
            return t

        def experts(layer, n_grp, per, ff, gate_w, up_w, down_w, *after):
            n_exp, n_ft = n_grp * per, ff // P
            logits, comb = cut(440, TT, n_grp + n_exp), cut(520, TT, n_exp)
            chosen, place, beyond = cut(600, TT, n_exp), cut(680, TT, n_exp), cut(760, TT, n_exp)
            route_w, route_b, got = router.pop()
            b = next_bank()
            for i in range(TT):
                m = mms(b.t[:, i * 64:i * 64 + n_grp + n_exp],
                        [(h_cols[:, k, i * P:(i + 1) * P], route_w[:, k, :]) for k in range(KD)],
                        got, *after, *b.free)
            bv = b.t[:, 0:TT * 64].rearrange("p (i n) -> p i n", i=TT)[:, :, 0:n_grp + n_exp]
            t = v_tt(logits, bv, route_b.unsqueeze(1).to_broadcast([P, TT, n_grp + n_exp]), ALU.add, m)
            b.free = [t]
            t = route(logits, n_grp, per, comb, chosen, 32, t)
            tap(layer + "_comb", comb, t)

            b = next_bank()
            for i in range(TT):
                pairs = [(before[:, :], chosen[:, i, :])] + ([(ones[:, :], chosen[:, 0, :])] if i else [])
                m = mms(b.t[:, i * n_exp:(i + 1) * n_exp], pairs, t, *b.free)
            bv = b.t[:, 0:TT * n_exp].rearrange("p (i n) -> p i n", i=TT)
            t = v_stt(place, chosen, -1000.0, bv, ALU.mult, ALU.add, m)
            b.free = [t]
            t = v_ts(place, place, 1000.0, None, ALU.add, None)
            t = v_ts(beyond, place, float(PLACES), None, ALU.is_ge, None)
            t = v_tt(beyond, beyond, chosen, ALU.mult)
            n_over = small[:, 0:1]
            t = v_sum(n_over, beyond.rearrange("p i n -> p (i n)"), t)
            b = next_bank()
            m = mms(b.t[:, 0:1], [(ones[:, :], n_over)], t, *b.free)
            t_flag = v_copy(overflow[:, 0:1], b.t[:, 0:1], m)
            b.free = [t_flag]
            t_route = v_tt(beyond, beyond, comb, ALU.mult)

            hot = [cut(1000 + 512 * j, TT, 4, PLACES) for j in range(2)]
            hot_w = [cut(2024 + 512 * j, TT, 4, PLACES) for j in range(2)]
            picked = [cut(3048 + 2048 * j, KD, 4 * PLACES) for j in range(2)]
            scatter = [cut(7144 + 256 * j, TT, P) for j in range(2)]
            gated = [cut(7656 + 512 * j, ff) for j in range(2)]
            act_cols = [cut(8680 + 512 * j, n_ft, P) for j in range(2)]
            y_rows = [cut(9704 + D * j, D) for j in range(2)]
            hot_free, picked_free, scatter_free = [None] * 2, [[]] * 2, [None] * 2
            act_free, y_free = [None] * 2, [None] * 2
            tokens = {}

            def choose(q):
                j, es = q % 2, slice(4 * q, 4 * q + 4)
                shape = [P, 4, PLACES]
                for i in range(TT):
                    t = v_tt(hot[j][:, i], place[:, i, es].unsqueeze(2).to_broadcast(shape),
                             places[:, :].unsqueeze(1).to_broadcast(shape), ALU.is_equal,
                             t_route, hot_free[j], chain=False)
                for i in range(TT):
                    tw = v_tt(hot_w[j][:, i], hot[j][:, i], comb[:, i, es].unsqueeze(2).to_broadcast(shape),
                              ALU.mult, t, chain=False)
                toks = []
                for k0 in range(0, KD, 2):
                    b = next_bank()
                    for k in range(2):
                        m = mms(b.t[:, k * 256:(k + 1) * 256],
                                [(strided(i, k0 + k), hot[j][:, i].rearrange("p e s -> p (e s)")) for i in range(TT)],
                                t, *b.free)
                    dst = picked[j][:, k0:k0 + 2, :]
                    src = b.t[:, :].rearrange("p (k s) -> p k s", k=2)
                    if k0 % 4:
                        b.free = [v_copy(dst, src, m, *picked_free[j], chain=False)]
                    else:
                        b.free = [a_fn(dst, src, ACT.Copy, m, *picked_free[j], chain=False)]
                    toks += b.free
                tokens[q] = toks, tw

            def take_pair(pr):
                q, j, e0 = pr // 2, pr % 2, 2 * pr
                toks, tw = tokens[q]
                off = (pr % 2) * 2
                halves = [slice(0, 64), slice(64, 128)]
                cols = [picked[q % 2][:, :, (off + c) * PLACES:(off + c + 1) * PLACES] for c in range(2)]
                if n_ft == 4:
                    g_slots = [load((lambda v: v[:, :], gate_w[e0 + c].rearrange("(p k) f -> p (k f)", k=KD)))
                               for c in range(2)]
                    u_slots = [load((lambda v: v[:, :], up_w[e0 + c].rearrange("(p k) f -> p (k f)", k=KD)))
                               for c in range(2)]
                    parts = [(g_slots, ff), (u_slots, ff)]
                else:
                    both = lambda v: v[:, :].rearrange("p (k s f) -> p k s f", k=KD, s=2)
                    parts = [([load((lambda v: both(v)[:, :, 0, :], by_p(gate_w[e0 + c])),
                                    (lambda v: both(v)[:, :, 1, :], by_p(up_w[e0 + c]))) for c in range(2)], 2 * ff)]
                results = []
                for slots_, width in parts:
                    b = next_bank()
                    for k in range(KD):
                        for c, (s, got_s) in enumerate(slots_):
                            w = s.t[:, :].rearrange("p (k f) -> p k f", k=KD)[:, k, :]
                            m = mms(b.t[halves[c], 0:width], [(cols[c][:, k, :], w)], got_s, *toks, *b.free,
                                    start=k == 0, stop=k == KD - 1, loose=True, signal=k == KD - 1 and c == 1)
                    for s, _ in slots_:
                        s.free = [m]
                    results.append((b, m))
                if n_ft == 4:
                    (bg_, mg), (bu, mu) = results
                    g_ps, u_ps = bg_.t[:, 0:ff], bu.t[:, 0:ff]
                else:
                    (bg_, mg), = results
                    bu, mu = bg_, mg
                    g_ps, u_ps = bg_.t[:, 0:ff], bg_.t[:, ff:2 * ff]
                down_slots = []
                if n_ft == 4:
                    down_slots = [load((lambda v: v[:, :].rearrange("p (k n) -> p k n", k=4), by_k(down_w[e0 + c])))
                                  for c in range(2)]
                    wd = [s.t[:, :].rearrange("p (k n) -> p k n", k=4) for s, _ in down_slots]
                else:
                    d = load(*[(lambda v, c=c: v[:, c * 2048:(c + 1) * 2048].rearrange("p (k n) -> p k n", k=2),
                                by_k(down_w[e0 + c])) for c in range(2)])
                    down_slots = [d, d]
                    wd = [d[0].t[:, c * 2048:(c + 1) * 2048].rearrange("p (k n) -> p k n", k=2) for c in range(2)]
                b = next_bank()
                for i in range(TT):
                    m = turn(b.t[:, i * P:(i + 1) * P],
                             hot_w[q % 2][:, i, off:off + 2, :].rearrange("p e s -> p (e s)"), tw, *b.free)
                if pr % 2:
                    hot_free[q % 2] = m
                ts = a_fn(scatter[j], b.t[:, 0:TOKENS].rearrange("p (i t) -> p i t", i=TT), ACT.Copy, m,
                          scatter_free[j], chain=False)
                b.free = [ts]
                g = gated[j]
                t1 = a_fn(g, g_ps, ACT.Silu, mg, act_free[j], chain=False)
                t2 = v_tt(g, u_ps, g, ALU.mult, t1, mu, chain=False)
                bg_.free = [t2]
                bu.free = [t2]
                b = next_bank()
                for ft in range(n_ft):
                    m = turn(b.t[:, ft * P:(ft + 1) * P], g[:, ft * P:(ft + 1) * P], t2, *b.free)
                act_free[j] = m
                ta = a_fn(act_cols[j], b.t[:, 0:ff].rearrange("p (k s) -> p k s", k=n_ft), ACT.Copy, m, chain=False)
                b.free = [ta]
                if pr % 2:
                    picked_free[q % 2] = [mu]
                for half in range(2):
                    b = next_bank()
                    hs = slice(half * BANK, (half + 1) * BANK)
                    for ft in range(n_ft):
                        for c in range(2):
                            m = mms(b.t[halves[c], :], [(act_cols[j][:, ft, halves[c]], wd[c][:, ft, hs])],
                                    ta, down_slots[c][1], *b.free, start=ft == 0, stop=ft == n_ft - 1, loose=True,
                                    signal=ft == n_ft - 1 and c == 1)
                    ty = v_tt(y_rows[j][:, hs], b.t[:, :], mod[:, 2, hs], ALU.mult, m, y_free[j], chain=False)
                    b.free = [ty]
                for s, _ in down_slots:
                    s.free = [m]
                for half in range(2):
                    hs = slice(half * BANK, (half + 1) * BANK)
                    for i in range(TT):
                        b = next_bank()
                        m = mms(b.t[:, :], [(scatter[j][:, i, :], y_rows[j][:, hs])], ts, ty, *b.free)
                        b.free = [v_tt(x[:, i, hs], x[:, i, hs], b.t[:, :], ALU.add, m, x_last.get((i, half)), chain=False)]
                        x_last[i, half] = b.free[0]
                y_free[j] = m
                scatter_free[j] = m

            x_last = {}
            for pr in range(n_exp // 2):
                if pr % 2 == 0:
                    choose(pr // 2)
                take_pair(pr)

            before_branch = everyone()
            kept = [(s, s.sem, s.count, s.free) for s in slots], [(b, b.free) for b in banks], slot_at[0], bank_at[0]
            for lane, n in lanes:
                lane.enter(sem(f"{layer}_rest_{n}"))
            for i, s in enumerate(slots):
                s.sem, s.count = sem(f"{layer}_rest_weights{i}"), 0
            for lane, _ in lanes:
                lane.wait(*before_branch)
            experts_for_all(n_exp, n_ft, gate_w, up_w, down_w, beyond)
            ends = everyone()
            for lane, _ in lanes:
                lane.wait(*ends)
            for lane, _ in lanes:
                lane.leave(overflow[0:1, 0:1], t_flag)
            for s, sem_, count, free in kept[0]:
                s.sem, s.count, s.free = sem_, count, free
            for b, free in kept[1]:
                b.free = free
            slot_at[0], bank_at[0] = kept[2], kept[3]
            return vector.last()

        def experts_for_all(n_exp, n_ft, gate_w, up_w, down_w, comb):
            t = None
            diag = [cut(1000 + 256 * j, TT, P) for j in range(2)]
            spread = [cut(1600 + 256 * j, TOKENS) for j in range(2)]
            gated = [cut(2200 + 256 * j, TOKENS) for j in range(3)]
            act_cols = [cut(3000 + 256 * j, TOKENS) for j in range(8)]
            diag_free, spread_free, gated_free, cols_free = [None] * 2, [None] * 2, [None] * 3, [None] * 8
            total, pair = banks[0:4], banks[4:7]
            spread_bank = banks[7]
            pending = []
            n = 0
            last = None

            def down(e, ft, s, got_down, tok, index, final):
                wd = s.t[:, (0 if n_ft == 4 else (e % 2) * 2048):][:, 0:n_ft * D].rearrange("p (k n) -> p k n", k=n_ft)
                col = act_cols[index % 8]
                m = None
                for i in range(TT):
                    for half in range(2):
                        tb = total[i * 2 + half]
                        first = e == 0 and ft == 0
                        m = mms(tb.t[:, :], [(col[:, i * P:(i + 1) * P], wd[:, ft, half * BANK:(half + 1) * BANK])],
                                tok, got_down, *(tb.free if first else []), start=first, stop=final,
                                signal=(i == TT - 1 and half == 1), loose=True)
                cols_free[index % 8] = m
                if ft == n_ft - 1 and (n_ft == 4 or e % 2 == 1):
                    s.free = [m]
                return m

            down_slot = None
            for e in range(n_exp):
                j = e % 2
                for i in range(TT):
                    dt = v_ts(diag[j][:, i, :], ident[:, :], comb[:, i, e:e + 1], None, ALU.mult, None,
                              diag_free[j], t if e == 0 else None, chain=(e == 0))
                for i in range(TT):
                    m = mms(spread_bank.t[:, i * P:(i + 1) * P], [(ones[:, :], diag[j][:, i, :])],
                            dt, *spread_bank.free)
                diag_free[j] = m
                sp = a_fn(spread[j], spread_bank.t[:, 0:TOKENS], ACT.Copy, m, spread_free[j], chain=False)
                spread_bank.free = [sp]
                if n_ft == 4:
                    s1, got1 = load((lambda v: v[:, :], gate_w[e].rearrange("(p k) f -> p (k f)", k=KD)))
                    s3, got3 = load((lambda v: v[:, :], up_w[e].rearrange("(p k) f -> p (k f)", k=KD)))
                    w1v = s1.t[:, :].rearrange("p (k f) -> p k f", k=KD)
                    w3v = s3.t[:, :].rearrange("p (k f) -> p k f", k=KD)
                    down_slot, got_down = load((lambda v: v[:, :].rearrange("p (k n) -> p k n", k=4), by_k(down_w[e])))
                else:
                    s1, got1 = load((lambda v: v[:, 0:2048], gate_w[e].rearrange("(p k) f -> p (k f)", k=KD)),
                                    (lambda v: v[:, 2048:4096], up_w[e].rearrange("(p k) f -> p (k f)", k=KD)))
                    s3, got3 = s1, got1
                    w1v = s1.t[:, 0:2048].rearrange("p (k f) -> p k f", k=KD)
                    w3v = s1.t[:, 2048:4096].rearrange("p (k f) -> p k f", k=KD)
                    if e % 2 == 0:
                        down_slot, got_down = load(*[
                            (lambda v, q=q: v[:, q * 2048:(q + 1) * 2048].rearrange("p (k n) -> p k n", k=2),
                             by_k(down_w[e + q])) for q in range(2)])
                for ft in range(n_ft):
                    b = pair[n % 3]
                    f = slice(ft * P, (ft + 1) * P)
                    mms(b.t[:, 0:TOKENS], [(w1v[:, k, f], h_cols[:, k, :]) for k in range(KD)], got1, *b.free)
                    m = mms(b.t[:, TOKENS:2 * TOKENS], [(w3v[:, k, f], h_cols[:, k, :]) for k in range(KD)], got3)
                    if ft == n_ft - 1:
                        s1.free = [m]
                        s3.free = [m]
                    g = gated[n % 3]
                    t1 = a_fn(g, b.t[:, 0:TOKENS], ACT.Silu, m, gated_free[n % 3], chain=False)
                    t2 = pool.put(lambda g=g, q=spread[j]: nc.gpsimd.tensor_tensor(g, g, q, ALU.mult), t1, sp)
                    t3 = v_tt(act_cols[n % 8], b.t[:, TOKENS:2 * TOKENS], g, ALU.mult, t2, cols_free[n % 8],
                              chain=False)
                    b.free = [t3]
                    gated_free[n % 3] = t3
                    if ft == n_ft - 1:
                        spread_free[j] = t2
                    pending.append((e, ft, down_slot, got_down, t3, n))
                    if len(pending) > 1:
                        last = down(*pending.pop(0), False)
                    n += 1
            last = down(*pending.pop(0), True)
            for i in range(TT):
                for half in range(2):
                    b = total[i * 2 + half]
                    put = residual(mod[:, 2, :])
                    b.free = [put(i, half * BANK, BANK, b, last)]
            return vector.last()

        def into_h_cols(*after):
            return rows_to_cols(strided, h_cols, KD, *after)

        def softmax_rows(scores, n, scale, probs, st, m, *after):
            t = v_max(st[:, 0:1], scores, m)
            t = v_ts(st[:, 1:2], st[:, 0:1], -scale, None, ALU.mult, None, t)
            e = a_fn(probs, scores, ACT.Exp, t, *after, scale=scale, bias=st[:, 1:2], accum_out=st[:, 2:3])
            t = v_recip(st[:, 3:4], st[:, 2:3], e)
            return e, v_ts(probs, probs, st[:, 3:4], None, ALU.mult, None, t)

        context = cut(7680, TT, D)
        ctx_cols = cut(9728, KD, TOKENS)
        ctx_mod = cut(11776, 2, D)
        rep_ctx, conds = cut(13824, KD, 32), [cut(14100 + 16 * j, KD) for j in range(3)]
        rows = lambda ap: ap.rearrange("(i p) d -> p i d", p=P)
        c_cols = lambda v: v.rearrange("(p k) -> p k", k=KD)
        stored = {n: nc.dram_tensor(n, (6 * D,), F32, kind="Internal").ap() for n in ("mod_ctx", "mod_one", "mod_two0", "mod_two1")}
        t_cc = repeat_silu(c_cols(a["c_ctx"]), conds[0], rep_ctx, "c_ctx")
        t_c1 = repeat_silu(c_cols(a["c"][0]), conds[1], c_rep[:, 0], "c")
        t_c2 = repeat_silu(c_cols(a["c_2"][0]), conds[2], c_rep[:, 1], "c_2")
        got_ctx = side_load("context", [(context, rows(a["ctx"][0]))], lane=scalar)
        got_x = side_load("x", [(x[:, :, :], rows(a["x"][0]))], lane=scalar)
        got_w = side_load("norm_w", [(norm_w[:, 0, :], a["norm1_w"][0].partition_broadcast(P)),
                                     (norm_w[:, 1, :], a["norm2_w"][0].partition_broadcast(P))])
        for _ in modulation(rep_ctx, a["w_mod"][0], a["b_mod"][0], stored["mod_ctx"], [0], "mod_ctx", t_cc):
            pass
        got_ctx_mod = side_load("ctx_mod", [(ctx_mod, stored["mod_ctx"][0:2 * D].partition_broadcast(P).rearrange("p (a d) -> p a d", a=2))],
                                mod_stored["mod_ctx", 0])
        first = modulation(c_rep[:, 0], a["w_mod"][0], a["b_mod"][0], stored["mod_one"], [0], "mod_one", t_c1)
        for _ in range(3):
            next(first)
        t = norm_modulate(context, norm_w[:, 0, :], ctx_mod[:, 1, :], ctx_mod[:, 0, :], got_ctx, got_w, got_ctx_mod)
        for _ in first:
            pass
        t_ctx = rows_to_cols(strided, ctx_cols, KD, t)
        got_mod = [mod_load("mod_one", stored["mod_one"], part, part) for part in range(2)]
        got_chunk = side_load("chunk", [(ws_t, a["w_s_t"]), (bs_cols, a["b_s_t"])])
        got_attention = side_load("attention", [
            (axial, a["k_axial"].rearrange("p (i c d) -> p i c d", i=TT, c=2)),
            (qk_w, a["qk_norm_w"].partition_broadcast(P).rearrange("p (h d) -> p h d", h=10))])
        got_bounds = side_load("bounds", [(lb_logits, a["hgrn_lb_logits"][0].partition_broadcast(P))])
        got_hgrn_w = side_load("hgrn_w", [(w_c[:, h, :], a["hgrn_norm_w"][0].partition_broadcast(P)) for h in range(C_HEADS)])
        got_latent = side_load("latent", [
            (latent[:, 0:Q_LORA], a["mla_q_a_g_2"][0].partition_broadcast(P)),
            (latent[:, Q_LORA:384], a["mla_kv_a_g_2"][0].partition_broadcast(P)),
            (latent[:, 384:576], a["mla_q_norm_g_2"][0].partition_broadcast(P)),
            (latent[:, 576:768], a["mla_k_norm_g_2"][0].partition_broadcast(P)),
            (latent[:, 768:770].bitcast(I32), a["positions_2_cols"]), (latent[:, 772:804], a["k_freq"])])
        background.append(modulation(c_rep[:, 0], a["w_mod"][0], a["b_mod"][0], stored["mod_one"], [1, 2], "mod_one", t_c1))
        background.append(modulation(c_rep[:, 1], a["ada_w_2"][0], a["ada_b_2"][0], stored["mod_two0"], [0, 1, 2],
                                     "mod_two0", t_c2))
        t = norm_modulate(x, norm_w[:, 0, :], mod[:, 1, :], mod[:, 0, :], got_x, *got_mod, *t_ctx)
        tap("h", h_rows[:, :, :], t)
        t_h = into_h_cols(t)
        normed_1 = t
        route_load("one", a["route_w_one"], a["route_b_one"], normed_1)

        proj = cut(0, TT, IN_W)
        ctx_proj = cut(5120, TT, CTX_W)
        flip = [0]

        def copy_out(dst_of):
            def put(i, c0, n, b, m):
                flip[0] ^= 1
                if flip[0]:
                    return v_copy(dst_of(i, c0, n), b.t[:, 0:n], m, chain=False)
                return a_fn(dst_of(i, c0, n), b.t[:, 0:n], ACT.Copy, m, chain=False)
            return put

        for c0 in range(0, IN_W, BANK):
            s, got = load((lambda v: v[:, :].rearrange("p (k n) -> p k n", k=KD),
                           by_p(a["w_in"][0])[:, :, c0:c0 + BANK]))
            ws = s.t[:, :].rearrange("p (k n) -> p k n", k=KD)
            lo, hi = max(c0, OFF_KV), min(c0 + BANK, OFF_G)
            put_x = copy_out(lambda i, c, n: proj[:, i, c:c + n])
            put_c = copy_out(lambda i, c, n: ctx_proj[:, i, c:c + n])
            for i in range(TT):
                b = next_bank()
                m = mms(b.t[:, :], [(h_cols[:, k, i * P:(i + 1) * P], ws[:, k, :]) for k in range(KD)],
                        got, *t_h, *b.free)
                b.free = [put_x(i, c0, BANK, b, m)]
                if lo < hi:
                    b = next_bank()
                    m = mms(b.t[:, 0:hi - lo],
                            [(ctx_cols[:, k, i * P:(i + 1) * P], ws[:, k, lo - c0:hi - c0]) for k in range(KD)],
                            *t_ctx, *b.free)
                    b.free = [put_c(i, lo - OFF_KV, hi - lo, b, m)]
            s.free = [m]
            step()
        projected = everyone()
        tap("p", proj, *projected)
        tap("pc", ctx_proj, *projected)

        mix_cols = h_cols
        gelu = cut(8200, TT, OFF_B)
        sq = cut(9224, 16, HD)
        got = got_chunk
        t = a_fn(gelu, proj[:, :, 0:OFF_B], ACT.Gelu_apprx_tanh, *projected)
        ya = h_rows[:, :, 0:256]
        for i in range(TT):
            v = gelu[:, i, 256:512].rearrange("p (h d) -> p h d", h=A_HEADS)
            t = head_norm(v, v, A_HEADS, HD, None, sq[:, 0:A_HEADS, :], small[:, 8:12], t, *projected)
            b = next_bank()
            for h in range(A_HEADS):
                m = mms(b.t[:, h * HD:(h + 1) * HD], [(ws_t[:, h, :], v[:, h, :])], got, t, *b.free)
            for h in range(A_HEADS):
                f = slice(h * HD, (h + 1) * HD)
                b.free = [v_stt(ya[:, i, f], b.t[:, f], bs_cols[:, h:h + 1], gelu[:, i, f], ALU.add, ALU.mult, m, got)]
        t_a = b.free[0]
        b = next_bank()
        bv = b.t[:, :].rearrange("p (k t) -> p k t", k=2)
        for k in range(2):
            for i in range(TT):
                m = turn(bv[:, k, i * P:(i + 1) * P], ya[:, i, k * P:(k + 1) * P], t_a, *b.free)
        b.free = [a_fn(mix_cols[:, 0:2, :], bv, ACT.Copy, m)]
        done_a = everyone()

        rot = cut(8576, 10, HD)
        sq = cut(9216, 10, HD)
        q_cols = cut(9856, 4, TOKENS)
        k_cols = cut(10880, B_KV, 2 * TOKENS)
        k_pair = cut(11904, 2 * TT, B_KV, 2, HD)
        probs = [cut(12928 + 512 * j, 512) for j in range(3)]
        probs_t = [cut(11904, 4, TOKENS), cut(14464, 4, TOKENS)]
        got = got_attention
        vector.wait(got, *done_a)
        for i in range(TT):
            qk = proj[:, i, OFF_B:OFF_KV + 128].rearrange("p (h d) -> p h d", h=10)
            t = head_norm(qk, qk, 10, HD, qk_w, sq, small[:, 8:18])
            x4 = qk.rearrange("p h (a s e) -> p (h a) s e", a=2, s=2)
            r4 = rot.rearrange("p h (a s e) -> p (h a) s e", a=2, s=2)
            t = v_copy(r4[:, :, 0, :], x4[:, :, 1, :])
            t = v_copy(r4[:, :, 1, :], x4[:, :, 0, :])
            t = v_tt(rot, rot, axial[:, i, 1, :].unsqueeze(1).to_broadcast([P, 10, HD]), ALU.mult)
            t = v_tt(qk, qk, axial[:, i, 0, :].unsqueeze(1).to_broadcast([P, 10, HD]), ALU.mult)
            t = v_tt(qk, qk, rot, ALU.add)
            kk = ctx_proj[:, i, 0:128].rearrange("p (h d) -> p h d", h=2)
            t = head_norm(kk, kk, 2, HD, qk_w[:, 8:10, :], sq[:, 0:2, :], small[:, 8:10])
            for c in range(2):
                t = v_copy(k_pair[:, i, :, c, :], proj[:, i, OFF_KV:OFF_KV + 128].rearrange("p (h d) -> p h d", h=2))
                t = v_copy(k_pair[:, TT + i, :, c, :], kk)
        t_qk = t
        t_q = rows_to_cols(lambda i, k: proj[:, i, OFF_B + k * P:OFF_B + (k + 1) * P], q_cols, 4, t_qk)
        t_k = []
        for g in range(B_KV):
            b = next_bank()
            for i in range(2 * TT):
                m = turn(b.t[:, i * P:(i + 1) * P], k_pair[:, i, g].rearrange("p a b -> p (a b)"), t_qk, *b.free)
            b.free = [v_copy(k_cols[:, g, :], b.t[:, :], m)]
            t_k += b.free
        scale = HD ** -0.5
        jobs = [(h, i) for h in range(B_HEADS) for i in range(TT)]
        probs_free, probs_t_free = [None] * 3, [None] * 2
        state = {}

        def scores_of(n):
            h, i = jobs[n]
            part = slice(64 * (h % 2), 64 * (h % 2) + 64)
            b = next_bank()
            m = mms(b.t[:, :], [(q_cols[part, h // 2, i * P:(i + 1) * P], k_cols[part, h // 4, :])],
                    *t_q, *t_k, *b.free)
            state[n] = (b, m)

        def attend(n):
            h, i = jobs[n]
            b, m = state[n]
            pr, pt = probs[n % 3], probs_t[h % 2]
            e, t = softmax_rows(b.t[:, :], 512, scale, pr, small[:, 32 + 4 * (n % 4):36 + 4 * (n % 4)], m, probs_free[n % 3])
            b.free = [e]
            b2 = next_bank()
            for kt in range(4):
                m = turn(b2.t[:, kt * P:(kt + 1) * P], pr[:, kt * P:(kt + 1) * P], t, *b2.free)
            probs_free[n % 3] = m
            tc = a_fn(pt[:, :, i * P:(i + 1) * P], b2.t[:, :].rearrange("p (k t) -> p k t", k=4), ACT.Copy, m,
                      probs_t_free[h % 2])
            b2.free = [tc]
            if i == TT - 1:
                b3 = next_bank()
                part = slice(64 * (h % 2), 64 * (h % 2) + 64)
                g = h // 4
                vals = [proj[:, kt, OFF_KV + 128 + g * HD:OFF_KV + 128 + (g + 1) * HD] for kt in range(TT)] + \
                       [ctx_proj[:, kt, 128 + g * HD:128 + (g + 1) * HD] for kt in range(TT)]
                m = mms(b3.t[part, 0:TOKENS], [(vals[kt], pt[:, kt, :]) for kt in range(4)], tc, *b3.free)
                probs_t_free[h % 2] = m
                b3.free = [v_copy(mix_cols[part, 2 + h // 2, :], b3.t[part, 0:TOKENS], m)]

        scores_of(0)
        for n in range(len(jobs)):
            if n + 1 < len(jobs):
                scores_of(n + 1)
            attend(n)
            step()
        while len(background) > 1:
            step()
        got_mod = [mod_load("mod_one", stored["mod_one"], part, at, normed_1) for part, at in ((2, 2), (3, 0), (4, 1))]
        done_b = everyone()

        s_scan, got_scan = load((lambda v: v[:, 0:4096], a["k_scan"]))
        s_scan.held = True
        kc = s_scan.t
        sums = [kc[:, 0:1024], kc[:, 1024:2048]]
        after = [kc[:, 2048:2176], kc[:, 2176:2304]]
        masks = [kc[:, 2304 + d * 896:2304 + (d + 1) * 896].rearrange("p (j t) -> p j t", j=LEVELS) for d in range(2)]
        logf = cut(7680, 2 * TT, 2, CW)
        keys = cut(9728, 2 * TT, 2, CW)
        lb = cut(13824, 3, 2, CW)
        q_act = h_rows[:, :, 0:256]
        scalar.wait(*done_b)
        t = v_tt(lb[:, 0], lb_logits, lb_logits, ALU.subtract, got_bounds, *done_b)
        t = a_fn(lb[:, 0], lb[:, 0], ACT.Exp, t)
        t = v_recip(lb[:, 1], lb[:, 0], t)
        t = v_tt(lb[:, 0], lb[:, 0], lb[:, 1], ALU.mult, t)
        t = v_tt(lb[:, 0], lb[:, 0], lb[:, 0], ALU.subtract, t)
        t = v_ts(lb[:, 1], lb[:, 0], -1.0, 1.0, ALU.mult, ALU.add, t)
        zs = [proj[:, :, OFF_C + CW:OFF_C + 3 * CW], ctx_proj[:, :, 256 + CW:256 + 3 * CW]]
        logs = [logf[:, 2 * n:2 * n + 2].rearrange("p i a b -> p i (a b)") for n in range(2)]
        sigs = [keys[:, 2 * n:2 * n + 2].rearrange("p i a b -> p i (a b)") for n in range(2)]
        for n in range(2):
            a_fn(logs[n], zs[n], ACT.Abs, chain=False)
        for n in range(2):
            a_fn(logs[n], logs[n], ACT.Exp, scale=-1.0)
        t_ln = [a_fn(logs[n], logs[n], ACT.Ln, bias=1.0) for n in range(2)]
        t_lb = a_fn(lb[:, 2], lb[:, 1], ACT.Ln, t)
        t_sig = [a_fn(sigs[n], zs[n], ACT.Sigmoid, scale=-1.0) for n in range(2)]
        t_silu = a_fn(q_act, proj[:, :, OFF_C:OFF_C + CW], ACT.Silu)
        spread = lambda ap: ap.rearrange("p a b -> p (a b)").unsqueeze(1).to_broadcast([P, TT, 2 * CW])
        for n in range(2):
            v_stt(logs[n], zs[n], 0.0, logs[n], ALU.min, ALU.subtract, t_ln[n], chain=False)
        for n in range(2):
            t_logf = v_tt(logs[n], logs[n], spread(lb[:, 2]), ALU.add, t_lb)
        for n in range(2):
            t = v_tt(sigs[n], sigs[n], spread(lb[:, 1]), ALU.mult, t_sig[n], chain=False)
        t_in = [t, t_silu]

        q_c = proj[:, :, 512:768]
        k_c = [proj[:, :, 768:1024], ctx_proj[:, :, 0:256]]
        gates = cut(11776, 8, 2, TOKENS)
        att = [h_rows[:, par, 256:768].rearrange("p (c t) -> p c t", c=4) for par in range(2)]
        rows64 = [slice(0, 64), slice(64, 128)]
        t_q = rows_to_cols(lambda i, k: q_act[:, i, k * P:(k + 1) * P], q_c, 2, *t_in)
        t_k = []
        for d in range(2):
            t_k += rows_to_cols(lambda i, k: keys[:, i, d, k * P:(k + 1) * P], k_c[d], 2, *t_in)
        t_in.append(vector.last())
        ksum = gates[:, 0]
        t = v_tt(ksum, k_c[0], k_c[1], ALU.add, *t_k)
        blocks = [(i, pair_) for i in range(TT) for pair_ in range(2)]
        for par in range(2):
            b = next_bank()
            for c, (i, pair_) in enumerate(blocks):
                m = mms(b.t[:, c * P:(c + 1) * P],
                        [(ksum[rows64[par], pair_, i * P:(i + 1) * P], q_c[rows64[par], pair_, i * P:(i + 1) * P])],
                        t, *t_q, *t_in, *b.free)
            b.free = [v_tt(att[par], b.t[:, :].rearrange("p (c t) -> p c t", c=4),
                           ident[:, :].unsqueeze(1).to_broadcast([P, 4, P]), ALU.mult, m)]
        q_in = [proj[:, :, 0:256], proj[:, :, 256:512]]
        for d in range(2):
            gate_free = [tensor.last(), vector.last()]
            t_g = []
            for pair_ in range(2):
                for i in range(TT):
                    for half in range(2):
                        b = next_bank()
                        m = mms(b.t[:, :], [(logf[:, i, d, pair_ * P:(pair_ + 1) * P],
                                             sums[d][:, half * BANK:(half + 1) * BANK])], got_scan, *t_in, *b.free)
                        b.free = [a_fn(gates[:, half * 4:half * 4 + 4, pair_, i * P:(i + 1) * P],
                                       b.t[:, :].rearrange("p (j t) -> p j t", j=4), ACT.Exp, m, *gate_free)]
            t_g = b.free[0]
            for j in range(LEVELS):
                w = 1 << j
                cutj = lambda ap: ap.rearrange("p a (b s w) -> p a b s w", s=2, w=w)
                gj, qj, kj = cutj(gates[:, j]), cutj(q_c), cutj(k_c[d])
                qs, ks = (1, 0) if d == 0 else (0, 1)
                t = v_tt(gj[:, :, :, qs, :], gj[:, :, :, qs, :], qj[:, :, :, qs, :], ALU.mult, t_g, *t_q)
                t = v_tt(gj[:, :, :, ks, :], gj[:, :, :, ks, :], kj[:, :, :, ks, :], ALU.mult, *t_k)
                mask = masks[d][:, j, :].bitcast(U32).unsqueeze(1).to_broadcast([P, 4, P])
                for par in range(2):
                    b = next_bank()
                    for c, (i, pair_) in enumerate(blocks):
                        g = gates[rows64[par], j, pair_, i * P:(i + 1) * P]
                        m = mms(b.t[:, c * P:(c + 1) * P], [(g, g)], t, *b.free)
                    b.free = [dve(lambda par=par, b=b, mask=mask: nc.vector.copy_predicated(
                        att[par], mask, b.t[:, :].rearrange("p (c t) -> p c t", c=4)), m, got_scan)]
                step()
            t = v_tt(q_in[d], gates[:, 7], q_c, ALU.mult)
        t_att = t

        st_free = everyone()
        vals = [proj[:, i, OFF_C + 3 * CW:OFF_C + 4 * CW] for i in range(TT)] + \
               [ctx_proj[:, i, 256 + 3 * CW:256 + 4 * CW] for i in range(TT)]
        st = [[gates[:, 2 * d + j].rearrange("p a b -> p (a b)")[:, 0:128].rearrange("p (a b) -> p a b", a=2)
               for j in range(2)] for d in range(2)]
        order = [[2, 3, 0], [3, 2, 1]]
        state_at = {}
        for d in range(2):
            for nth, n in enumerate(order[d]):
                b = next_bank()
                m = mms(b.t[:, 0:CW], [(after[d], logf[:, n, d, :])], got_scan, *t_in, *b.free)
                for pair_ in range(2):
                    m = mms(b.t[:, CW + 2 * pair_:CW + 2 * pair_ + 1],
                            [(logf[:, n, d, pair_ * P:(pair_ + 1) * P], ones[:, 0:1])])
                te = a_fn(small[:, 60:62], b.t[:, CW:CW + 4:2], ACT.Exp, m, vector.last())
                t = a_fn(gates[:, 5, 0, :], b.t[:, 0:CW], ACT.Exp, vector.last())
                b.free = [t]
                t = v_tt(keys[:, n, d, :], keys[:, n, d, :], gates[:, 5, 0, :], ALU.mult, t, *st_free)
                b = next_bank()
                for h in range(C_HEADS):
                    part = slice(64 * (h % 2), 64 * (h % 2) + 64)
                    m = mms(b.t[part, (h // 2) * HD:(h // 2 + 1) * HD],
                            [(keys[:, n, d, h * HD:(h + 1) * HD], vals[n][:, h * HD:(h + 1) * HD])], t, *b.free)
                new = st[d][nth % 2]
                bv = b.t[:, 0:2 * HD].rearrange("p (a b) -> p a b", a=2)
                if nth == 0:
                    b.free = [v_copy(new, bv, m, *st_free)]
                else:
                    old = st[d][(nth - 1) % 2]
                    for pair_ in range(2):
                        b.free = [v_stt(new[:, pair_, :], old[:, pair_, :], small[:, 60 + pair_:61 + pair_],
                                        bv[:, pair_, :], ALU.mult, ALU.add, m, te, *st_free)]
                if nth >= 1:
                    tile = (0 if nth == 1 else 1) if d == 0 else (1 if nth == 1 else 0)
                    state_at[d, tile] = (new, b.free[0])
        o_rows = gates[:, 6:8].rearrange("p j a b -> p (j a b)")[:, 0:512].rearrange("p (i c) -> p i c", i=TT)
        for i in range(TT):
            for par in range(2):
                b = next_bank()
                for pair_ in range(2):
                    h = 2 * pair_ + par
                    o_part = b.t[:, pair_ * HD:(pair_ + 1) * HD]
                    m = mms(o_part, [(att[par][:, 2 * i + pair_, :], vals[i][:, h * HD:(h + 1) * HD])],
                            t_att, state_at[0, i][1], state_at[1, i][1], *b.free, stop=False)
                    m = mms(o_part, [(q_in[d][rows64[par], pair_, i * P:(i + 1) * P],
                                      state_at[d, i][0][rows64[par], pair_, :]) for d in range(2)], start=False)
                o4 = o_rows[:, i, :].rearrange("p (a b d) -> p a b d", a=2, b=2)
                b.free = [v_copy(o4[:, :, par, :], b.t[:, 0:P].rearrange("p (a d) -> p a d", a=2), m)]
        tap("o", o_rows, b.free[0])
        s_scan.free, s_scan.held = everyone(), False
        sq = cut(9984, C_HEADS, HD)
        sil = cut(10240, TT, CW)
        got = got_hgrn_w
        t = a_fn(sil, proj[:, :, OFF_G:IN_W], ACT.Silu, *everyone())
        vector.wait(got, t)
        for i in range(TT):
            o = o_rows[:, i, :].rearrange("p (h d) -> p h d", h=C_HEADS)
            t = head_norm(o, o, C_HEADS, HD, w_c, sq, small[:, 8:12])
            t = v_tt(o_rows[:, i, :], o_rows[:, i, :], sil[:, i, :], ALU.mult)
        t = rows_to_cols(lambda i, k: o_rows[:, i, k * P:(k + 1) * P], mix_cols[:, 6:8, :], 2, t)
        mixed = everyone()
        tap("mix", mix_cols[:, :, :], *mixed)

        product_rows(mix_cols, KD, a["w_out"][0], by_k, D, residual(mod[:, 2, :]), *mixed, *got_mod)
        finish()
        done = everyone()
        tap("x1", x[:, :, :], *done)
        got_gate = mod_load("mod_one", stored["mod_one"], 5, 2, *done)
        t = norm_modulate(x, norm_w[:, 1, :], mod[:, 1, :], mod[:, 0, :], *got_mod, *done)
        t = into_h_cols(t, *done)
        vector.wait(got_gate)
        experts("one", 4, 8, 512, a["w1"][0], a["w3"][0], a["w2"][0], *t, *everyone())
        done = everyone()
        tap("xa", x[:, :, :], *done)

        for layer in range(2):
            name = f"two{layer}"
            got_w = side_load(name + "_norm_w", [
                (norm_w[:, 0, :], a["norm_mix_g_2"][layer].partition_broadcast(P)),
                (norm_w[:, 1, :], a["norm_ffn_g_2"][layer].partition_broadcast(P))], *done)
            mod_name = "mod_" + name
            got_mod = [mod_load(mod_name, stored[mod_name], part, part, *done) for part in range(3)]
            if layer == 0:
                background.append(modulation(c_rep[:, 1], a["ada_w_2"][1], a["ada_b_2"][1], stored["mod_two1"],
                                             [0, 1, 2], "mod_two1", t_c2))
                background.append(filters(*done))
            t = norm_modulate(x, norm_w[:, 0, :], mod[:, 1, :], mod[:, 0, :], got_w, *got_mod, *done)
            route_load(name, a["route_w_" + name], a["route_b_" + name], t)
            next_mod = [mod_load(mod_name, stored[mod_name], part, at, t) for part, at in ((3, 0), (4, 1))]
            t_h = into_h_cols(t, *done)
            ready = everyone()

            if layer == 0:
                lat = cut(0, TT, 448)
                cq_c, ckv_c = cut(896, 2, TOKENS), cut(1408, 1, TOKENS)
                q = cut(1664, TT, 1536)
                kv = cut(4736, TT, 2048)
                q_pe = cut(8832, TT, 8, ROPE)
                k_pe2 = cut(9856, TT, 2, ROPE)
                qn_c, qp_c = cut(10112, 8, TOKENS), cut(12160, 4, TOKENS)
                kn_c, kp_c = cut(13184, 8, TOKENS), cut(15232, 1, TOKENS)
                pr = [cut(256 * j, TOKENS) for j in range(3)]
                pt = [cut(768 + 512 * j, TT, TOKENS) for j in range(2)]
                w_lat, w_q, w_k = latent[:, 0:384], latent[:, 384:576], latent[:, 576:768]
                cs, sn = (cut(15488 + 64 * j, TT, HALF) for j in range(2))
                ang, red = (h_rows[:, 0, 832 + 64 * j:896 + 64 * j].rearrange("p (i c) -> p i c", i=TT)
                            for j in range(2))
                pos_i, freq = latent[:, 768:770].bitcast(I32), latent[:, 772:804]
                pos_f = latent[:, 770:772]
                sq = h_rows[:, 1, :]
                got = got_latent
                vector.wait(got)
                t = v_copy(pos_f, pos_i, *ready)
                for i in range(TT):
                    t = v_ts(ang[:, i, :], freq, pos_f[:, i:i + 1], None, ALU.mult, None)
                for dst, turns in ((sn, 0.0), (cs, 0.25)):
                    t = v_ts(red, ang, float(1 / (2 * np.pi)), turns, ALU.mult, ALU.add)
                    t = v_ts(red, red, ROUND, -ROUND, ALU.add, ALU.add)
                    t = v_stt(dst, red, -TWO_PI_1, ang, ALU.mult, ALU.add)
                    t = v_stt(dst, red, -TWO_PI_2, dst, ALU.mult, ALU.add)
                    t = v_stt(dst, red, -TWO_PI_3, dst, ALU.mult, ALU.add)
                    t = v_ts(dst, dst, float(np.pi / 2) * turns * 4, PI_IN, ALU.add, ALU.min)
                    t = v_ts(dst, dst, -PI_IN, None, ALU.max, None)
                    t_trig = a_fn(dst, dst, ACT.Sin, t)

                product_rows(h_cols, KD, a["mla_w_down_2"][0], by_p, 448,
                             copy_out(lambda i, c, n: lat[:, i, c:c + n]), *t_h)
                vector.wait(*everyone())
                for i in range(TT):
                    g3 = lambda ap, g: ap.rearrange("p (g w) -> p g w", g=g)
                    for lo, hi in ((0, Q_LORA), (Q_LORA, 384)):
                        t = head_norm(g3(lat[:, i, lo:hi], 1), g3(lat[:, i, lo:hi], 1), 1, hi - lo,
                                      g3(w_lat[:, lo:hi], 1), g3(sq[:, 0:hi - lo], 1), small[:, 8:9], t_trig)
                    t = head_norm(g3(lat[:, i, 384:448], 1), g3(lat[:, i, 384:448], 1), 1, ROPE,
                                  g3(w_k[:, NOPE:], 1), g3(sq[:, 0:ROPE], 1), small[:, 8:9])
                    x1_, x2_ = lat[:, i, 384:416], lat[:, i, 416:448]
                    c_, s_ = cs[:, i, :], sn[:, i, :]
                    u1, u2 = sq[:, 0:32], sq[:, 32:64]
                    o1, o2 = k_pe2[:, i, 0, 0:32], k_pe2[:, i, 0, 32:64]
                    v_tt(u1, x1_, c_, ALU.mult)
                    v_tt(u2, x2_, s_, ALU.mult)
                    v_tt(o1, u1, u2, ALU.subtract)
                    v_tt(u1, x1_, s_, ALU.mult)
                    v_tt(u2, x2_, c_, ALU.mult)
                    v_tt(o2, u1, u2, ALU.add)
                    t = v_copy(k_pe2[:, i, 1, :], k_pe2[:, i, 0, :])
                t_cq = rows_to_cols(lambda i, k: lat[:, i, k * P:(k + 1) * P], cq_c, 2, t)
                t_ckv = rows_to_cols(lambda i, k: lat[:, i, Q_LORA:384], ckv_c, 1, t)
                t_kp = rows_to_cols(lambda i, k: k_pe2[:, i].rearrange("p a b -> p (a b)"), kp_c, 1, t)
                product_rows(cq_c, 2, a["mla_w_uq_2"][0], by_k, 1536,
                             copy_out(lambda i, c, n: q[:, i, c:c + n]), *t_cq)
                product_rows(ckv_c, 1, a["mla_w_ukv_2"][0], by_k, 2048,
                             copy_out(lambda i, c, n: kv[:, i, c:c + n]), *t_ckv)
                vector.wait(*everyone())
                for i in range(TT):
                    qi = q[:, i, :].rearrange("p (h d) -> p h d", h=8)
                    ki = kv[:, i, :].rearrange("p (h d) -> p h d", h=8)
                    sq3 = sq.rearrange("p (h d) -> p h d", h=8)
                    bw = lambda ap, n: ap.unsqueeze(1).to_broadcast([P, 8, n])
                    head_norm(qi[:, :, 0:NOPE], qi[:, :, 0:NOPE], 8, NOPE, bw(w_q[:, 0:NOPE], NOPE), sq3, small[:, 8:16])
                    head_norm(ki[:, :, 0:NOPE], ki[:, :, 0:NOPE], 8, NOPE, bw(w_k[:, 0:NOPE], NOPE), sq3, small[:, 8:16])
                    head_norm(qi[:, :, NOPE:], qi[:, :, NOPE:], 8, ROPE, bw(w_q[:, NOPE:], ROPE), sq3[:, :, 0:ROPE],
                              small[:, 8:16])
                    x1_, x2_ = qi[:, :, NOPE:NOPE + 32], qi[:, :, NOPE + 32:]
                    c_, s_ = bw(cs[:, i, :], HALF), bw(sn[:, i, :], HALF)
                    u1, u2 = sq3[:, :, 0:32], sq3[:, :, 32:64]
                    v_tt(u1, x1_, c_, ALU.mult)
                    v_tt(u2, x2_, s_, ALU.mult)
                    v_tt(q_pe[:, i, :, 0:32], u1, u2, ALU.subtract)
                    v_tt(u1, x1_, s_, ALU.mult)
                    v_tt(u2, x2_, c_, ALU.mult)
                    t = v_tt(q_pe[:, i, :, 32:64], u1, u2, ALU.add)
                t_qn = rows_to_cols(lambda i, h: q[:, i, h * 192:h * 192 + NOPE], qn_c, 8, t)
                t_kn = rows_to_cols(lambda i, h: kv[:, i, h * 256:h * 256 + NOPE], kn_c, 8, t)
                t_qp = rows_to_cols(lambda i, k: q_pe[:, i, 2 * k:2 * k + 2, :].rearrange("p a b -> p (a b)"),
                                    qp_c, 4, t)
                out_c = h_cols
                scale = (NOPE + ROPE) ** -0.5
                jobs = [(h, i) for h in range(8) for i in range(TT)]
                pr_free, pt_free, state = [None] * 3, [None] * 2, {}

                def scores2(n):
                    h, i = jobs[n]
                    part = slice(64 * (h % 2), 64 * (h % 2) + 64)
                    b = next_bank()
                    mms(b.t[:, 0:TOKENS], [(qn_c[:, h, i * P:(i + 1) * P], kn_c[:, h, :])],
                        *t_qn, *t_kn, *b.free, stop=False)
                    m = mms(b.t[:, 0:TOKENS], [(qp_c[part, h // 2, i * P:(i + 1) * P], kp_c[part, 0, :])],
                            *t_qp, *t_kp, start=False)
                    state[n] = (b, m)

                def attend2(n):
                    h, i = jobs[n]
                    b, m = state[n]
                    r, tr = pr[n % 3], pt[h % 2]
                    e, t = softmax_rows(b.t[:, 0:TOKENS], TOKENS, scale, r,
                                        small[:, 32 + 4 * (n % 4):36 + 4 * (n % 4)], m, pr_free[n % 3])
                    b.free = [e]
                    b2 = next_bank()
                    for kt in range(TT):
                        m = turn(b2.t[:, kt * P:(kt + 1) * P], r[:, kt * P:(kt + 1) * P], t, *b2.free)
                    pr_free[n % 3] = m
                    tc = a_fn(tr[:, :, i * P:(i + 1) * P], b2.t[:, 0:TOKENS].rearrange("p (k t) -> p k t", k=TT),
                              ACT.Copy, m, pt_free[h % 2])
                    b2.free = [tc]
                    if i == TT - 1:
                        b3 = next_bank()
                        m = mms(b3.t[:, 0:TOKENS], [(kv[:, kt, h * 256 + NOPE:(h + 1) * 256], tr[:, kt, :])
                                                    for kt in range(TT)], tc, *b3.free)
                        pt_free[h % 2] = m
                        b3.free = [v_copy(out_c[:, h, :], b3.t[:, 0:TOKENS], m)]

                scalar.wait(*everyone())
                scores2(0)
                for n in range(len(jobs)):
                    if n + 1 < len(jobs):
                        scores2(n + 1)
                    attend2(n)
                    for _ in range(3):
                        step()
                product_rows(out_c, KD, a["mla_w_o_2"][0], by_k, D, residual(mod[:, 2, :]), *everyone())
            else:
                u = cut(0, 24, TOKENS)
                params = cut(6144, 5, 24)
                padded = [cut(6272 + 264 * j, 264) for j in range(3)]
                kr, ki, kn = ([cut(7064 + 2560 * h, TT, BANK) for h in range(2)],
                              [cut(8088 + 2560 * h, TT, BANK) for h in range(2)],
                              [cut(9112 + 2560 * h, BANK) for h in range(2)])
                spec, tmp = cut(12184, 4, BANK), cut(14232, BANK)
                prod = spare[:, 0:2048].rearrange("p (a b) -> p a b", a=4)
                got = side_load("hyena", [(params.rearrange("p a b -> p (a b)"), a["hy_cols"])], *ready)

                def spectrum_load(o, hv, *after_):
                    cols = slice(hv * BANK, (hv + 1) * BANK)
                    return side_load(f"spectrum{o}{hv}", [
                        (kr[hv], spectra["real"][o][:, :, cols]), (ki[hv], spectra["imag"][o][:, :, cols]),
                        (kn[hv][1:P, :], spectra["real"][o][1:P, 0, cols]),
                        (kn[hv][0:1, :], spectra["nyquist"][o][:, cols])],
                        *spectrum_stored[o, 2 * hv], *spectrum_stored[o, 2 * hv + 1], *after_, lane=sync)

                zeroed = [dve(lambda q=q: nc.vector.memset(q, 0.0), *ready) for q in padded]
                vector.wait(got)
                scalar.wait(got)
                pad_free = [zeroed[-1]] * 3
                wv = by_p(a["hy_w_in_2"][0])
                n = 0
                for c0 in range(0, 3 * D, BANK):
                    s, got_s = load((lambda v: v[:, :].rearrange("p (k n) -> p k n", k=KD), wv[:, :, c0:c0 + BANK]))
                    ws = s.t[:, :].rearrange("p (k n) -> p k n", k=KD)
                    for f in range(4):
                        b = next_bank()
                        m = mms(b.t[:, 0:TOKENS], [(ws[:, k, f * P:(f + 1) * P], h_cols[:, k, :]) for k in range(KD)],
                                got_s, *t_h, *b.free)
                        pd = padded[n % 3]
                        t = a_fn(pd[:, 1:257], b.t[:, 0:TOKENS], ACT.Identity, m, pad_free[n % 3],
                                 bias=params[:, 0, n:n + 1], chain=False)
                        b.free = [t]
                        v_ts(u[:, n, :], pd[:, 1:257], params[:, 2, n:n + 1], params[:, 4, n:n + 1], ALU.mult, ALU.add, t)
                        v_stt(u[:, n, :], pd[:, 0:256], params[:, 1, n:n + 1], u[:, n, :], ALU.mult, ALU.add)
                        pad_free[n % 3] = v_stt(u[:, n, :], pd[:, 2:258], params[:, 3, n:n + 1], u[:, n, :],
                                                ALU.mult, ALU.add)
                        n += 1
                    s.free = [m]
                tap("u", u, vector.last())
                s_four, got_four = load((lambda v: v[:, 0:2048], a["k_fourier"][:, 0:2048]))
                s_four.held = True
                got_k = {hv: spectrum_load(0, hv, *ready) for hv in range(2)}
                fc = s_four.t
                ahead = fc[:, 0:1024].rearrange("p (k f) -> p k f", k=TT)
                back = fc[:, 1024:2048].rearrange("p (k t) -> p k t", k=4)
                z_rows = h_rows
                def cols_to_rows(src, after_):
                    toks = []
                    for i in range(TT):
                        for q4 in range(2):
                            b = next_bank()
                            for k in range(4):
                                m = turn(b.t[:, k * P:(k + 1) * P], src(q4 * 4 + k)[:, i * P:(i + 1) * P], *after_, *b.free)
                            b.free = [a_fn(z_rows[:, i, q4 * BANK:(q4 + 1) * BANK], b.t[:, :], ACT.Copy, m)]
                            toks += b.free
                    return toks
                done_u = everyone()
                t_z = cols_to_rows(lambda k: u[:, 16 + k, :], done_u)
                for o in range(2):
                    for hv in range(2):
                        dcol = slice(hv * BANK, (hv + 1) * BANK)
                        for f4 in range(4):
                            b = next_bank()
                            m = mms(b.t[:, :], [(ahead[:, i, f4 * P:(f4 + 1) * P], z_rows[:, i, dcol]) for i in range(TT)],
                                    *t_z, got_four, *b.free)
                            b.free = [a_fn(spec[:, f4, :], b.t[:, :], ACT.Copy, m, vector.last(), chain=False)]
                        vector.wait(b.free[0], got_k[hv])
                        prod_free = tensor.last()
                        for ft in range(TT):
                            ur, ui = spec[:, ft, :], spec[:, 2 + ft, :]
                            kni = kn[hv] if ft == 0 else kr[hv][:, 1, :]
                            v_tt(prod[:, ft, :], ur, kr[hv][:, ft, :], ALU.mult, prod_free)
                            v_tt(tmp, ui, ki[hv][:, ft, :], ALU.mult)
                            v_tt(prod[:, ft, :], prod[:, ft, :], tmp, ALU.subtract)
                            v_tt(prod[:, 2 + ft, :], ur, ki[hv][:, ft, :], ALU.mult)
                            v_tt(tmp, ui, kni, ALU.mult)
                            t = v_tt(prod[:, 2 + ft, :], prod[:, 2 + ft, :], tmp, ALU.add)
                        if o == 0:
                            got_k[hv] = spectrum_load(1, hv, t)
                        for dt in range(4):
                            k = hv * 4 + dt
                            b = next_bank()
                            m = mms(b.t[:, 0:TOKENS], [(prod[:, f4, dt * P:(dt + 1) * P], back[:, f4, :]) for f4 in range(4)],
                                    t, *b.free)
                            gate_u = u[:, o * 8 + k, :]
                            b.free = [v_tt(gate_u, b.t[:, 0:TOKENS], gate_u, ALU.mult, m)]
                    if o == 0:
                        t_z = cols_to_rows(lambda k: u[:, k, :], everyone())
                s_four.free, s_four.held = everyone(), False
                product_rows(u[:, 8:16, :], KD, a["hy_w_out_2"][0], by_k, D, residual(mod[:, 2, :]), *everyone())

            finish()
            done = everyone()
            tap(f"xmix{layer}", x[:, :, :], *done)
            got_gate = mod_load(mod_name, stored[mod_name], 5, 2, *done)
            t = norm_modulate(x, norm_w[:, 1, :], mod[:, 1, :], mod[:, 0, :], *next_mod, *done)
            t = into_h_cols(t, *done)
            vector.wait(got_gate)
            experts(name, 4, 4, 256, a["moe_w_gate_2"][layer], a["moe_w_up_2"][layer], a["moe_w_down_2"][layer],
                    *t, *everyone())
            done = everyone()
            tap(f"xout{layer}", x[:, :, :], *done)

        stored = sem("stored")
        sync.dma(out[0].rearrange("(i p) d -> p i d", p=P), x[:, :, :], stored, *done)
        sync.wait((stored, 16))

        block = ctx.enter_context(nc.Block())

        @block.sync
        def _(e):
            sync.run(e)

        @block.tensor
        def _(e):
            tensor.run(e)

        @block.vector
        def _(e):
            vector.run(e)

        @block.scalar
        def _(e):
            scalar.run(e)

        @block.gpsimd
        def _(e):
            pool.run(e)


def lay_out(inputs):
    arrays = {k: np.ascontiguousarray(v) for k, v in inputs.items()}
    arrays["w_s_t"] = np.ascontiguousarray(arrays.pop("w_s")[0].transpose(2, 0, 1))
    arrays["b_s_t"] = np.ascontiguousarray(arrays.pop("b_s")[0].T)
    arrays["positions_2_cols"] = np.ascontiguousarray(arrays.pop("positions_2")[0].astype(np.int32).reshape(TT, P).T)
    cols = [arrays.pop("hy_b_in_2")[0], *arrays.pop("hy_conv_w_2")[0], arrays.pop("hy_conv_b_2")[0]]
    arrays["hy_cols"] = np.ascontiguousarray(
        np.stack([c.reshape(24, P) for c in cols]).transpose(2, 0, 1).reshape(P, 120))
    arrays["hy_f_cols"] = np.ascontiguousarray(np.stack(
        [arrays.pop(f"hy_f_{w}{l}_2")[0] for l in (1, 2, 3) for w in ("b", "freq")], axis=1))
    arrays["route_w_one"] = np.concatenate([arrays.pop("w_grp")[0], arrays.pop("w_exp")[0]], axis=1)
    arrays["route_b_one"] = np.concatenate([arrays.pop("b_grp")[0], arrays.pop("b_exp")[0]])
    wg, we, bg, be = (arrays.pop(f"moe_{n}_2") for n in ("wg", "we", "bg", "be"))
    for layer in range(2):
        arrays[f"route_w_two{layer}"] = np.concatenate([wg[layer], we[layer]], axis=1)
        arrays[f"route_b_two{layer}"] = np.concatenate([bg[layer], be[layer]])
    arrays["qk_norm_w"] = np.concatenate([arrays.pop("q_norm_w")[0]] * B_HEADS + [arrays.pop("k_norm_w")[0]] * B_KV)
    arrays.update(shape_constants())
    return arrays


def kernel(**inputs):
    import concourse.bacc as bacc
    from concourse.bass_utils import run_bass_kernel_spmd

    arrays = lay_out(inputs)
    nc = bacc.Bacc("TRN2", target_bir_lowering=False, num_devices=1)
    handles = {k: nc.dram_tensor(f"in_{k}", v.shape, mybir.dt.from_np(v.dtype), kind="ExternalInput").ap()
               for k, v in arrays.items()}
    out = nc.dram_tensor("out", (1, TOKENS, D), F32, kind="ExternalOutput").ap()
    build(nc, handles, out)
    result = run_bass_kernel_spmd(nc, [{f"in_{k}": v for k, v in arrays.items()}], core_ids=[0])
    return result.results[0]["out"]
```

```python
from contextlib import ExitStack

import numpy as np

import concourse.bass as bass
import concourse.mybir as mybir

F32 = mybir.dt.float32
I32 = mybir.dt.int32
U32 = mybir.dt.uint32
ACT = mybir.ActivationFunctionType
ALU = mybir.AluOpType
AX = mybir.AxisListType.X

P = 128
TOKENS = 256
TT = TOKENS // P
D = 1024
KD = D // P
EPS = 1e-6
BANK = 512

A_HEADS, HD = 4, 64
B_HEADS, B_KV = 8, 2
C_HEADS = 4
CW = C_HEADS * HD
OFF_B, OFF_KV, OFF_C, OFF_G, IN_W = 512, 1024, 1280, 2304, 2560
CTX_W = OFF_G - OFF_KV
GRID_W = 64

Q_LORA, NOPE, ROPE = 256, 128, 64
HALF = ROPE // 2
LEVELS = 7
CTX_NORM = 6
BIG = 1e30

SLOT, SLOTS = 4096, 5
WORK = 15872
SPARE = 4096

PLACES = 64

TWO_PI_1 = 6.28125
TWO_PI_2 = float(np.float32(2 * np.pi - 6.28125))
TWO_PI_3 = float(2 * np.pi - 6.28125 - np.float64(np.float32(2 * np.pi - 6.28125)))
ROUND = 1.5 * 2.0 ** 23
PI_IN = 3.1415925


def shape_constants():
    t = np.arange(P)
    fwd, bwd, mask_f, mask_b = [], [], [], []
    r = t[:, None]
    for j in range(LEVELS):
        size = 2 << j
        mid = t // size * size + size // 2
        right = (t >> j & 1) == 1
        fwd.append(np.where(right, (r >= mid) & (r <= t), (r > t) & (r < mid)))
        bwd.append(np.where(right, (r >= mid) & (r < t), (r >= t) & (r < mid)))
        same = (r // size) == (t // size)
        rright = (r >> j & 1) == 1
        mask_f.append(same & ~rright & right)
        mask_b.append(same & rright & ~right)
    fwd.append(r <= t)
    bwd.append(r >= t)
    after_f, after_b = r > t, r < t
    scan = np.concatenate(fwd + bwd + [after_f, after_b] + mask_f + mask_b, axis=1)
    scan = scan.astype(np.float32)

    row = np.repeat(np.arange(TOKENS // GRID_W), GRID_W).astype(np.float32)
    col = np.tile(np.arange(GRID_W), TOKENS // GRID_W).astype(np.float32)
    inv = (1.0 / (np.float32(10000.0) ** (np.arange(0, 32, 2, dtype=np.float32) / np.float32(32)))).astype(np.float32)
    ang = np.stack([row[:, None] * inv, col[:, None] * inv], axis=1)
    cos = np.repeat(np.cos(ang)[:, :, None, :], 2, axis=2).reshape(TOKENS, HD)
    sin = np.stack([-np.sin(ang), np.sin(ang)], axis=2).reshape(TOKENS, HD)
    axial = np.concatenate([cos, sin], axis=1).astype(np.float32)
    axial = axial.reshape(TT, P, 2 * HD).transpose(1, 0, 2).reshape(P, -1)

    inv2 = (1.0 / (np.float32(10000.0) ** (np.arange(0, ROPE, 2, dtype=np.float32) / np.float32(ROPE)))).astype(np.float32)
    freq = np.tile(inv2[None, :], (P, 1)).astype(np.float32)

    L = TOKENS
    f, s = np.arange(L)[None, :], np.arange(L)[:, None]
    w = 2 * np.pi * ((f * s) % (2 * L)) / (2 * L)
    alt = np.where(np.arange(L) % 2 == 0, 1.0, -1.0)
    real, imag = np.cos(w), -np.sin(w)
    imag[:, 0] = alt
    ahead = np.concatenate([real, imag], axis=1)
    back_r = 2 * np.cos(w).T / (2 * L)
    back_r[0] /= 2
    back_i = -2 * np.sin(w).T / (2 * L)
    back_i[0] = alt / (2 * L)
    back = np.concatenate([back_r, back_i], axis=0)
    tl = np.linspace(0.0, 1.0, L, dtype=np.float32)[:, None]
    deltas = np.abs(np.linspace(np.log(0.3) / 1e-2, np.log(1.5) / 1e-2, D, dtype=np.float32))
    decay = np.exp(-tl * deltas)
    fold = lambda a, n: a.reshape(n, P, -1).transpose(1, 0, 2).reshape(P, -1)
    fourier = np.concatenate([fold(ahead, 2), fold(back, 4), fold(decay, 2)], axis=1).astype(np.float32)

    bands = 16
    wl = (2.0 * np.pi * np.arange(L, dtype=np.float32)[:, None] / L).astype(np.float32)
    fr = np.linspace(1e-4, bands - 1, bands, dtype=np.float32)[None, :]
    feats = np.concatenate([tl, np.cos(fr * wl), -np.sin(fr * wl)], axis=-1).astype(np.float32)
    return {
        "k_scan": scan, "k_axial": axial, "k_freq": freq, "k_fourier": fourier,
        "k_before": np.concatenate([(r < t), np.tile(np.concatenate([np.arange(PLACES) - 1000] + [
            np.arange(TT * n) % n != 0 for n in (4, 16, 32)]), (P, 1))], axis=1).astype(np.float32),
        "k_feats": np.ascontiguousarray(feats.T), "k_ident": np.eye(P, dtype=np.float32),
    }


class Lane:

    def __init__(self, sem):
        self.sem, self.count, self.steps, self.seen = sem, 0, [], {}

    def wait(self, *tokens):
        for tok in tokens:
            if tok is None:
                continue
            if isinstance(tok, list):
                self.wait(*tok)
                continue
            sem, value = tok
            if self.seen.get(id(sem), 0) < value:
                self.seen[id(sem)] = value
                self.steps.append(lambda e, s=sem, v=value: e.wait_ge(s, v))

    def last(self):
        return (self.sem, self.count) if self.count else None

    def put(self, make, *after, signal=True):
        self.wait(*after)
        if not signal:
            self.steps.append(lambda e: make())
            return None
        self.count += 1
        self.steps.append(lambda e, s=self.sem: make().then_inc(s, 1))
        return self.sem, self.count

    def dma(self, out, in_, sem, *after):
        self.wait(*after)
        self.steps.append(lambda e: e.dma_start(out, in_).then_inc(sem, 16))

    def run(self, engine):
        for step in self.steps:
            step(engine)

    def enter(self, sem):
        self.outside = self.sem, self.count, self.steps, self.seen
        self.sem, self.count, self.steps, self.seen = sem, 0, [], dict(self.seen)

    def leave(self, flag, written):
        inside = self.steps
        self.sem, self.count, self.steps, self.seen = self.outside
        self.wait(written)

        def branch(e):
            with e.If(e.value_load(flag) > 0):
                for step in inside:
                    step(e)
        self.steps.append(branch)


class Bank:

    def __init__(self, tensor):
        self.t, self.free = tensor, []


class Slot:

    def __init__(self, tensor, sem):
        self.t, self.sem, self.count, self.free, self.held = tensor, sem, 0, [], False


def build(nc, a, out):
    ctx = ExitStack()
    with ctx:
        def sb(name, shape, dt=F32):
            return ctx.enter_context(nc.sbuf_tensor(name, shape, dt))

        def sem(name):
            return ctx.enter_context(nc.semaphore(name))

        slots = [Slot(sb(f"weights{i}", [P, SLOT]), sem(f"weights{i}_in")) for i in range(SLOTS)]
        x = sb("x", [P, TT, D])
        gates_row = sb("gates_row", [P, 2, D])
        affine = sb("affine", [P, 7, 2, KD])
        norm_w = sb("norm_w", [P, 6, KD])
        router_in = sb("router_in", [P, 2, 336])
        h_rows = sb("h_rows", [P, TT, D])
        h_cols = sb("h_cols", [P, KD, TOKENS])
        filter_out = sb("filter_out", [P, 1536])
        work = sb("work", [P, WORK])
        spare = sb("spare", [P, SPARE])
        c_rep = sb("c_rep", [P, 2, KD, 32])
        ident = sb("ident", [P, P])
        ones = sb("ones", [P, P])
        before = sb("before", [P, P])
        places = sb("places", [P, PLACES])
        resets = sb("resets", [P, 2 * 64])
        overflow = sb("overflow", [P, 8], I32)
        small = sb("small", [P, 384])
        banks = [Bank(ctx.enter_context(nc.psum_tensor(f"bank{i}", [P, BANK], F32))) for i in range(8)]

        tensor, vector, scalar, pool, sync = (Lane(sem(n)) for n in (
            "tensor_done", "vector_done", "scalar_done", "pool_done", "sync_done"))
        lanes = ((tensor, "tensor"), (vector, "vector"), (scalar, "scalar"), (pool, "pool"), (sync, "sync"))

        def dve(make, *after, chain=True):
            return vector.put(make, vector.last() if chain else None, *after)

        def act(make, *after, chain=True):
            return scalar.put(make, scalar.last() if chain else None, *after)

        def mms(out_ap, pairs, *after, start=True, stop=True, signal=True, loose=False):
            tensor.wait(*after)
            tok = None
            for i, (l, r) in enumerate(pairs):
                end = i == len(pairs) - 1
                tok = tensor.put(
                    lambda l=l, r=r, s=start and i == 0, e=stop and end: nc.tensor.matmul(
                        out_ap, l, r, start=s, stop=e, skip_group_check=loose),
                    signal=end and signal)
            return tok

        def turn(out_ap, in_ap, *after, signal=True):
            n = in_ap.shape[0]
            return tensor.put(lambda: nc.tensor.transpose(out_ap, in_ap, ident[0:n, 0:n]), *after, signal=signal)

        def a_fn(out_ap, in_ap, func, *after, chain=True, **kw):
            return act(lambda: nc.scalar.activation(out_ap, in_ap, func, **kw), *after, chain=chain)

        def v_copy(out_ap, in_ap, *after, chain=True):
            return dve(lambda: nc.vector.tensor_copy(out_ap, in_ap), *after, chain=chain)

        def v_tt(out_ap, p, q, op, *after, chain=True):
            return dve(lambda: nc.vector.tensor_tensor(out_ap, p, q, op), *after, chain=chain)

        def pool_tt(out_ap, p, q, op, *after):
            return pool.put(lambda: nc.gpsimd.tensor_tensor(out_ap, p, q, op), pool.last(), *after)

        def v_ts(out_ap, p, s1, s2, op0, op1, *after, chain=True):
            if s2 is None:
                return dve(lambda: nc.vector.tensor_scalar(out_ap, p, s1, None, op0), *after, chain=chain)
            return dve(lambda: nc.vector.tensor_scalar(out_ap, p, s1, s2, op0, op1), *after, chain=chain)

        def v_stt(out_ap, p, s, q, op0, op1, *after, chain=True):
            return dve(lambda: nc.vector.scalar_tensor_tensor(out=out_ap, in0=p, scalar=s, in1=q, op0=op0, op1=op1),
                       *after, chain=chain)

        def v_recip(out_ap, in_ap, *after):
            return dve(lambda: nc.vector.reciprocal(out_ap, in_ap), *after)

        def v_sum(out_ap, in_ap, *after):
            return dve(lambda: nc.vector.reduce_sum(out_ap, in_ap, AX), *after)

        def v_max(out_ap, in_ap, *after):
            return dve(lambda: nc.vector.reduce_max(out_ap, in_ap, AX), *after)

        bank_at = [0]

        def next_bank():
            b = banks[bank_at[0] % 7]
            bank_at[0] += 1
            return b

        slot_at = [0]

        def load(*pieces):
            while slots[slot_at[0] % SLOTS].held:
                slot_at[0] += 1
            s = slots[slot_at[0] % SLOTS]
            slot_at[0] += 1
            for view, src in pieces:
                s.count += 16
                sync.dma(view(s.t), src, s.sem, *s.free)
            s.free = []
            return s, (s.sem, s.count)

        def side_load(name, pieces, *after, lane=None):
            s = sem(name + "_in")
            for dst, src in pieces:
                (lane or pool).dma(dst, src, s, *after)
            return s, 16 * len(pieces)

        def cut(at, *dims):
            n = int(np.prod(dims))
            assert at + n <= WORK, (at, n)
            v = work[:, at:at + n]
            if len(dims) == 1:
                return v
            if len(dims) == 2:
                return v.rearrange("p (a b) -> p a b", a=dims[0])
            if len(dims) == 3:
                return v.rearrange("p (a b c) -> p a b c", a=dims[0], b=dims[1])
            return v.rearrange("p (a b c d) -> p a b c d", a=dims[0], b=dims[1], c=dims[2])

        def everyone():
            return [l.last() for l in (tensor, vector, scalar, pool)]

        got_ident = side_load("ident", [(ident[:, :], a["k_ident"])], lane=sync)
        vector.wait(got_ident)
        made_ones = vector.put(lambda: nc.vector.memset(ones[:, :], 1.0))
        tensor.wait(got_ident, made_ones)

        def rstd(dst, ssum, width, *after):
            t = v_ts(ssum, ssum, 1.0 / width, EPS, ALU.mult, ALU.add, *after)
            t = a_fn(ssum, ssum, ACT.Sqrt, t)
            return v_recip(dst, ssum, t)

        def head_norm(src, dst, groups, width, weight, sq, stat, *after):
            t = v_tt(sq, src, src, ALU.mult, *after)
            t = v_sum(stat, sq, t)
            t = rstd(stat, stat, width, t)
            t = v_tt(dst, src, stat.unsqueeze(2).to_broadcast([P, groups, width]), ALU.mult, t)
            if weight is not None:
                t = v_tt(dst, dst, weight, ALU.mult, t)
            return t

        def modulation(rep, w, b_row, stored, groups, name, first_norm, *after):
            wv = w.rearrange("(p k) n -> p k n", k=KD)
            four = 4 * BANK
            for g in groups:
                cols = slice(g * four, (g + 1) * four)
                bias, tmp = (spare[:, j * BANK:(j + 1) * BANK] for j in range(2))
                got_b = side_load(f"{name}_b{g}", [
                    (bias[32 * j:32 * j + 32, :], b_row[g * four + j * BANK:g * four + (j + 1) * BANK].partition_broadcast(32))
                    for j in range(4)], *after, *spare_free[0])
                b = mod_bank
                for k0 in range(0, KD, 2):
                    s, got = load((lambda v: v[:, :].rearrange("p (k n) -> p k n", k=2), wv[:, k0:k0 + 2, cols]))
                    ws = s.t[:, :].rearrange("p (k n) -> p k n", k=2)
                    for k in range(2):
                        for j in range(4):
                            m = mms(b.t[32 * j:32 * j + 32, :], [(rep[:, k0 + k, :], ws[:, k, j * BANK:(j + 1) * BANK])],
                                    got, *after, *b.free, start=k0 + k == 0, stop=k0 + k == KD - 1, loose=True,
                                    signal=k == 1 and j == 3)
                    s.free = [m]
                    if k0 < KD - 2:
                        yield
                t = v_tt(tmp, b.t[:, :], bias, ALU.add, m, got_b)
                b.free = [t]
                done = sem(f"{name}_stored{g}")
                pool.dma(stored[cols].rearrange("(j n) -> j n", j=4), tmp[0:P:32, :], done, t)
                spare_free[0] = [(done, 16)]
                mod_stored[name, g] = (done, 16)
                yield
            affine_load(name, first_norm, stored)

        def affine_load(name, first_norm, stored):
            toks = [mod_stored[name, g] for g in range(3) if (name, g) in mod_stored]
            for n, part in ((0, 0), (1, 3)) if (name, 0) in mod_stored else ((1, 3),):
                got_affine[first_norm + n] = side_load(f"{name}_norm{n}", [
                    (affine[:, first_norm + n], stored[part * D:(part + 2) * D].rearrange("(a p k) -> p a k", a=2, k=KD))],
                    *toks)

        def fold(n):
            return v_stt(affine[:, n, 1], affine[:, n, 1], 1.0, norm_w[:, n], ALU.add, ALU.mult, got_affine[n], got_norms)

        def filters(room, *after):
            W = D // 4
            at = lambda o, *d: spare[:, o:o + int(np.prod(d))].rearrange("p (a b) -> p a b", a=d[0]) if len(d) > 1 \
                else spare[:, o:o + d[0]]
            hidden, turns, f_small = at(0, TOKENS), at(256, TOKENS), at(512, 208)
            hf, hb, ab = at(720, TT, W), at(1232, TT, W), at(1744, TT, W)
            norm_r, imag, nyquist = at(2256, W), at(2512, TT, W), at(3024, W)[0:1, :]
            real = filter_out[:, 0:2 * W].rearrange("p (i c) -> p i c", i=TT)
            skips = [filter_out[0:1, 512 * j:512 * j + 512].rearrange("p (o c) -> p o c", o=2) for j in (1, 2)]
            last_w = room[:, 0:2048]
            ahead = room[:, 2048:3072].rearrange("p (k f) -> p k f", k=TT)
            decays = [room[:, 3072 + 512 * j:3584 + 512 * j].rearrange("p (k d) -> p k d", k=TT) for j in range(2)]
            ahead_in, decay_in = a["k_fourier"][:, 0:1024], a["k_fourier"][:, 2048:4096]
            got = side_load("filters", [
                (f_small[0:33, 0:64], a["hy_f_w1_2"][0]), (f_small[0:64, 64:128], a["hy_f_w2_2"][0]),
                (f_small[0:64, 128:192], a["hy_f_w3_2"][0]), (f_small[0:64, 192:198], a["hy_f_cols"]),
                (f_small[64:P, 192:198], a["hy_f_cols"]), (turns[0:33, :], a["k_feats"])], *after, *spare_free[0])
            got_last = side_load("filters_last", [(last_w[64 * o:64 * o + 64, :], a["hy_f_w4_2"][0][:, 2048 * o:2048 * o + 2048])
                                                  for o in range(2)] + [(ahead.rearrange("p k f -> p (k f)"), ahead_in)], *after)

            def quarter_load(q, *after_):
                cols = slice(q * W, (q + 1) * W)
                return side_load(f"quarter{q}", [
                    (decays[q % 2], decay_in.rearrange("p (k d) -> p k d", k=TT)[:, :, cols]),
                    (skips[q % 2], a["hy_filt_bias_2"][0][:, cols].unsqueeze(0))], *after, *after_)

            got_quarter = {q: quarter_load(q) for q in range(2)}
            b = mod_bank
            for _ in range(6):
                yield
            layers = ((f_small[0:33, 0:64], turns[0:33, :]), (f_small[0:64, 64:128], hidden[0:64, :]),
                      (f_small[0:64, 128:192], hidden[0:64, :]))
            t = None
            for l, (w_l, src) in enumerate(layers):
                for half in range(2):
                    m = mms(b.t[64 * half:64 * half + 64, 0:TOKENS], [(w_l, src)], got, t, *b.free, loose=True)
                t = v_ts(hidden, b.t[:, 0:TOKENS], f_small[:, 192 + 2 * l:193 + 2 * l],
                         f_small[:, 193 + 2 * l:194 + 2 * l], ALU.add, ALU.mult, m, *after)
                b.free = [t]
                v_ts(turns, hidden, float(1 / (2 * np.pi)), ROUND, ALU.mult, ALU.add)
                v_ts(turns, turns, -ROUND, None, ALU.add, None)
                v_stt(hidden, turns, -TWO_PI_1, hidden, ALU.mult, ALU.add)
                v_stt(hidden, turns, -TWO_PI_2, hidden, ALU.mult, ALU.add)
                v_stt(hidden, turns, -TWO_PI_3, hidden, ALU.mult, ALU.add)
                t = v_ts(hidden, hidden, PI_IN, -PI_IN, ALU.min, ALU.max)
                t = a_fn(hidden, hidden, ACT.Sin, t)
                yield
            t_hidden = t
            real_stored = imag_stored = nyquist_stored = m = None
            for q in range(4):
                cols = slice(q * W, (q + 1) * W)
                decay, skip = decays[q % 2], skips[q % 2]
                for o in range(2):
                    half = slice(64 * o, 64 * o + 64)
                    for side, dst in ((0, hf), (1, hb)):
                        c0 = side * D + q * W
                        for i in range(TT):
                            m = mms(b.t[:, i * W:(i + 1) * W],
                                    [(hidden[half, i * P:(i + 1) * P], last_w[half, c0:c0 + W])],
                                    got_last, t_hidden, *b.free)
                        t = v_tt(dst, b.t[:, :].rearrange("p (i c) -> p i c", i=TT), decay, ALU.mult,
                                 m, got_quarter[q])
                        b.free = [t]
                        t = a_fn(ab, dst, ACT.Abs, t, m, chain=False)
                        yield
                        m = mms(b.t[:, 0:W], [(ones[:, :], ab[:, i, :]) for i in range(TT)], t, *b.free)
                        t = v_ts(norm_r, b.t[:, 0:W], EPS, None, ALU.add, None, m)
                        b.free = [t]
                        v_recip(norm_r, norm_r)
                        t = v_tt(dst, dst, norm_r.unsqueeze(1).to_broadcast([P, TT, W]), ALU.mult)
                        yield
                    v_tt(hf[0:1, 0, :], hf[0:1, 0, :], skip[:, o, :], ALU.add)
                    dve(lambda: nc.vector.memset(hb[0:1, 0, :], 0.0))
                    v_tt(ab, hf, hb, ALU.add, m)
                    t = v_tt(hf, hf, hb, ALU.subtract)
                    if o == 1 and q < 2:
                        got_quarter[q + 2] = quarter_load(q + 2, t)
                    yield
                    for ft in range(TT):
                        m = mms(b.t[:, ft * W:(ft + 1) * W],
                                [(ahead[:, i, ft * P:(ft + 1) * P], ab[:, i, :]) for i in range(TT)], t, *b.free)
                    t = v_copy(real, b.t[:, :].rearrange("p (i c) -> p i c", i=TT), m, real_stored)
                    b.free = [t]
                    done = sem(f"real{o}{q}")
                    pool.dma(spectra["real"][o][:, :, cols], real, done, t)
                    real_stored = (done, 16)
                    yield
                    for ft in range(TT):
                        m = mms(b.t[:, ft * W:(ft + 1) * W],
                                [(ahead[:, i, TOKENS + ft * P:TOKENS + (ft + 1) * P], hf[:, i, :]) for i in range(TT)],
                                t, *b.free)
                    v_copy(imag, b.t[:, :].rearrange("p (i c) -> p i c", i=TT), m, imag_stored)
                    t = dve(lambda: nc.vector.memset(imag[0:1, 0, :], 0.0))
                    b.free = [t]
                    done_i = sem(f"imag{o}{q}")
                    pool.dma(spectra["imag"][o][:, :, cols], imag, done_i, t)
                    imag_stored = (done_i, 16)
                    yield
                    m = mms(b.t[0:1, 0:W], [(ahead[:, i, TOKENS:TOKENS + 1], ab[:, i, :]) for i in range(TT)], t, *b.free)
                    t = v_copy(nyquist, b.t[0:1, 0:W], m, nyquist_stored)
                    b.free = [t]
                    done_n = sem(f"nyquist{o}{q}")
                    pool.dma(spectra["nyquist"][o][:, cols], nyquist, done_n, t)
                    nyquist_stored = (done_n, 16)
                    spectrum_stored[o, q] = [real_stored, imag_stored, nyquist_stored]
                    if o == 1 and q == 3:
                        spare_free[0] = spectrum_stored[o, q]
                    yield

        spectra = {n: nc.dram_tensor("filter_" + n, shape, F32, kind="Internal").ap() for n, shape in (
            ("real", (2, P, TT, D)), ("imag", (2, P, TT, D)), ("nyquist", (2, 1, D)))}
        spectrum_stored = {}

        def gate_load(name, stored, half, *after):
            part = 3 * half + 2
            return side_load(f"{name}_gate{half}", [(gates_row[:, half, :], stored[part * D:(part + 1) * D].partition_broadcast(P))],
                             mod_stored[name, part // 2], *after)

        ws_t = spare[:, 1024:1536].rearrange("p (h t) -> p h t", h=A_HEADS)
        bs_cols = spare[:, 1536:1540]
        axial = spare[:, 1540:1796].rearrange("p (i c d) -> p i c d", i=TT, c=2)
        qk_w = spare[:, 1796:2436].rearrange("p (h d) -> p h d", h=10)
        w_c = spare[:, 2436:2692].rearrange("p (h d) -> p h d", h=C_HEADS)
        lb_logits = spare[:, 2692:3204].rearrange("p (a b) -> p a b", a=2)
        latent = spare[:, 3292:4096]
        w_cq, w_ckv, w_qn, w_kn = latent[:, 0:2], latent[:, 2:3], latent[:, 3:4], latent[:, 4:5]

        got_affine = {}
        mod_stored, spare_free, mod_bank = {}, [[]], banks[7]
        background = []

        def step():
            while background:
                try:
                    next(background[0])
                    return
                except StopIteration:
                    background.pop(0)

        def finish():
            while background:
                step()

        half_sums = small[:, 376:380]
        idle = small[:, 383:384]

        def load_sqrt():
            a_fn(idle, ones[:, 0:1], ACT.Sqrt, chain=False)

        def normalize(*after, halves=()):
            ss = small[:, 0:TT]
            if not halves:
                load_sqrt()
            if halves:
                t = v_sum(ss, half_sums.rearrange("p (i c) -> p i c", i=TT), *halves)
            else:
                t = [a_fn(h_rows[:, i, :], x[:, i, :], ACT.Square, *after, accum_out=ss[:, i:i + 1], chain=False)
                     for i in range(TT)][-1]
            t = rstd(small[:, 4:4 + TT], ss, D, t)
            return [v_ts(h_rows[:, 0, :], x[:, 0, :], small[:, 4:5], None, ALU.mult, None, t, *after),
                    a_fn(h_rows[:, 1, :], x[:, 1, :], ACT.Copy, t, *after, scale=small[:, 5:6])]

        def scaled_out(dst, src, n, k, *after):
            scale, shift = affine[:, n, 1, k:k + 1], affine[:, n, 0, k:k + 1]
            if k // 2 % 2:
                return v_ts(dst, src, scale, shift, ALU.mult, ALU.add, *after, chain=False)
            return a_fn(dst, src, ACT.Identity, *after, scale=scale, bias=shift, chain=False)

        def normed_cols(rows_, dst, n, *after, follow=None):
            toks = []
            for k0 in range(0, KD, 2):
                b = next_bank()
                bv = b.t[:, :].rearrange("p (k t) -> p k t", k=2)
                for k in range(2):
                    for i in range(TT):
                        m = turn(bv[:, k, i * P:(i + 1) * P], by_feature(rows_, i, k0 + k), *after, *b.free)
                b.free = [scaled_out(dst[:, k0 + k, :], bv[:, k, :], n, k0 + k, m, *after) for k in range(2)]
                toks += b.free
                if follow and k0 >= 2:
                    follow(k0 - 2, toks[-3])
            if follow:
                follow(KD - 2, toks[-1])
            return toks

        def rows_to_cols(piece, dst, n, *after, weight=None):
            toks = []
            for k0 in range(0, n, 2):
                b = next_bank()
                bv = b.t[:, :].rearrange("p (k t) -> p k t", k=2)
                m = None
                for k in range(k0, min(k0 + 2, n)):
                    for i in range(TT):
                        m = turn(bv[:, k - k0, i * P:(i + 1) * P], piece(i, k), *after, *b.free)
                kk = min(2, n - k0)
                if weight:
                    for k in range(kk):
                        args = (dst[:, k0 + k, :], bv[:, k, :])
                        if (k0 // 2) % 2:
                            b.free = [v_ts(*args, weight(k0 + k), None, ALU.mult, None, m, *after, chain=False)]
                        else:
                            b.free = [a_fn(*args, ACT.Copy, m, *after, scale=weight(k0 + k), chain=False)]
                elif (k0 // 2) % 2:
                    b.free = [v_copy(dst[:, k0:k0 + kk, :], bv[:, 0:kk, :], m, *after, chain=False)]
                else:
                    b.free = [a_fn(dst[:, k0:k0 + kk, :], bv[:, 0:kk, :], ACT.Copy, m, *after, chain=False)]
                toks += b.free
            return toks

        def by_feature(rows_, i, k):
            return rows_[:, i, :].rearrange("p (f k) -> p k f", k=KD)[:, k, :]

        def load_columns(n_k, view, c0, n):
            s, got = load((lambda v: v[:, 0:n_k * n].rearrange("p (k n) -> p k n", k=n_k), view[:, :, c0:c0 + n]))
            return s, got, s.t[:, 0:n_k * n].rearrange("p (k n) -> p k n", k=n_k)

        def product_rows(cols, n_k, weight, w_view, width, put, *after, loaded=None):
            per_slot = SLOT // n_k
            for start in range(0, width, per_slot):
                wide = min(per_slot, width - start)
                s, got, ws = loaded or load_columns(n_k, w_view(weight), start, wide)
                for c0 in range(0, wide, BANK):
                    n = min(BANK, wide - c0)
                    for i in range(TT):
                        b = next_bank()
                        m = mms(b.t[:, 0:n], [(cols[:, k, i * P:(i + 1) * P], ws[:, k, c0:c0 + n]) for k in range(n_k)],
                                got, *after, *b.free)
                        b.free = [put(i, start + c0, n, b, m)]
                s.free = [m]
                step()
            return [b.free[0], m]

        by_p = lambda w: w.rearrange("(p k) n -> p k n", k=KD)
        by_k = lambda w: w.rearrange("(k p) n -> p k n", p=P)

        squared = {}

        def residual(gate, sums=True):
            if sums:
                load_sqrt()

            def put(i, c0, n, b, m):
                tmp = h_rows[:, i, c0:c0 + n]
                t = v_tt(tmp, b.t[:, 0:n], gate[:, c0:c0 + n], ALU.mult, m)
                free = t
                t = v_tt(x[:, i, c0:c0 + n], x[:, i, c0:c0 + n], tmp, ALU.add, t)
                at = 2 * i + c0 // BANK
                if sums:
                    squared[at] = a_fn(tmp, x[:, i, c0:c0 + n], ACT.Square, t, accum_out=half_sums[:, at:at + 1], chain=False)
                return free
            return put

        router = []

        def route_load(name, w, bias, place, *after):
            n = w.shape[1]
            wv = router_in[:, place, 0:KD * n].rearrange("p (k n) -> p k n", k=KD)
            bv = router_in[:, place, KD * n:KD * n + n]
            got = side_load(name + "_route", [(wv, by_p(w)), (bv, bias.partition_broadcast(P))], *after)
            router.append((wv, bv, got))

        logit_sums = []

        def route_products():
            route_w, route_b, got = router.pop(0)
            n = route_b.shape[1]
            bs = [next_bank() for _ in range(TT)]

            def part(k0, t_cols):
                m = [mms(b.t[:, 0:n], [(h_cols[:, k, i * P:(i + 1) * P], route_w[:, k, :]) for k in (k0, k0 + 1)],
                         got, t_cols, *b.free, start=k0 == 0, stop=k0 == KD - 2) for i, b in enumerate(bs)]
                if k0 == KD - 2:
                    logit_sums.append((route_b, list(zip(bs, m))))
            return part

        def route(logits, n_grp, per, comb, chosen, at, *after):
            n_exp = n_grp * per
            g, e = logits[:, :, 0:n_grp], logits[:, :, n_grp:n_grp + n_exp]
            s = lambda o, n: small[:, at + o:at + o + n]
            gmax, ex, gsum, picked = s(0, TT), s(8, TT * n_grp), s(16, TT), s(24, TT * n_grp)
            masked, hot1, hot2, top = s(40, TT * n_exp), s(104, TT * n_exp), s(168, TT * n_exp), s(232, 16)
            cnt = s(250, TT * n_exp)
            v3 = lambda ap, n: ap.rearrange("p (i n) -> p i n", i=TT)
            bc = lambda ap, n: ap.unsqueeze(2).to_broadcast([P, TT, n])

            def first_of(hot, values, best, n, t):
                at_ = {4: 0, 16: 8, 32: 40}[n]
                t = v_tt(v3(hot, n), values, bc(best, n), ALU.is_equal, t)
                c = cnt[:, 0:TT * n]
                t = dve(lambda: nc.vector.tensor_tensor_scan(c, resets[:, at_:at_ + TT * n], hot, 0.0, ALU.mult, ALU.add), t)
                return v_stt(hot, c, 1.0, hot, ALU.is_equal, ALU.mult, t)

            t = t_gmax = v_max(gmax, g, *after)
            t = first_of(picked, g, gmax, n_grp, t)
            t = v_ts(picked, picked, BIG, -BIG, ALU.mult, ALU.add, t)
            four = lambda ap: ap.rearrange("p i (a b) -> p i a b", a=n_grp)
            t = v_tt(four(v3(masked, n_exp)), four(e),
                     v3(picked, n_grp).unsqueeze(3).to_broadcast([P, TT, n_grp, per]), ALU.add, t)
            m1, m2, w1, w2 = top[:, 0:2], top[:, 2:4], top[:, 4:6], top[:, 6:8]
            t = v_max(m1, v3(masked, n_exp), t)
            t = first_of(hot1, v3(masked, n_exp), m1, n_exp, t)
            t = v_stt(masked, hot1, -2 * BIG, masked, ALU.mult, ALU.add, t)
            t = v_max(m2, v3(masked, n_exp), t)
            t = first_of(hot2, v3(masked, n_exp), m2, n_exp, t)
            t_chosen = v_tt(chosen.rearrange("p i n -> p (i n)"), hot1, hot2, ALU.add, t)

            def weights():
                t = v_tt(v3(ex, n_grp), g, bc(gmax, n_grp), ALU.subtract, t_gmax)
                v_tt(w2, m2, m1, ALU.subtract)
                t = a_fn(ex, ex, ACT.Exp, vector.last())
                t = a_fn(w2, w2, ACT.Exp, t)
                v_sum(gsum, v3(ex, n_grp), t)
                v_recip(gsum, gsum)
                v_ts(w1, w2, 1.0, None, ALU.add, None)
                v_recip(w1, w1)
                v_tt(w1, w1, gsum, ALU.mult)
                v_tt(w2, w2, w1, ALU.mult)
                for i in range(TT):
                    c = comb[:, i, 0:n_exp]
                    v_ts(c, v3(hot1, n_exp)[:, i, :], w1[:, i:i + 1], None, ALU.mult, None)
                    t = v_stt(c, v3(hot2, n_exp)[:, i, :], w2[:, i:i + 1], c, ALU.mult, ALU.add)
                return t
            return t_chosen, weights

        def experts(layer, norm, n_grp, per, ff, gate_w, up_w, down_w, got_gate, *after):
            n_exp, n_ft = n_grp * per, ff // P
            logits, comb = cut(440, TT, n_grp + n_exp), cut(520, TT, n_exp)
            chosen, place, beyond = cut(600, TT, n_exp), cut(680, TT, n_exp), cut(760, TT, n_exp)
            route_b, sums_of = logit_sums.pop()
            for i, (b, m) in enumerate(sums_of):
                t = v_tt(logits[:, i, :], b.t[:, 0:n_grp + n_exp], route_b, ALU.add, m, *after)
                b.free = [t]
            t, weights = route(logits, n_grp, per, comb, chosen, 32, t)

            b = next_bank()
            for i in range(TT):
                pairs = [(before[:, :], chosen[:, i, :])] + ([(ones[:, :], chosen[:, 0, :])] if i else [])
                m = mms(b.t[:, i * n_exp:(i + 1) * n_exp], pairs, t, *b.free)
            bv = b.t[:, 0:TT * n_exp].rearrange("p (i n) -> p i n", i=TT)
            t_route = v_stt(place, chosen, -1000.0, bv, ALU.mult, ALU.add, m)
            b.free = [t_route]

            def overflows():
                v_ts(beyond, place, float(PLACES - 1000), None, ALU.is_ge, None)
                v_tt(beyond, beyond, chosen, ALU.mult)
                n_over = small[:, 0:1]
                t = v_sum(n_over, beyond.rearrange("p i n -> p (i n)"))
                b = next_bank()
                m = mms(b.t[:, 0:1], [(ones[:, :], n_over)], t, *b.free)
                t_flag = v_copy(overflow[:, 0:1], b.t[:, 0:1], m)
                b.free = [t_flag]
                v_tt(beyond, beyond, comb, ALU.mult)
                return t_flag

            hot = [cut(1000 + 512 * j, TT, 4, PLACES) for j in range(2)]
            hot_w = [cut(2024 + 512 * j, TT, 4, PLACES) for j in range(2)]
            picked = [cut(3048 + 2048 * j, KD, 4 * PLACES) for j in range(2)]
            scatter = [cut(7144 + 256 * j, TT, P) for j in range(2)]
            gated = [cut(7656 + 512 * j, ff) for j in range(2)]
            act_cols = [cut(8680 + 512 * j, n_ft, P) for j in range(2)]
            y_rows = [cut(9704 + D * j, D) for j in range(2)]
            hot_free, picked_free, scatter_free = [None] * 2, [[]] * 2, [None] * 2
            act_free, y_free = [None] * 2, [None] * 2
            tokens, weighed = {}, {}

            def choose(q):
                j, es = q % 2, slice(4 * q, 4 * q + 4)
                shape = [P, 4, PLACES]
                for i in range(TT):
                    t = v_tt(hot[j][:, i], place[:, i, es].unsqueeze(2).to_broadcast(shape),
                             places[:, :].unsqueeze(1).to_broadcast(shape), ALU.is_equal,
                             t_route, hot_free[j], chain=False)
                tokens[q] = t
                if q == 0:
                    gather(0)
                    weights()
                for i in range(TT):
                    tw = v_tt(hot_w[j][:, i], hot[j][:, i], comb[:, i, es].unsqueeze(2).to_broadcast(shape),
                              ALU.mult, t, vector.last() if q == 0 else None, chain=False)
                weighed[q] = tw

            def gather(q):
                j, toks = q % 2, []
                t = tokens[q]
                for k0 in range(0, KD, 2):
                    b = next_bank()
                    for k in range(2):
                        m = mms(b.t[:, k * 256:(k + 1) * 256],
                                [(by_feature(h_rows, i, k0 + k), hot[j][:, i].rearrange("p e s -> p (e s)")) for i in range(TT)],
                                t, *b.free)
                    b.free = [scaled_out(picked[j][:, k0 + k, :], b.t[:, k * 256:(k + 1) * 256], norm, k0 + k, m,
                                         *picked_free[j]) for k in range(2)]
                    toks += b.free
                tokens[q] = toks

            def take_pair(pr):
                if pr % 2 and pr + 1 < n_exp // 2:
                    choose(pr // 2 + 1)
                q, j, e0 = pr // 2, pr % 2, 2 * pr
                toks, tw = tokens[q], weighed[q]
                off = (pr % 2) * 2
                halves = [slice(0, 64), slice(64, 128)]
                cols = [picked[q % 2][:, :, (off + c) * PLACES:(off + c + 1) * PLACES] for c in range(2)]
                if n_ft == 4:
                    g_slots = [load((lambda v: v[:, :], gate_w[e0 + c].rearrange("(p k) f -> p (k f)", k=KD)))
                               for c in range(2)]
                    u_slots = [load((lambda v: v[:, :], up_w[e0 + c].rearrange("(p k) f -> p (k f)", k=KD)))
                               for c in range(2)]
                    parts = [(g_slots, ff), (u_slots, ff)]
                else:
                    both = lambda v: v[:, :].rearrange("p (k s f) -> p k s f", k=KD, s=2)
                    parts = [([load((lambda v: both(v)[:, :, 0, :], by_p(gate_w[e0 + c])),
                                    (lambda v: both(v)[:, :, 1, :], by_p(up_w[e0 + c]))) for c in range(2)], 2 * ff)]
                results = []
                for slots_, width in parts:
                    b = next_bank()
                    for k in range(KD):
                        for c, (s, got_s) in enumerate(slots_):
                            w = s.t[:, :].rearrange("p (k f) -> p k f", k=KD)[:, k, :]
                            m = mms(b.t[halves[c], 0:width], [(cols[c][:, k, :], w)], got_s, *toks, *b.free,
                                    start=k == 0, stop=k == KD - 1, loose=True, signal=k == KD - 1 and c == 1)
                    for s, _ in slots_:
                        s.free = [m]
                    results.append((b, m))
                if n_ft == 4:
                    (bg_, mg), (bu, mu) = results
                    g_ps, u_ps = bg_.t[:, 0:ff], bu.t[:, 0:ff]
                else:
                    (bg_, mg), = results
                    bu, mu = bg_, mg
                    g_ps, u_ps = bg_.t[:, 0:ff], bg_.t[:, ff:2 * ff]
                g = gated[j]
                t1 = a_fn(g, g_ps, ACT.Silu, mg, act_free[j], chain=False)
                t2 = v_tt(g, u_ps, g, ALU.mult, t1, mu, chain=False)
                bg_.free = [t2]
                bu.free = [t2]
                step()
                if put_back:
                    put_back.pop()()
                step()
                if pr % 2:
                    picked_free[q % 2] = [mu]
                    if pr + 1 < n_exp // 2:
                        gather(pr // 2 + 1)
                down_slots = []
                if n_ft == 4:
                    down_slots = [load((lambda v: v[:, :].rearrange("p (k n) -> p k n", k=4), by_k(down_w[e0 + c])))
                                  for c in range(2)]
                    wd = [s.t[:, :].rearrange("p (k n) -> p k n", k=4) for s, _ in down_slots]
                else:
                    d = load(*[(lambda v, c=c: v[:, c * 2048:(c + 1) * 2048].rearrange("p (k n) -> p k n", k=2),
                                by_k(down_w[e0 + c])) for c in range(2)])
                    down_slots = [d, d]
                    wd = [d[0].t[:, c * 2048:(c + 1) * 2048].rearrange("p (k n) -> p k n", k=2) for c in range(2)]
                b = next_bank()
                for i in range(TT):
                    m = turn(b.t[:, i * P:(i + 1) * P],
                             hot_w[q % 2][:, i, off:off + 2, :].rearrange("p e s -> p (e s)"), tw, *b.free)
                if pr % 2:
                    hot_free[q % 2] = m
                ts = a_fn(scatter[j], b.t[:, 0:TOKENS].rearrange("p (i t) -> p i t", i=TT), ACT.Copy, m,
                          scatter_free[j], chain=False)
                b.free = [ts]
                step()
                b = next_bank()
                for ft in range(n_ft):
                    m = turn(b.t[:, ft * P:(ft + 1) * P], g[:, ft * P:(ft + 1) * P], t2, *b.free)
                act_free[j] = m
                ta = a_fn(act_cols[j], b.t[:, 0:ff].rearrange("p (k s) -> p k s", k=n_ft), ACT.Copy, m, chain=False)
                b.free = [ta]
                step()
                for half in range(2):
                    b = next_bank()
                    hs = slice(half * BANK, (half + 1) * BANK)
                    for ft in range(n_ft):
                        for c in range(2):
                            m = mms(b.t[halves[c], :], [(act_cols[j][:, ft, halves[c]], wd[c][:, ft, hs])],
                                    ta, down_slots[c][1], *b.free, start=ft == 0, stop=ft == n_ft - 1, loose=True,
                                    signal=ft == n_ft - 1 and c == 1)
                    ty = v_tt(y_rows[j][:, hs], b.t[:, :], gates_row[:, 1, hs], ALU.mult, m, y_free[j], got_gate, chain=False)
                    b.free = [ty]
                for s, _ in down_slots:
                    s.free = [m]
                step()

                def back():
                    for half in range(2):
                        hs = slice(half * BANK, (half + 1) * BANK)
                        for i in range(TT):
                            b = next_bank()
                            m = mms(b.t[:, :], [(scatter[j][:, i, :], y_rows[j][:, hs])], ts, ty, *b.free)
                            b.free = [v_tt(x[:, i, hs], x[:, i, hs], b.t[:, :], ALU.add, m, x_last.get((i, half)),
                                           chain=False)]
                            x_last[i, half] = b.free[0]
                    y_free[j] = scatter_free[j] = m
                put_back.append(back)

            x_last, put_back = {}, []
            choose(0)
            for pr in range(n_exp // 2):
                take_pair(pr)
                if pr == 0:
                    t_flag = overflows()
            put_back.pop()()
            finish()

            before_branch = everyone()
            kept = [(s, s.sem, s.count, s.free) for s in slots], [(b, b.free) for b in banks], slot_at[0], bank_at[0]
            for lane, n in lanes:
                lane.enter(sem(f"{layer}_rest_{n}"))
            for i, s in enumerate(slots):
                s.sem, s.count = sem(f"{layer}_rest_weights{i}"), 0
            for lane, _ in lanes:
                lane.wait(*before_branch)
            experts_for_all(n_exp, n_ft, gate_w, up_w, down_w, beyond)
            ends = everyone()
            for lane, _ in lanes:
                lane.wait(*ends)
            for lane, _ in lanes:
                lane.leave(overflow[0:1, 0:1], t_flag)
            for s, sem_, count, free in kept[0]:
                s.sem, s.count, s.free = sem_, count, free
            for b, free in kept[1]:
                b.free = free
            slot_at[0], bank_at[0] = kept[2], kept[3]
            return vector.last()

        def experts_for_all(n_exp, n_ft, gate_w, up_w, down_w, comb):
            t = None
            diag = [cut(1000 + 256 * j, TT, P) for j in range(2)]
            spread = [cut(1600 + 256 * j, TOKENS) for j in range(2)]
            gated = [cut(2200 + 256 * j, TOKENS) for j in range(3)]
            act_cols = [cut(3000 + 256 * j, TOKENS) for j in range(8)]
            diag_free, spread_free, gated_free, cols_free = [None] * 2, [None] * 2, [None] * 3, [None] * 8
            total, pair = banks[0:4], banks[4:7]
            spread_bank = banks[7]
            pending = []
            n = 0
            last = None

            def down(e, ft, s, got_down, tok, index, final):
                wd = s.t[:, (0 if n_ft == 4 else (e % 2) * 2048):][:, 0:n_ft * D].rearrange("p (k n) -> p k n", k=n_ft)
                col = act_cols[index % 8]
                m = None
                for i in range(TT):
                    for half in range(2):
                        tb = total[i * 2 + half]
                        first = e == 0 and ft == 0
                        m = mms(tb.t[:, :], [(col[:, i * P:(i + 1) * P], wd[:, ft, half * BANK:(half + 1) * BANK])],
                                tok, got_down, *(tb.free if first else []), start=first, stop=final,
                                signal=(i == TT - 1 and half == 1), loose=True)
                cols_free[index % 8] = m
                if ft == n_ft - 1 and (n_ft == 4 or e % 2 == 1):
                    s.free = [m]
                return m

            down_slot = None
            for e in range(n_exp):
                j = e % 2
                for i in range(TT):
                    dt = v_ts(diag[j][:, i, :], ident[:, :], comb[:, i, e:e + 1], None, ALU.mult, None,
                              diag_free[j], t if e == 0 else None, chain=(e == 0))
                for i in range(TT):
                    m = mms(spread_bank.t[:, i * P:(i + 1) * P], [(ones[:, :], diag[j][:, i, :])],
                            dt, *spread_bank.free)
                diag_free[j] = m
                sp = a_fn(spread[j], spread_bank.t[:, 0:TOKENS], ACT.Copy, m, spread_free[j], chain=False)
                spread_bank.free = [sp]
                if n_ft == 4:
                    s1, got1 = load((lambda v: v[:, :], gate_w[e].rearrange("(p k) f -> p (k f)", k=KD)))
                    s3, got3 = load((lambda v: v[:, :], up_w[e].rearrange("(p k) f -> p (k f)", k=KD)))
                    w1v = s1.t[:, :].rearrange("p (k f) -> p k f", k=KD)
                    w3v = s3.t[:, :].rearrange("p (k f) -> p k f", k=KD)
                    down_slot, got_down = load((lambda v: v[:, :].rearrange("p (k n) -> p k n", k=4), by_k(down_w[e])))
                else:
                    s1, got1 = load((lambda v: v[:, 0:2048], gate_w[e].rearrange("(p k) f -> p (k f)", k=KD)),
                                    (lambda v: v[:, 2048:4096], up_w[e].rearrange("(p k) f -> p (k f)", k=KD)))
                    s3, got3 = s1, got1
                    w1v = s1.t[:, 0:2048].rearrange("p (k f) -> p k f", k=KD)
                    w3v = s1.t[:, 2048:4096].rearrange("p (k f) -> p k f", k=KD)
                    if e % 2 == 0:
                        down_slot, got_down = load(*[
                            (lambda v, q=q: v[:, q * 2048:(q + 1) * 2048].rearrange("p (k n) -> p k n", k=2),
                             by_k(down_w[e + q])) for q in range(2)])
                for ft in range(n_ft):
                    b = pair[n % 3]
                    f = slice(ft * P, (ft + 1) * P)
                    mms(b.t[:, 0:TOKENS], [(w1v[:, k, f], h_cols[:, k, :]) for k in range(KD)], got1, *b.free)
                    m = mms(b.t[:, TOKENS:2 * TOKENS], [(w3v[:, k, f], h_cols[:, k, :]) for k in range(KD)], got3)
                    if ft == n_ft - 1:
                        s1.free = [m]
                        s3.free = [m]
                    g = gated[n % 3]
                    t1 = a_fn(g, b.t[:, 0:TOKENS], ACT.Silu, m, gated_free[n % 3], chain=False)
                    t2 = pool.put(lambda g=g, q=spread[j]: nc.gpsimd.tensor_tensor(g, g, q, ALU.mult), t1, sp)
                    t3 = v_tt(act_cols[n % 8], b.t[:, TOKENS:2 * TOKENS], g, ALU.mult, t2, cols_free[n % 8],
                              chain=False)
                    b.free = [t3]
                    gated_free[n % 3] = t3
                    if ft == n_ft - 1:
                        spread_free[j] = t2
                    pending.append((e, ft, down_slot, got_down, t3, n))
                    if len(pending) > 1:
                        last = down(*pending.pop(0), False)
                    n += 1
            last = down(*pending.pop(0), True)
            for i in range(TT):
                for half in range(2):
                    b = total[i * 2 + half]
                    put = residual(gates_row[:, 1, :], sums=False)
                    b.free = [put(i, half * BANK, BANK, b, last)]
            return vector.last()

        def exp_rows(scores, scale, probs, st, m, *after):
            t = v_max(st[:, 0:1], scores, m)
            t = v_ts(st[:, 1:2], st[:, 0:1], -scale, None, ALU.mult, None, t)
            return a_fn(probs, scores, ACT.Exp, t, *after, scale=scale, bias=st[:, 1:2], accum_out=st[:, 2:3],
                        chain=False)

        def over_sum(probs, st, e):
            t = v_recip(st[:, 3:4], st[:, 2:3], e)
            return v_ts(probs, probs, st[:, 3:4], None, ALU.mult, None, t)

        context = cut(7680, TT, D)
        ctx_cols = cut(9728, KD, TOKENS)
        pick = cut(11776, 8)
        rep_both, conds = cut(13824, KD, 32), cut(14100, 3, KD)
        rows = lambda ap: ap.rearrange("(i p) d -> p i d", p=P)
        c_cols = lambda v: v.rearrange("(p k) -> p k", k=KD)
        stored = {n: nc.dram_tensor(n, (6 * D,), F32, kind="Internal").ap() for n in ("mod_one", "mod_two0", "mod_two1")}
        got_c = side_load("c", [(conds[:, 0], c_cols(a["c"][0])), (conds[:, 1], c_cols(a["c_ctx"])),
                                (conds[:, 2], c_cols(a["c_2"][0]))], lane=sync)
        t = a_fn(conds, conds, ACT.Silu, got_c)
        repeated = lambda j, n: conds[:, j].unsqueeze(2).to_broadcast([P, KD, n])
        for j in range(2):
            t_both = v_copy(rep_both[:, :, 16 * j:16 * j + 16], repeated(j, 16), t)
        v_copy(c_rep[:, 0], repeated(0, 32), t)
        t_rep = v_copy(c_rep[:, 1], repeated(2, 32), t)
        for j, c in enumerate((0, 64, 16, 80, 32, 96, 48, 112)):
            t_pick = v_copy(pick[:, j:j + 1], ident[:, c:c + 1])
        got_norms = side_load("norms", [(norm_w[:, :, :].rearrange("p n k -> p (n k)"), a["norm_cols"])], lane=scalar)
        first_mod = a["w_mod"][0].rearrange("(p k) n -> p k n", k=KD)
        bias, sums_ = (spare[:, j * BANK:(j + 1) * BANK] for j in range(2))
        got_bias = side_load("first_bias", [
            (bias[32 * j:32 * j + 32, :], a["b_mod"][0][j * BANK:(j + 1) * BANK].partition_broadcast(32))
            for j in range(4)], lane=scalar)
        b = mod_bank
        for k0 in range(0, KD, 2):
            s, got = load((lambda v: v[:, :].rearrange("p (k n) -> p k n", k=2), first_mod[:, k0:k0 + 2, 0:2 * D]))
            ws = s.t[:, :].rearrange("p (k n) -> p k n", k=2)
            for k in range(2):
                for j in range(4):
                    m = mms(b.t[32 * j:32 * j + 32, :], [(rep_both[:, k0 + k, :], ws[:, k, j * BANK:(j + 1) * BANK])],
                            got, t_both, start=k0 + k == 0, stop=k0 + k == KD - 1, loose=True,
                            signal=k == 1 and j == 3)
            s.free = [m]
            if k0 == 2:
                got_x = side_load("x", [(x[:, :, :], rows(a["x"][0]))], lane=sync)
                got_ctx = side_load("context", [(context, rows(a["ctx"][0]))], lane=sync)
        stats = small[:, 0:8]
        q = [a_fn(h_rows[:, i, :], src[:, i, :], ACT.Square, got, accum_out=stats[:, 2 * n + i:2 * n + i + 1])
             for n, (src, got) in enumerate(((x, got_x), (context, got_ctx))) for i in range(TT)]
        t_stats = rstd(stats[:, 4:8], stats[:, 0:4], D, *q)
        t = v_tt(sums_, b.t[:, :], bias, ALU.add, m, got_bias)
        b.free = [t]
        b = next_bank()
        for k in range(KD):
            for half in range(2):
                m = mms(b.t[64 * half:64 * half + 64, 4 * k:4 * k + 4],
                        [(sums_.rearrange("p (f k) -> p k f", k=KD)[:, k, :], pick[:, 4 * half:4 * half + 4])], t, t_pick, *b.free, loose=True)
        cols4 = b.t[:, 0:4 * KD].rearrange("p (k s) -> p s k", s=4)
        for n, at in ((0, 0), (CTX_NORM, 2)):
            v_copy(affine[:, n, 0], cols4[:, at, :], m)
            t_affine = v_stt(affine[:, n, 1], cols4[:, at + 1, :], 1.0, norm_w[:, 0], ALU.add, ALU.mult, m, got_norms)
        b.free = [t_affine]
        spare_free[0] = [t, m]
        normed = [a_fn(h_rows[:, 1, :], x[:, 1, :], ACT.Copy, t_stats, scale=stats[:, 5:6]),
                  v_ts(h_rows[:, 0, :], x[:, 0, :], stats[:, 4:5], None, ALU.mult, None, t_stats)]
        t_h = normed_cols(h_rows, h_cols, 0, *normed, t_affine)
        normed = [a_fn(context[:, 1, :], context[:, 1, :], ACT.Copy, t_stats, scale=stats[:, 7:8]),
                  v_ts(context[:, 0, :], context[:, 0, :], stats[:, 6:7], None, ALU.mult, None, t_stats)]
        t_ctx = normed_cols(context, ctx_cols, CTX_NORM, *normed, t_affine)
        got_places = side_load("places", [(before[:, :], a["k_before"][:, 0:P]), (places[:, :], a["k_before"][:, P:P + PLACES]),
                                            (resets[:, 0:104], a["k_before"][:, P + PLACES:])])
        got_chunk = side_load("chunk", [(ws_t, a["w_s_t"]), (bs_cols, a["b_s_t"])])
        got_attention = side_load("attention", [
            (axial, a["k_axial"].rearrange("p (i c d) -> p i c d", i=TT, c=2)),
            (qk_w, a["qk_norm_w"].partition_broadcast(P).rearrange("p (h d) -> p h d", h=10))])
        got_bounds = side_load("bounds", [(lb_logits, a["hgrn_lb_logits"][0].partition_broadcast(P))])
        got_hgrn_w = side_load("hgrn_w", [(w_c[:, h, :], a["hgrn_norm_w"][0].partition_broadcast(P)) for h in range(C_HEADS)])
        got_latent = side_load("latent", [
            (latent[:, 0:5], a["mla_cols"]),
            (latent[:, 384:576], a["mla_q_norm_g_2"][0].partition_broadcast(P)),
            (latent[:, 576:768], a["mla_k_norm_g_2"][0].partition_broadcast(P)),
            (latent[:, 768:770].bitcast(I32), a["positions_2_cols"]), (latent[:, 772:804], a["k_freq"])])
        background.append(modulation(c_rep[:, 0], a["w_mod"][0], a["b_mod"][0], stored["mod_one"], [1, 2], "mod_one", 0, t_rep))
        background.append(modulation(c_rep[:, 1], a["ada_w_2"][0], a["ada_b_2"][0], stored["mod_two0"], [0, 1, 2],
                                     "mod_two0", 2, t_rep))
        route_load("one", a["route_w_one"], a["route_b_one"], 0)
        route_load("two0", a["route_w_two0"], a["route_b_two0"], 1)

        proj = cut(0, TT, IN_W)
        ctx_proj = cut(5120, TT, CTX_W)
        flip = [0]

        def copy_out(dst_of):
            def put(i, c0, n, b, m):
                flip[0] ^= 1
                if flip[0]:
                    return v_copy(dst_of(i, c0, n), b.t[:, 0:n], m, chain=False)
                return a_fn(dst_of(i, c0, n), b.t[:, 0:n], ACT.Copy, m, chain=False)
            return put

        mix_cols = h_cols
        gelu = cut(8200, TT, OFF_B)
        ya = h_rows[:, :, 0:256]
        sq_a = cut(9224, A_HEADS, HD)

        def chunk_gate(ready):
            t = a_fn(gelu, proj[:, :, 0:OFF_B], ACT.Gelu_apprx_tanh, *ready, *t_ctx)
            for i in range(TT):
                v = gelu[:, i, 256:512].rearrange("p (h d) -> p h d", h=A_HEADS)
                t = head_norm(v, v, A_HEADS, HD, None, sq_a, small[:, 20:24], t)
            return t

        def chunk_mix(t_v):
            for i in range(TT):
                b = next_bank()
                for h in range(A_HEADS):
                    m = mms(b.t[:, h * HD:(h + 1) * HD],
                            [(ws_t[:, h, :], gelu[:, i, 256 + h * HD:256 + (h + 1) * HD])], got_chunk, t_v, *b.free)
                for h in range(A_HEADS):
                    f = slice(h * HD, (h + 1) * HD)
                    b.free = [v_stt(ya[:, i, f], b.t[:, f], bs_cols[:, h:h + 1], gelu[:, i, f], ALU.add, ALU.mult,
                                    m, got_chunk, *t_h, chain=False)]
            return b.free[0]

        rot, sq_qk = cut(13184, 10, HD), cut(14464, 10, HD)
        k_pair = cut(11904, 2 * TT, B_KV, 2, HD)

        def rotate(i, ready):
            qk = proj[:, i, OFF_B:OFF_KV + 128].rearrange("p (h d) -> p h d", h=10)
            head_norm(qk, qk, 10, HD, qk_w, sq_qk, small[:, 8:18], got_attention, *ready)
            x4 = qk.rearrange("p h (a s e) -> p (h a) s e", a=2, s=2)
            r4 = rot.rearrange("p h (a s e) -> p (h a) s e", a=2, s=2)
            v_copy(r4[:, :, 0, :], x4[:, :, 1, :])
            v_copy(r4[:, :, 1, :], x4[:, :, 0, :])
            v_tt(rot, rot, axial[:, i, 1, :].unsqueeze(1).to_broadcast([P, 10, HD]), ALU.mult)
            v_tt(qk, qk, axial[:, i, 0, :].unsqueeze(1).to_broadcast([P, 10, HD]), ALU.mult)
            v_tt(qk, qk, rot, ALU.add)
            kk = ctx_proj[:, i, 0:128].rearrange("p (h d) -> p h d", h=2)
            head_norm(kk, kk, 2, HD, qk_w[:, 8:10, :], sq_qk[:, 0:2, :], small[:, 8:10])
            for c in range(2):
                v_copy(k_pair[:, i, :, c, :], proj[:, i, OFF_KV:OFF_KV + 128].rearrange("p (h d) -> p h d", h=2))
                t = v_copy(k_pair[:, TT + i, :, c, :], kk)
            return t

        for c0 in range(0, IN_W, BANK):
            s, got = load((lambda v: v[:, :].rearrange("p (k n) -> p k n", k=KD),
                           by_p(a["w_in"][0])[:, :, c0:c0 + BANK]))
            ws = s.t[:, :].rearrange("p (k n) -> p k n", k=KD)
            lo, hi = max(c0, OFF_KV), min(c0 + BANK, OFF_G)
            put_x = copy_out(lambda i, c, n: proj[:, i, c:c + n])
            put_c = copy_out(lambda i, c, n: ctx_proj[:, i, c:c + n])
            for i in range(TT):
                b = next_bank()
                m = mms(b.t[:, :], [(h_cols[:, k, i * P:(i + 1) * P], ws[:, k, :]) for k in range(KD)],
                        got, *t_h, *b.free)
                b.free = [put_x(i, c0, BANK, b, m)]
                if lo < hi:
                    b = next_bank()
                    m = mms(b.t[:, 0:hi - lo],
                            [(ctx_cols[:, k, i * P:(i + 1) * P], ws[:, k, lo - c0:hi - c0]) for k in range(KD)],
                            *t_ctx, *b.free)
                    b.free = [put_c(i, lo - OFF_KV, hi - lo, b, m)]
            s.free = [m]
            here = [vector.last(), scalar.last()]
            if c0 == 0:
                t_v = chunk_gate(here)
            elif c0 == BANK:
                t_a = chunk_mix(t_v)
            elif c0 == 2 * BANK:
                rotate(0, here)
            elif c0 == 3 * BANK:
                t_qk = rotate(1, here)
            step()
        b = next_bank()
        bv = b.t[:, :].rearrange("p (k t) -> p k t", k=2)
        for k in range(2):
            for i in range(TT):
                m = turn(bv[:, k, i * P:(i + 1) * P], ya[:, i, k * P:(k + 1) * P], t_a, *b.free)
        b.free = [a_fn(mix_cols[:, 0:2, :], bv, ACT.Copy, m)]
        mixed_a = [t_a, b.free[0], m]

        q_cols = cut(9856, 4, TOKENS)
        k_cols = cut(10880, B_KV, 2 * TOKENS)
        probs = [cut(12928 + 512 * j, 512) for j in range(3)]
        probs_t = [cut(11904, 4, TOKENS), cut(14464, 4, TOKENS)]
        t_q = rows_to_cols(lambda i, k: proj[:, i, OFF_B + k * P:OFF_B + (k + 1) * P], q_cols, 4, t_qk)
        t_k = []
        for g in range(B_KV):
            b = next_bank()
            for i in range(2 * TT):
                m = turn(b.t[:, i * P:(i + 1) * P], k_pair[:, i, g].rearrange("p a b -> p (a b)"), t_qk, *b.free)
            b.free = [v_copy(k_cols[:, g, :], b.t[:, :], m)]
            t_k += b.free
        scale = HD ** -0.5
        jobs = [(h, i) for h in range(B_HEADS) for i in range(TT)]
        probs_free, probs_t_free = [None] * 3, [None] * 2
        state = {}

        def scores_of(n):
            h, i = jobs[n]
            part = slice(64 * (h % 2), 64 * (h % 2) + 64)
            b = next_bank()
            m = mms(b.t[:, :], [(q_cols[part, h // 2, i * P:(i + 1) * P], k_cols[part, h // 4, :])],
                    *t_q, *t_k, *b.free)
            state[n] = (b, m)

        def begin(n):
            b, m = state[n]
            st = small[:, 32 + 4 * (n % 4):36 + 4 * (n % 4)]
            e = exp_rows(b.t[:, :], scale, probs[n % 3], st, m, probs_free[n % 3])
            b.free = [e]
            state[n] = (st, e)

        def attend(n):
            h, i = jobs[n]
            pr, pt = probs[n % 3], probs_t[h % 2]
            t = over_sum(pr, *state[n])
            b2 = next_bank()
            for kt in range(4):
                m = turn(b2.t[:, kt * P:(kt + 1) * P], pr[:, kt * P:(kt + 1) * P], t, *b2.free)
            probs_free[n % 3] = m
            tc = a_fn(pt[:, :, i * P:(i + 1) * P], b2.t[:, :].rearrange("p (k t) -> p k t", k=4), ACT.Copy, m,
                      probs_t_free[h % 2])
            b2.free = [tc]
            if late:
                late.pop()()

            def values():
                b3 = next_bank()
                part = slice(64 * (h % 2), 64 * (h % 2) + 64)
                g = h // 4
                vals = [proj[:, kt, OFF_KV + 128 + g * HD:OFF_KV + 128 + (g + 1) * HD] for kt in range(TT)] + \
                       [ctx_proj[:, kt, 128 + g * HD:128 + (g + 1) * HD] for kt in range(TT)]
                m = mms(b3.t[part, 0:TOKENS], [(vals[kt], pt[:, kt, :]) for kt in range(4)], tc, *b3.free)
                probs_t_free[h % 2] = m
                b3.free = [v_copy(mix_cols[part, 2 + h // 2, :], b3.t[part, 0:TOKENS], m)]
            if i == TT - 1:
                late.append(values)

        logf = cut(7680, 2 * TT, 2, CW)
        q_act = proj[:, :, OFF_C:OFF_C + CW]
        sil = h_rows[:, :, 0:256]
        lb = h_rows[:, 0, 256:768], h_rows[:, 1, 256:768], spare[:, 1024:1536]
        zs = [proj[:, :, OFF_C + CW:OFF_C + 3 * CW], ctx_proj[:, :, 256 + CW:256 + 3 * CW]]
        logs = [logf[:, 2 * n:2 * n + 2].rearrange("p i a b -> p i (a b)") for n in range(2)]
        spread = lambda ap: ap.unsqueeze(1).to_broadcast([P, TT, 2 * CW])
        bounds_in = lb_logits.rearrange("p a b -> p (a b)")

        def gate_inputs(n):
            if n == 0:
                t = v_tt(lb[0], bounds_in, bounds_in, ALU.subtract, got_bounds, *mixed_a)
                t = a_fn(lb[0], lb[0], ACT.Exp, t)
                for k in range(2):
                    a_fn(logs[k], zs[k], ACT.Abs, *mixed_a, chain=False)
                t = v_recip(lb[1], lb[0], t)
                t = v_tt(lb[0], lb[0], lb[1], ALU.mult, t)
                t = v_tt(lb[0], lb[0], lb[0], ALU.subtract, t)
                gate_at["bound"] = v_ts(lb[1], lb[0], -1.0, 1.0, ALU.mult, ALU.add, t)
            elif n == 1:
                for k in range(2):
                    a_fn(logs[k], logs[k], ACT.Exp, scale=-1.0)
            elif n == 2:
                gate_at["ln"] = [a_fn(logs[k], logs[k], ACT.Ln, bias=1.0) for k in range(2)][-1]
                gate_at["log_bound"] = a_fn(lb[2], lb[1], ACT.Ln, gate_at["bound"])
            elif n == 3:
                for k in range(2):
                    t = v_stt(logs[k], zs[k], 0.0, logs[k], ALU.min, ALU.subtract, gate_at["ln"], chain=False)
                gate_at["min"] = t
            elif n == 4:
                for k in range(2):
                    gate_at["logf"] = v_tt(logs[k], logs[k], spread(lb[2]), ALU.add, gate_at["log_bound"])
                gate_at["sigmoid"] = [a_fn(zs[k], zs[k], ACT.Sigmoid, gate_at["min"], scale=-1.0) for k in range(2)][-1]
            elif n == 5:
                a_fn(q_act, q_act, ACT.Silu, chain=False)
                gate_at["silu"] = a_fn(sil, proj[:, :, OFF_G:IN_W], ACT.Silu, chain=False)
                for k in range(2):
                    gate_at["keys"] = v_tt(zs[k], zs[k], spread(lb[1]), ALU.mult, gate_at["sigmoid"])

        gate_at = {}
        late = []
        scores_of(0)
        scores_of(1)
        begin(0)
        for n in range(len(jobs)):
            if n + 2 < len(jobs):
                scores_of(n + 2)
            if n + 1 < len(jobs):
                begin(n + 1)
            attend(n)
            if n % 4 != 3:
                step()
            gate_inputs(n)
        late.pop()()
        while len(background) > 1:
            step()
        got_gates = [gate_load("mod_one", stored["mod_one"], half) for half in range(2)]
        done_b = everyone()

        s_scan, got_scan = load((lambda v: v[:, 0:4096], a["k_scan"]))
        s_scan.held = True
        kc = s_scan.t
        sums = [kc[:, 0:1024], kc[:, 1024:2048]]
        after = [kc[:, 2048:2176], kc[:, 2176:2304]]
        masks = [kc[:, 2304 + d * 896:2304 + (d + 1) * 896].rearrange("p (j t) -> p j t", j=LEVELS) for d in range(2)]
        key_rows = lambda n, d: (proj[:, n, OFF_C + CW + d * CW:OFF_C + 2 * CW + d * CW] if n < TT else
                                 ctx_proj[:, n - TT, 256 + CW + d * CW:256 + 2 * CW + d * CW])
        t_in = [gate_at["keys"], gate_at["silu"]]

        q_c = proj[:, :, 512:768]
        k_c = [proj[:, :, 768:1024], ctx_proj[:, :, 0:256]]
        gates = cut(11776, 8, 2, TOKENS)
        att = [h_rows[:, par, 256:768].rearrange("p (c t) -> p c t", c=4) for par in range(2)]
        rows64 = [slice(0, 64), slice(64, 128)]
        t_q = rows_to_cols(lambda i, k: q_act[:, i, k * P:(k + 1) * P], q_c, 2, *t_in, *done_b)
        t_k = []
        for d in range(2):
            t_k += rows_to_cols(lambda i, k: key_rows(i, d)[:, k * P:(k + 1) * P], k_c[d], 2, *t_in, *done_b)
        t_in.append(vector.last())
        ksum = gates[:, 0]
        t = v_tt(ksum, k_c[0], k_c[1], ALU.add, *t_k)
        att_last = [None, None]
        blocks = [(i, pair_) for i in range(TT) for pair_ in range(2)]
        for par in range(2):
            b = next_bank()
            for c, (i, pair_) in enumerate(blocks):
                m = mms(b.t[:, c * P:(c + 1) * P],
                        [(ksum[rows64[par], pair_, i * P:(i + 1) * P], q_c[rows64[par], pair_, i * P:(i + 1) * P])],
                        t, *t_q, *t_in, *b.free)
            b.free = [v_tt(att[par], b.t[:, :].rearrange("p (c t) -> p c t", c=4),
                           ident[:, :].unsqueeze(1).to_broadcast([P, 4, P]), ALU.mult, m)]
            att_last[par] = b.free[0]
        vals = [proj[:, i, OFF_C + 3 * CW:OFF_C + 4 * CW] for i in range(TT)] + \
               [ctx_proj[:, i, 256 + 3 * CW:256 + 4 * CW] for i in range(TT)]
        st = [[h_rows[:, d, 768 + 128 * j:896 + 128 * j].rearrange("p (a b) -> p a b", a=2) for j in range(2)]
              for d in range(2)]
        order = [[2, 3, 0], [3, 2, 1]]
        rests = [(nth, d, order[d][nth]) for nth in range(3) for d in range(2)]
        decay_to_end = [gates[:, 2 + j // 2, j % 2, :] for j in range(6)]
        whole = small[:, 60:72].rearrange("p (j a) -> p j a", j=6)
        t_rest, state_at = [], {}
        for j, (nth, d, n) in enumerate(rests):
            b = next_bank()
            m = mms(b.t[:, 0:CW], [(after[d], logf[:, n, d, :])], got_scan, *t_in, *t_k, *b.free)
            for pair_ in range(2):
                m = mms(b.t[:, CW + 2 * pair_:CW + 2 * pair_ + 1],
                        [(logf[:, n, d, pair_ * P:(pair_ + 1) * P], ones[:, 0:1])])
            a_fn(whole[:, j, :], b.t[:, CW:CW + 4:2], ACT.Exp, m, chain=False)
            t = a_fn(decay_to_end[j], b.t[:, 0:CW], ACT.Exp, *done_b, chain=False)
            b.free = [t]
            t_rest.append(v_tt(key_rows(n, d), key_rows(n, d), decay_to_end[j], ALU.mult, t, chain=False))
        for j, (nth, d, n) in enumerate(rests):
            b = next_bank()
            for h in range(C_HEADS):
                part = slice(64 * (h % 2), 64 * (h % 2) + 64)
                m = mms(b.t[part, (h // 2) * HD:(h // 2 + 1) * HD],
                        [(key_rows(n, d)[:, h * HD:(h + 1) * HD], vals[n][:, h * HD:(h + 1) * HD])], t_rest[j], *b.free)
            new, old = st[d][nth % 2], st[d][(nth - 1) % 2]
            bv = b.t[:, 0:2 * HD].rearrange("p (a b) -> p a b", a=2)
            if nth == 0:
                b.free = [v_copy(new, bv, m, *done_b)]
            else:
                for pair_ in range(2):
                    b.free = [v_stt(new[:, pair_, :], old[:, pair_, :], whole[:, j, pair_:pair_ + 1],
                                    bv[:, pair_, :], ALU.mult, ALU.add, m)]
                tile = (0 if nth == 1 else 1) if d == 0 else (1 if nth == 1 else 0)
                state_at[d, tile] = (new, b.free[0])
        q_in = [proj[:, :, 0:256], proj[:, :, 256:512]]
        for d in range(2):
            gate_free = [tensor.last(), vector.last()]
            t_g = []
            for pair_ in range(2):
                for i in range(TT):
                    for half in range(2):
                        b = next_bank()
                        m = mms(b.t[:, :], [(logf[:, i, d, pair_ * P:(pair_ + 1) * P],
                                             sums[d][:, half * BANK:(half + 1) * BANK])], got_scan, *t_in, *b.free)
                        b.free = [a_fn(gates[:, half * 4:half * 4 + 4, pair_, i * P:(i + 1) * P],
                                       b.t[:, :].rearrange("p (j t) -> p j t", j=4), ACT.Exp, m, *gate_free)]
            t_g = b.free[0]

            def factors(j):
                w = 1 << j
                cutj = lambda ap: ap.rearrange("p a (b s w) -> p a b s w", s=2, w=w)
                gj, qj, kj = cutj(gates[:, j]), cutj(q_c), cutj(k_c[d])
                qs, ks = (1, 0) if d == 0 else (0, 1)
                v_tt(gj[:, :, :, qs, :], gj[:, :, :, qs, :], qj[:, :, :, qs, :], ALU.mult, t_g, *t_q, chain=False)
                return v_tt(gj[:, :, :, ks, :], gj[:, :, :, ks, :], kj[:, :, :, ks, :], ALU.mult, *t_k, chain=False)

            t_next = factors(0)
            for j in range(LEVELS):
                t = t_next
                if j + 1 < LEVELS:
                    t_next = factors(j + 1)
                mask = masks[d][:, j, :].bitcast(U32).unsqueeze(1).to_broadcast([P, 4, P])
                for par in range(2):
                    b = next_bank()
                    for c, (i, pair_) in enumerate(blocks):
                        g = gates[rows64[par], j, pair_, i * P:(i + 1) * P]
                        m = mms(b.t[:, c * P:(c + 1) * P], [(g, g)], t, *b.free)
                    b.free = [dve(lambda par=par, b=b, mask=mask: nc.vector.copy_predicated(
                        att[par], mask, b.t[:, :].rearrange("p (c t) -> p c t", c=4)), m, got_scan, att_last[par],
                        chain=False)]
                    att_last[par] = b.free[0]
                step()
            t = v_tt(q_in[d], gates[:, 7], q_c, ALU.mult)
        t_att = [t, *att_last]

        att_done = everyone()
        o_rows = gates[:, 6:8].rearrange("p j a b -> p (j a b)")[:, 0:512].rearrange("p (i c) -> p i c", i=TT)
        for i in range(TT):
            for par in range(2):
                b = next_bank()
                for pair_ in range(2):
                    h = 2 * pair_ + par
                    o_part = b.t[:, pair_ * HD:(pair_ + 1) * HD]
                    m = mms(o_part, [(att[par][:, 2 * i + pair_, :], vals[i][:, h * HD:(h + 1) * HD])],
                            *t_att, state_at[0, i][1], state_at[1, i][1], *b.free, stop=False)
                    m = mms(o_part, [(q_in[d][rows64[par], pair_, i * P:(i + 1) * P],
                                      state_at[d, i][0][rows64[par], pair_, :]) for d in range(2)], start=False)
                o4 = o_rows[:, i, :].rearrange("p (a b d) -> p a b d", a=2, b=2)
                b.free = [v_copy(o4[:, :, par, :], b.t[:, 0:P].rearrange("p (a d) -> p a d", a=2), m, *att_done)]
        s_scan.free, s_scan.held = everyone(), False
        sq = cut(9984, C_HEADS, HD)
        vector.wait(got_hgrn_w)
        for i in range(TT):
            o = o_rows[:, i, :].rearrange("p (h d) -> p h d", h=C_HEADS)
            t = head_norm(o, o, C_HEADS, HD, w_c, sq, small[:, 8:12])
            t = v_tt(o_rows[:, i, :], o_rows[:, i, :], sil[:, i, :], ALU.mult)
        t = rows_to_cols(lambda i, k: o_rows[:, i, k * P:(k + 1) * P], mix_cols[:, 6:8, :], 2, t)
        mixed = everyone()

        product_rows(mix_cols, KD, a["w_out"][0], by_k, D, residual(gates_row[:, 0, :]), *mixed, got_gates[0])
        finish()
        done = everyone()
        got_first_gate = gate_load("mod_two0", stored["mod_two0"], 0, *done)
        t_affine = fold(1)
        t = normalize(*done, halves=squared.values())
        t = normed_cols(h_rows, h_cols, 1, *t, t_affine, follow=route_products())
        vector.wait(got_places)
        tensor.wait(got_places)
        background.append(filters(cut(11776, 4096), *done))
        experts("one", 1, 4, 8, 512, a["w1"][0], a["w3"][0], a["w2"][0], got_gates[1], *t, *everyone())
        filters_stored = spectrum_stored[1, 3]
        done = everyone()

        for layer in range(2):
            name = f"two{layer}"
            mod_name = "mod_" + name
            got_gates = [got_first_gate, gate_load(mod_name, stored[mod_name], 1, *done)]
            if layer == 1:
                route_load(name, a["route_w_" + name], a["route_b_" + name], 0, *done)
            t_affine = fold(2 * layer + 2)
            t = normalize(*done)
            t_h = normed_cols(h_rows, h_cols, 2 * layer + 2, *t, t_affine)
            ready = everyone()

            if layer == 0:
                lat = cut(0, TT, 448)
                cq_c, ckv_c = cut(896, 2, TOKENS), cut(1408, 1, TOKENS)
                q = cut(1664, TT, 1536)
                kv = cut(4736, TT, 2048)
                q_pe = cut(8832, TT, 8, ROPE)
                k_pe2 = cut(9856, TT, 2, ROPE)
                qn_c, qp_c = cut(10112, 8, TOKENS), cut(12160, 4, TOKENS)
                kn_c, kp_c = cut(13184, 8, TOKENS), cut(15232, 1, TOKENS)
                pr = [cut(256 * j, TOKENS) for j in range(3)]
                pt = [cut(768 + 512 * j, TT, TOKENS) for j in range(2)]
                w_q_pe, w_k_pe = latent[:, 384 + NOPE:576], latent[:, 576 + NOPE:768]
                cs, sn = (cut(15488 + 64 * j, TT, HALF) for j in range(2))
                ang, red = (h_rows[:, 0, 832 + 64 * j:896 + 64 * j].rearrange("p (i c) -> p i c", i=TT)
                            for j in range(2))
                pos_i, freq = latent[:, 768:770].bitcast(I32), latent[:, 772:804]
                pos_f = latent[:, 770:772]
                sq = h_rows[:, 1, :]
                squares = [h_rows.rearrange("p i d -> p (i d)")[:, 0:1536], filter_out[:, :]]
                vector.wait(got_latent)
                t = v_copy(pos_f, pos_i, *ready)
                for i in range(TT):
                    t = v_ts(ang[:, i, :], freq, pos_f[:, i:i + 1], None, ALU.mult, None)
                for dst, turns in ((sn, 0.0), (cs, 0.25)):
                    t = v_ts(red, ang, float(1 / (2 * np.pi)), turns, ALU.mult, ALU.add)
                    t = v_ts(red, red, ROUND, -ROUND, ALU.add, ALU.add)
                    t = v_stt(dst, red, -TWO_PI_1, ang, ALU.mult, ALU.add)
                    t = v_stt(dst, red, -TWO_PI_2, dst, ALU.mult, ALU.add)
                    t = v_stt(dst, red, -TWO_PI_3, dst, ALU.mult, ALU.add)
                    t = v_ts(dst, dst, float(np.pi / 2) * turns * 4, PI_IN, ALU.add, ALU.min)
                    t = v_ts(dst, dst, -PI_IN, None, ALU.max, None)
                    t_trig = a_fn(dst, dst, ACT.Sin, t)

                down_in = load_columns(KD, by_p(a["mla_w_down_2"][0]), 0, 448)
                uq_in = load_columns(2, by_k(a["mla_w_uq_2"][0]), 0, 1536)
                ukv_in = load_columns(1, by_k(a["mla_w_ukv_2"][0]), 0, 2048)
                background.append(modulation(c_rep[:, 1], a["ada_w_2"][1], a["ada_b_2"][1], stored["mod_two1"],
                                             [0, 1, 2], "mod_two1", 4, t_rep))
                product_rows(h_cols, KD, None, None, 448,
                             copy_out(lambda i, c, n: lat[:, i, c:c + n]), *t_h, loaded=down_in)
                here = [vector.last(), scalar.last()]
                stat = small[:, 8:14].rearrange("p (g i) -> p g i", g=3)
                groups = ((0, Q_LORA), (Q_LORA, 384), (384, 448))
                for i in range(TT):
                    for g, (lo, hi) in enumerate(groups):
                        t = a_fn(sq[:, 0:hi - lo], lat[:, i, lo:hi], ACT.Square, *here, accum_out=stat[:, g, i:i + 1])
                for g, (lo, hi) in enumerate(groups):
                    t = v_ts(stat[:, g, :], stat[:, g, :], 1.0 / (hi - lo), EPS, ALU.mult, ALU.add, t, t_trig)
                t = a_fn(small[:, 8:14], small[:, 8:14], ACT.Sqrt, t)
                t = v_recip(small[:, 8:14], small[:, 8:14], t)
                for i in range(TT):
                    for g, (lo, hi) in enumerate(groups[0:2]):
                        t_lat = v_ts(lat[:, i, lo:hi], lat[:, i, lo:hi], stat[:, g, i:i + 1], None, ALU.mult, None, t)
                for i in range(TT):
                    v_stt(lat[:, i, 384:448], lat[:, i, 384:448], stat[:, 2, i:i + 1], w_k_pe, ALU.mult, ALU.mult)

                def turn_pairs(op, x1_, x2_, c_, s_, u1, u2, o1, o2):
                    op(u1, x1_, c_, ALU.mult)
                    op(u2, x2_, s_, ALU.mult)
                    op(o1, u1, u2, ALU.subtract)
                    op(u1, x1_, s_, ALU.mult)
                    op(u2, x2_, c_, ALU.mult)
                    return op(o2, u1, u2, ALU.add)

                u_k = [sq[:, 256 + 64 * j:320 + 64 * j].rearrange("p (i c) -> p i c", i=TT) for j in range(2)]
                turn_pairs(v_tt, lat[:, :, 384:416], lat[:, :, 416:448], cs, sn, *u_k,
                           k_pe2[:, :, 0, 0:32], k_pe2[:, :, 0, 32:64])
                t = v_copy(k_pe2[:, :, 1, :], k_pe2[:, :, 0, :])
                t_cq = rows_to_cols(lambda i, k: lat[:, i, k * P:(k + 1) * P], cq_c, 2, t_lat,
                                    weight=lambda k: w_cq[:, k:k + 1])
                t_ckv = rows_to_cols(lambda i, k: lat[:, i, Q_LORA:384], ckv_c, 1, t_lat, weight=lambda k: w_ckv)
                t_kp = rows_to_cols(lambda i, k: k_pe2[:, i].rearrange("p a b -> p (a b)"), kp_c, 1, t)
                bw = lambda ap, n: ap.unsqueeze(1).to_broadcast([P, 8, n])
                q_heads = [q[:, i, :].rearrange("p (h d) -> p h d", h=8) for i in range(TT)]
                k_heads = [kv[:, i, :].rearrange("p (h d) -> p h d", h=8) for i in range(TT)]
                across = lambda ap, n: ap.unsqueeze(2).to_broadcast([P, 8, n])

                product_rows(cq_c, 2, None, None, 1536,
                             copy_out(lambda i, c, n: q[:, i, c:c + n]), *t_cq, loaded=uq_in)
                here = [vector.last(), scalar.last()]
                stat = [small[:, 8 + 16 * i:24 + 16 * i] for i in range(TT)]
                t_sq = [a_fn(squares[i], q[:, i, :], ACT.Square, *here, *filters_stored, chain=False) for i in range(TT)]
                t_q = []
                for i in range(TT):
                    s8 = squares[i].rearrange("p (h d) -> p h d", h=8)
                    v_sum(stat[i][:, 0:8], s8[:, :, 0:NOPE], t_sq[i])
                    v_sum(stat[i][:, 8:16], s8[:, :, NOPE:])
                    v_ts(stat[i][:, 0:8], stat[i][:, 0:8], 1.0 / NOPE, EPS, ALU.mult, ALU.add)
                    t_q.append(v_ts(stat[i][:, 8:16], stat[i][:, 8:16], 1.0 / ROPE, EPS, ALU.mult, ALU.add))
                t_q = [a_fn(stat[i], stat[i], ACT.Sqrt, t_q[i], chain=False) for i in range(TT)]
                t_q = [v_recip(stat[i], stat[i], t_q[i]) for i in range(TT)]
                for i in range(TT):
                    t_qn_rows = v_tt(q_heads[i][:, :, 0:NOPE], q_heads[i][:, :, 0:NOPE], across(stat[i][:, 0:8], NOPE),
                                     ALU.mult)
                    pe = q_heads[i][:, :, NOPE:]
                    pool_tt(pe, pe, across(stat[i][:, 8:16], ROPE), ALU.mult, t_q[i])
                    pool_tt(pe, pe, bw(w_q_pe, ROPE), ALU.mult)
                    u_q = [squares[i][:, 256 * j:256 * j + 256].rearrange("p (h d) -> p h d", h=8) for j in range(2)]
                    t_qp_rows = turn_pairs(pool_tt, pe[:, :, 0:32], pe[:, :, 32:64], bw(cs[:, i, :], HALF),
                                           bw(sn[:, i, :], HALF), *u_q, q_pe[:, i, :, 0:32], q_pe[:, i, :, 32:64])
                product_rows(ckv_c, 1, None, None, 2048,
                             copy_out(lambda i, c, n: kv[:, i, c:c + n]), *t_ckv, loaded=ukv_in)
                here = [vector.last(), scalar.last()]
                t_qn = rows_to_cols(lambda i, h: q[:, i, h * 192:h * 192 + NOPE], qn_c, 8, t_qn_rows, weight=lambda k: w_qn)
                k_squares = [squares[i][:, 512:1536].rearrange("p (h d) -> p h d", h=8) for i in range(TT)]
                for i in range(TT):
                    t = a_fn(k_squares[i], k_heads[i][:, :, 0:NOPE], ACT.Square, *here, t_q[i], chain=False)
                    t = v_sum(small[:, 40 + 8 * i:48 + 8 * i], k_squares[i], t)
                t = rstd(small[:, 40:56], small[:, 40:56], NOPE, t)
                for i in range(TT):
                    t = v_tt(k_heads[i][:, :, 0:NOPE], k_heads[i][:, :, 0:NOPE],
                             across(small[:, 40 + 8 * i:48 + 8 * i], NOPE), ALU.mult, t)
                t_kn = rows_to_cols(lambda i, h: kv[:, i, h * 256:h * 256 + NOPE], kn_c, 8, t, weight=lambda k: w_kn)
                t_qp = rows_to_cols(lambda i, k: q_pe[:, i, 2 * k:2 * k + 2, :].rearrange("p a b -> p (a b)"),
                                    qp_c, 4, t_qp_rows)
                out_c = h_cols
                scale = (NOPE + ROPE) ** -0.5
                jobs = [(h, i) for h in range(8) for i in range(TT)]
                pr_free, pt_free, state = [None] * 3, [None] * 2, {}

                def scores2(n):
                    h, i = jobs[n]
                    part = slice(64 * (h % 2), 64 * (h % 2) + 64)
                    b = next_bank()
                    mms(b.t[:, 0:TOKENS], [(qn_c[:, h, i * P:(i + 1) * P], kn_c[:, h, :])],
                        *t_qn, *t_kn, *b.free, stop=False)
                    m = mms(b.t[:, 0:TOKENS], [(qp_c[part, h // 2, i * P:(i + 1) * P], kp_c[part, 0, :])],
                            *t_qp, *t_kp, start=False)
                    state[n] = (b, m)

                def begin2(n):
                    b, m = state[n]
                    st = small[:, 32 + 4 * (n % 4):36 + 4 * (n % 4)]
                    e = exp_rows(b.t[:, 0:TOKENS], scale, pr[n % 3], st, m, pr_free[n % 3])
                    b.free = [e]
                    state[n] = (st, e)

                def attend2(n):
                    h, i = jobs[n]
                    r, tr = pr[n % 3], pt[h % 2]
                    t = over_sum(r, *state[n])
                    b2 = next_bank()
                    for kt in range(TT):
                        m = turn(b2.t[:, kt * P:(kt + 1) * P], r[:, kt * P:(kt + 1) * P], t, *b2.free)
                    pr_free[n % 3] = m
                    tc = a_fn(tr[:, :, i * P:(i + 1) * P], b2.t[:, 0:TOKENS].rearrange("p (k t) -> p k t", k=TT),
                              ACT.Copy, m, pt_free[h % 2])
                    b2.free = [tc]
                    if late:
                        late.pop()()

                    def values():
                        b3 = next_bank()
                        m = mms(b3.t[:, 0:TOKENS], [(kv[:, kt, h * 256 + NOPE:(h + 1) * 256], tr[:, kt, :])
                                                    for kt in range(TT)], tc, *b3.free)
                        pt_free[h % 2] = m
                        b3.free = [v_copy(out_c[:, h, :], b3.t[:, 0:TOKENS], m)]
                    if i == TT - 1:
                        late.append(values)

                scalar.wait(*everyone())
                scores2(0)
                scores2(1)
                begin2(0)
                for n in range(len(jobs)):
                    if n + 2 < len(jobs):
                        scores2(n + 2)
                    if n + 1 < len(jobs):
                        begin2(n + 1)
                    attend2(n)
                    step()
                late.pop()()
                product_rows(out_c, KD, a["mla_w_o_2"][0], by_k, D, residual(gates_row[:, 0, :]), *everyone(), got_gates[0])
            else:
                u = cut(0, 24, TOKENS)
                params = cut(6144, 5, 24)
                padded = [cut(6272 + 264 * j, 264) for j in range(3)]
                kr, ki, kn = ([cut(7064 + 2560 * h, TT, BANK) for h in range(2)],
                              [cut(8088 + 2560 * h, TT, BANK) for h in range(2)],
                              [cut(9112 + 2560 * h, BANK) for h in range(2)])
                spec = [cut(12184, 4, BANK), spare[:, 2048:4096].rearrange("p (a b) -> p a b", a=4)]
                tmp, pool_tmp = cut(14232, BANK), cut(15256, BANK)
                prod = [[spare[:, j * BANK:(j + 1) * BANK] for j in range(4)],
                        [*(filter_out[:, j * BANK:(j + 1) * BANK] for j in range(3)), cut(14744, BANK)]]
                got = side_load("hyena", [(params.rearrange("p a b -> p (a b)"), a["hy_cols"])], *ready)

                def spectrum_load(o, hv, *after_):
                    cols = slice(hv * BANK, (hv + 1) * BANK)
                    return side_load(f"spectrum{o}{hv}", [
                        (kr[hv], spectra["real"][o][:, :, cols]), (ki[hv], spectra["imag"][o][:, :, cols]),
                        (kn[hv][1:P, :], spectra["real"][o][1:P, 0, cols]),
                        (kn[hv][0:1, :], spectra["nyquist"][o][:, cols])],
                        *spectrum_stored[o, 2 * hv], *spectrum_stored[o, 2 * hv + 1], *after_, lane=sync)

                zeroed = [dve(lambda q=q: nc.vector.memset(q, 0.0), *ready) for q in padded]
                vector.wait(got)
                scalar.wait(got)
                pad_free = [zeroed[-1]] * 3
                wv = by_p(a["hy_w_in_2"][0])
                n = 0
                for c0 in range(0, 3 * D, BANK):
                    s, got_s = load((lambda v: v[:, :].rearrange("p (k n) -> p k n", k=KD), wv[:, :, c0:c0 + BANK]))
                    ws = s.t[:, :].rearrange("p (k n) -> p k n", k=KD)
                    for f in range(4):
                        b = next_bank()
                        m = mms(b.t[:, 0:TOKENS], [(ws[:, k, f * P:(f + 1) * P], h_cols[:, k, :]) for k in range(KD)],
                                got_s, *t_h, *b.free)
                        pd = padded[n % 3]
                        t = a_fn(pd[:, 1:257], b.t[:, 0:TOKENS], ACT.Identity, m, pad_free[n % 3],
                                 bias=params[:, 0, n:n + 1], chain=False)
                        b.free = [t]
                        v_ts(u[:, n, :], pd[:, 1:257], params[:, 2, n:n + 1], params[:, 4, n:n + 1], ALU.mult, ALU.add, t)
                        v_stt(u[:, n, :], pd[:, 0:256], params[:, 1, n:n + 1], u[:, n, :], ALU.mult, ALU.add)
                        pad_free[n % 3] = v_stt(u[:, n, :], pd[:, 2:258], params[:, 3, n:n + 1], u[:, n, :],
                                                ALU.mult, ALU.add)
                        n += 1
                    s.free = [m]
                s_four, got_four = load((lambda v: v[:, 0:2048], a["k_fourier"][:, 0:2048]))
                s_four.held = True
                got_k = {hv: spectrum_load(0, hv, *ready) for hv in range(2)}
                fc = s_four.t
                ahead = fc[:, 0:1024].rearrange("p (k f) -> p k f", k=TT)
                back = fc[:, 1024:2048].rearrange("p (k t) -> p k t", k=4)
                z_rows = h_rows
                def cols_to_rows(src, q4, *after_):
                    for i in range(TT):
                        b = next_bank()
                        for k in range(4):
                            m = turn(b.t[:, k * P:(k + 1) * P], src(q4 * 4 + k)[:, i * P:(i + 1) * P], *after_, *b.free)
                        b.free = [a_fn(z_rows[:, i, q4 * BANK:(q4 + 1) * BANK], b.t[:, :], ACT.Copy, m, *after_)]
                    return b.free[0]

                def spectrum_of(hv, t_z):
                    for f4 in range(4):
                        b = next_bank()
                        m = mms(b.t[:, :], [(ahead[:, i, f4 * P:(f4 + 1) * P], z_rows[:, i, hv * BANK:(hv + 1) * BANK])
                                            for i in range(TT)], t_z, got_four, *b.free)
                        b.free = [a_fn(spec[hv][:, f4, :], b.t[:, :], ACT.Copy, m, *spec_free[hv], chain=False)]
                    return b.free[0]

                def times_filter(hv, t_spec):
                    pr_ = prod[hv]
                    toks = []
                    for part in range(4):
                        ft, imaginary = part % 2, part >= 2
                        ur, ui = spec[hv][:, ft, :], spec[hv][:, 2 + ft, :]
                        kni = kn[hv] if ft == 0 else kr[hv][:, 1, :]
                        one, two = (ki[hv][:, ft, :], kni) if imaginary else (kr[hv][:, ft, :], ki[hv][:, ft, :])
                        last = ALU.add if imaginary else ALU.subtract
                        op, scratch = (pool_tt, pool_tmp) if part == 3 else (v_tt, tmp)
                        op(pr_[part], ur, one, ALU.mult, t_spec, got_k[hv], *prod_free[hv])
                        op(scratch, ui, two, ALU.mult)
                        toks.append(op(pr_[part], pr_[part], scratch, last))
                    return toks

                def back_and_gate(hv, o, toks):
                    for dt in range(4):
                        k = hv * 4 + dt
                        b = next_bank()
                        m = mms(b.t[:, 0:TOKENS], [(prod[hv][f4][:, dt * P:(dt + 1) * P], back[:, f4, :]) for f4 in range(4)],
                                *toks, *b.free)
                        gate_u = u[:, o * 8 + k, :]
                        b.free = [v_tt(gate_u, b.t[:, 0:TOKENS], gate_u, ALU.mult, m)]
                    prod_free[hv] = [m]
                    return b.free[0]

                done_u = everyone()
                spec_free, prod_free = [done_u, done_u], [done_u, done_u]
                gated_u = [done_u, done_u]
                for o in range(2):
                    src = (lambda k: u[:, 16 + k, :]) if o == 0 else (lambda k: u[:, k, :])
                    toks = []
                    for hv in range(2):
                        t_z = cols_to_rows(src, hv, *gated_u[hv])
                        t_spec = spectrum_of(hv, t_z)
                        toks.append(times_filter(hv, t_spec))
                        spec_free[hv] = toks[hv]
                        if o == 0:
                            got_k[hv] = spectrum_load(1, hv, *toks[hv])
                    for hv in range(2):
                        gated_u[hv] = [back_and_gate(hv, o, toks[hv])]
                s_four.free, s_four.held = everyone(), False
                product_rows(u[:, 8:16, :], KD, a["hy_w_out_2"][0], by_k, D, residual(gates_row[:, 0, :]), *everyone(), got_gates[0])

            finish()
            done = everyone()
            if layer == 0:
                got_first_gate = gate_load("mod_two1", stored["mod_two1"], 0, *done)
            t_affine = fold(2 * layer + 3)
            t = normalize(*done, halves=squared.values())
            t = normed_cols(h_rows, h_cols, 2 * layer + 3, *t, t_affine, follow=route_products())
            experts(name, 2 * layer + 3, 4, 4, 256, a["moe_w_gate_2"][layer], a["moe_w_up_2"][layer],
                    a["moe_w_down_2"][layer], got_gates[1], *t, *everyone())
            done = everyone()

        stored = sem("stored")
        sync.dma(out[0].rearrange("(i p) d -> p i d", p=P), x[:, :, :], stored, *done)
        sync.wait((stored, 16))

        block = ctx.enter_context(nc.Block())

        @block.sync
        def _(e):
            sync.run(e)

        @block.tensor
        def _(e):
            tensor.run(e)

        @block.vector
        def _(e):
            vector.run(e)

        @block.scalar
        def _(e):
            scalar.run(e)

        @block.gpsimd
        def _(e):
            pool.run(e)


def lay_out(inputs):
    arrays = {k: np.ascontiguousarray(v) for k, v in inputs.items()}
    arrays["w_s_t"] = np.ascontiguousarray(arrays.pop("w_s")[0].transpose(2, 0, 1))
    arrays["b_s_t"] = np.ascontiguousarray(arrays.pop("b_s")[0].T)
    arrays["positions_2_cols"] = np.ascontiguousarray(arrays.pop("positions_2")[0].astype(np.int32).reshape(TT, P).T)
    cols = [arrays.pop("hy_b_in_2")[0], *arrays.pop("hy_conv_w_2")[0], arrays.pop("hy_conv_b_2")[0]]
    arrays["hy_cols"] = np.ascontiguousarray(
        np.stack([c.reshape(24, P) for c in cols]).transpose(2, 0, 1).reshape(P, 120))
    arrays["hy_f_cols"] = np.ascontiguousarray(np.stack(
        [arrays.pop(f"hy_f_{w}{l}_2")[0] for l in (1, 2, 3) for w in ("b", "freq")], axis=1))
    arrays["route_w_one"] = np.concatenate([arrays.pop("w_grp")[0], arrays.pop("w_exp")[0]], axis=1)
    arrays["route_b_one"] = np.concatenate([arrays.pop("b_grp")[0], arrays.pop("b_exp")[0]])
    wg, we, bg, be = (arrays.pop(f"moe_{n}_2") for n in ("wg", "we", "bg", "be"))
    for layer in range(2):
        arrays[f"route_w_two{layer}"] = np.concatenate([wg[layer], we[layer]], axis=1)
        arrays[f"route_b_two{layer}"] = np.concatenate([bg[layer], be[layer]])
    mix, ffn = arrays.pop("norm_mix_g_2"), arrays.pop("norm_ffn_g_2")
    norms = np.stack([arrays.pop("norm1_w")[0], arrays.pop("norm2_w")[0], mix[0], ffn[0], mix[1], ffn[1]])
    heads = [arrays[f"mla_{n}_norm_g_2"][0][0:NOPE] for n in ("q", "k")]
    arrays["mla_cols"] = np.ascontiguousarray(
        np.concatenate([arrays.pop("mla_q_a_g_2")[0], arrays.pop("mla_kv_a_g_2")[0], *heads]).reshape(5, P).T)
    arrays["norm_cols"] = np.ascontiguousarray(norms.reshape(6, P, KD).transpose(1, 0, 2).reshape(P, 6 * KD))
    arrays["qk_norm_w"] = np.concatenate([arrays.pop("q_norm_w")[0]] * B_HEADS + [arrays.pop("k_norm_w")[0]] * B_KV)
    arrays.update(shape_constants())
    return arrays


def kernel(**inputs):
    import concourse.bacc as bacc
    from concourse.bass_utils import run_bass_kernel_spmd

    arrays = lay_out(inputs)
    nc = bacc.Bacc("TRN2", target_bir_lowering=False, num_devices=1)
    handles = {k: nc.dram_tensor(f"in_{k}", v.shape, mybir.dt.from_np(v.dtype), kind="ExternalInput").ap()
               for k, v in arrays.items()}
    out = nc.dram_tensor("out", (1, TOKENS, D), F32, kind="ExternalOutput").ap()
    build(nc, handles, out)
    result = run_bass_kernel_spmd(nc, [{f"in_{k}": v for k, v in arrays.items()}], core_ids=[0])
    return result.results[0]["out"]
```
